# Optimizing a Trainium2 kernel written in Bass

```python
import jax, jax.numpy as jnp
from jax import lax
import numpy as np

D_MODEL = 1024
BATCH = 1
SEQ = 128
DEPTH = 2
DEC_BATCH = 1
DEC_SEQ = 512
PAST_LEN = 128

GRID_W = 64
HEAD_DIM = 64
N_HEADS = D_MODEL // HEAD_DIM
H_RET = N_HEADS // 2
H_NA = N_HEADS - H_RET
RET_DK = HEAD_DIM
RET_DV = HEAD_DIM
RET_CHUNK = 128
WIN_R = 8
WIN_C = 16
NA_QB = 16
NA_KBW = NA_QB + WIN_C
NA_NCB = GRID_W // NA_QB
MLA_HEADS = N_HEADS
MLA_Q_LORA = 384
MLA_KV_LORA = 256
MLA_NOPE = 64
MLA_ROPE = 32
MLA_V = 64
MLA_SCALE = (MLA_NOPE + MLA_ROPE) ** -0.5
ROPE_BASE = 10000.0
D_FF = 4 * D_MODEL
Q_BLOCK = 128
N_A_LAYERS = (DEPTH + 1) // 2
N_C_LAYERS = DEPTH // 2
EPS = 1e-6
NEG_INF = -1e30
AC_IN = 2 * H_RET * RET_DK + 2 * H_RET * RET_DV + 3 * H_NA * HEAD_DIM
AC_OUT = H_RET * RET_DV + H_NA * HEAD_DIM
C_IN = MLA_Q_LORA + MLA_KV_LORA + MLA_ROPE

kernel_name = 'hybrid_retention_na_mla_flow_step'

def rms_norm(x, g):
    xf = x.astype(jnp.float32)
    y = xf * lax.rsqrt(jnp.mean(xf * xf, axis=-1, keepdims=True) + EPS)
    return (y * g.astype(jnp.float32)).astype(x.dtype)

def split_heads(x, h):
    b, l, _ = x.shape
    return x.reshape(b, l, h, -1).transpose(0, 2, 1, 3)

def merge_heads(x):
    b, h, l, d = x.shape
    return x.transpose(0, 2, 1, 3).reshape(b, l, h * d)

def axial_rope(x):
    l = x.shape[-2]
    t = jnp.arange(l)
    row = (t // GRID_W).astype(jnp.float32)
    col = (t % GRID_W).astype(jnp.float32)
    nf = MLA_ROPE // 4
    inv = ROPE_BASE ** (-jnp.arange(nf, dtype=jnp.float32) / nf)
    ang = jnp.concatenate([row[:, None] * inv, col[:, None] * inv], axis=-1)
    cos, sin = jnp.cos(ang), jnp.sin(ang)
    xf = x.astype(jnp.float32).reshape(x.shape[:-1] + (MLA_ROPE // 2, 2))
    x1, x2 = xf[..., 0], xf[..., 1]
    out = jnp.stack([x1 * cos - x2 * sin, x1 * sin + x2 * cos], axis=-1)
    return out.reshape(x.shape).astype(x.dtype)

def joint_attention(qs, ks, vs, scale):
    b, h, l, _ = qs[0].shape
    nb = l // Q_BLOCK
    splits = [int(s) for s in np.cumsum([k.shape[2] for k in ks])[:-1]]

    def block(i):
        start = i * Q_BLOCK
        s = jnp.concatenate(
            [jnp.einsum('bhqd,bhkd->bhqk', lax.dynamic_slice_in_dim(q, start, Q_BLOCK, axis=2), k)
             for q, k in zip(qs, ks)], axis=-1).astype(jnp.float32) * scale
        p = jax.nn.softmax(s, axis=-1)
        ps = jnp.split(p, splits, axis=-1)
        out = jnp.einsum('bhqk,bhkd->bhqd', ps[0].astype(vs[0].dtype), vs[0])
        for j in range(1, len(vs)):
            out = out + jnp.einsum('bhqk,bhkd->bhqd', ps[j].astype(vs[j].dtype), vs[j])
        return out

    outs = lax.map(block, jnp.arange(nb))
    return jnp.moveaxis(outs, 0, 2).reshape(b, h, l, -1)

def log_decay(p):
    return jnp.log1p(-jnp.exp2(p.astype(jnp.float32)))

def retention_chunkwise(q, k, v, lg, s0):
    dtype = v.dtype
    q, k, v = q.astype(jnp.float32), k.astype(jnp.float32), v.astype(jnp.float32)
    b, h, l, dk = q.shape
    dv = v.shape[-1]
    n = l // RET_CHUNK
    qc = q.reshape(b, h, n, RET_CHUNK, dk)
    kc = k.reshape(b, h, n, RET_CHUNK, dk)
    vc = v.reshape(b, h, n, RET_CHUNK, dv)
    pos = jnp.arange(RET_CHUNK, dtype=jnp.float32)
    lgc = lg[:, None]
    diff = pos[:, None] - pos[None, :]
    dmask = jnp.where(diff >= 0, jnp.exp(lgc[:, :, None] * jnp.maximum(diff, 0.0)), 0.0)
    s = jnp.einsum('bhncd,bhnmd->bhncm', qc, kc) * dmask[None, :, None]
    o_intra = jnp.einsum('bhncm,bhnme->bhnce', s, vc)
    k_dec = jnp.exp(lgc * (RET_CHUNK - 1 - pos))
    kv = jnp.einsum('bhnmd,bhnme->bhnde', kc * k_dec[None, :, None, :, None], vc)
    chunk_dec = jnp.exp(lg * RET_CHUNK)[:, None, None]

    def step(state, kv_i):
        return chunk_dec * state + kv_i, state

    s_fin, s_prev = lax.scan(step, s0.astype(jnp.float32), jnp.moveaxis(kv, 2, 0))
    q_dec = jnp.exp(lgc * (pos + 1.0))
    o_cross = jnp.einsum('bhncd,nbhde->bhnce', qc * q_dec[None, :, None, :, None], s_prev)
    return (o_intra + o_cross).reshape(b, h, l, dv).astype(dtype), s_fin.astype(dtype)

def retention_bidir(q, k, v, lg_f, lg_b, s_f, s_b):
    o_f, fin_f = retention_chunkwise(q, k, v, lg_f, s_f)
    o_b, fin_b = retention_chunkwise(jnp.flip(q, 2), jnp.flip(k, 2), jnp.flip(v, 2), lg_b, s_b)
    return o_f + jnp.flip(o_b, 2), fin_f, fin_b

def retention_out(o, g):
    of = o.astype(jnp.float32)
    mu = jnp.mean(of, axis=-1, keepdims=True)
    var = jnp.mean(jnp.square(of - mu), axis=-1, keepdims=True)
    on = ((of - mu) * lax.rsqrt(var + EPS)).astype(o.dtype)
    return merge_heads(on) * jax.nn.silu(g)

def even_project(h, w_in):
    sizes = [H_RET * RET_DK, H_RET * RET_DK, H_RET * RET_DV, H_RET * RET_DV,
             H_NA * HEAD_DIM, H_NA * HEAD_DIM, H_NA * HEAD_DIM]
    parts = jnp.split(h @ w_in, [int(s) for s in np.cumsum(sizes)[:-1]], axis=-1)
    rq, rk, rv, rg, nq, nk, nv = parts
    rq = split_heads(rq, H_RET)
    rk = split_heads(rk, H_RET) * (RET_DK ** -0.5)
    rv = split_heads(rv, H_RET)
    return rq, rk, rv, rg, split_heads(nq, H_NA), split_heads(nk, H_NA), split_heads(nv, H_NA)

def neighborhood_attention(q, k, v, k_ctx, v_ctx, rpb):
    b, h, l, d = q.shape
    rows = l // GRID_W
    wr = min(WIN_R, rows)
    r = np.arange(rows)
    row_idx = np.clip(r - wr // 2, 0, rows - wr)[:, None] + np.arange(wr)[None]
    blk = np.arange(NA_NCB)
    col_start = np.clip(blk * NA_QB - WIN_C // 2, 0, GRID_W - NA_KBW)
    col_idx = col_start[:, None] + np.arange(NA_KBW)[None]
    q_col = blk[:, None] * NA_QB + np.arange(NA_QB)[None]
    win_start = np.clip(q_col - WIN_C // 2, 0, GRID_W - WIN_C)
    valid = (col_idx[:, None, :] >= win_start[:, :, None]) & (col_idx[:, None, :] < win_start[:, :, None] + WIN_C)
    dr = row_idx - r[:, None] + (WIN_R - 1)
    dc = np.clip(col_idx[:, None, :] - q_col[:, :, None], -(WIN_C - 1), WIN_C - 1) + (WIN_C - 1)
    bias = rpb[:, dr[:, None, None, :, None], dc[None, :, :, None, :]].astype(jnp.float32)
    bias = jnp.where(valid[None, None, :, :, None, :], bias, NEG_INF).reshape(h, rows, NA_NCB, NA_QB, wr * NA_KBW)
    qg = q.reshape(b, h, rows, NA_NCB, NA_QB, d)
    gidx = (row_idx[:, None, :, None], col_idx[None, :, None, :])
    kg = k.reshape(b, h, rows, GRID_W, d)[:, :, gidx[0], gidx[1]].reshape(b, h, rows, NA_NCB, wr * NA_KBW, d)
    vg = v.reshape(b, h, rows, GRID_W, d)[:, :, gidx[0], gidx[1]].reshape(b, h, rows, NA_NCB, wr * NA_KBW, d)
    scale = HEAD_DIM ** -0.5
    s_loc = jnp.einsum('bhrnqd,bhrnkd->bhrnqk', qg, kg).astype(jnp.float32) * scale + bias[None]
    s_ctx = jnp.einsum('bhrnqd,bhkd->bhrnqk', qg, k_ctx).astype(jnp.float32) * scale
    p = jax.nn.softmax(jnp.concatenate([s_loc, s_ctx], axis=-1), axis=-1).astype(v.dtype)
    nloc = wr * NA_KBW
    o = (jnp.einsum('bhrnqk,bhrnkd->bhrnqd', p[..., :nloc], vg)
         + jnp.einsum('bhrnqk,bhkd->bhrnqd', p[..., nloc:], v_ctx))
    return o.reshape(b, h, l, d)

def mixer_ac_context(h, w_in, w_out, lg_f, lg_b):
    rq, rk, rv, rg, nq, nk, nv = even_project(h, w_in)
    zeros = jnp.zeros((h.shape[0], H_RET, RET_DK, RET_DV), h.dtype)
    o_ret, s_f, s_b = retention_bidir(rq, rk, rv, lg_f, lg_b, zeros, zeros)
    o_na = joint_attention([nq], [nk], [nv], HEAD_DIM ** -0.5)
    y = jnp.concatenate([retention_out(o_ret, rg), merge_heads(o_na)], axis=-1) @ w_out
    return y, s_f, s_b, nk, nv

def mixer_ac_latent(h, w_in, w_out, lg_f, lg_b, s_f, s_b, k_ctx, v_ctx, rpb):
    rq, rk, rv, rg, nq, nk, nv = even_project(h, w_in)
    o_ret, _, _ = retention_bidir(rq, rk, rv, lg_f, lg_b, s_f, s_b)
    o_na = neighborhood_attention(nq, nk, nv, k_ctx, v_ctx, rpb)
    return jnp.concatenate([retention_out(o_ret, rg), merge_heads(o_na)], axis=-1) @ w_out

def mla_project(h, w_in, q_norm, kv_norm, w_uq):
    c_q, c_kv, k_pe = jnp.split(h @ w_in, [MLA_Q_LORA, MLA_Q_LORA + MLA_KV_LORA], axis=-1)
    c_kv = rms_norm(c_kv, kv_norm)
    q = split_heads(rms_norm(c_q, q_norm) @ w_uq, MLA_HEADS)
    return q[..., :MLA_NOPE], q[..., MLA_NOPE:], c_kv, k_pe

def bcast_heads(k_pe):
    b, l, r = k_pe.shape
    return jnp.broadcast_to(k_pe[:, None], (b, MLA_HEADS, l, r))

def mla_context(h, w_in, q_norm, kv_norm, w_uq, w_uk, w_uv, w_out):
    q_nope, q_pe, c_kv, k_pe = mla_project(h, w_in, q_norm, kv_norm, w_uq)
    k_nope = split_heads(c_kv @ w_uk, MLA_HEADS)
    v = split_heads(c_kv @ w_uv, MLA_HEADS)
    q = jnp.concatenate([q_nope, q_pe], axis=-1)
    k = jnp.concatenate([k_nope, bcast_heads(k_pe)], axis=-1)
    o = joint_attention([q], [k], [v], MLA_SCALE)
    return merge_heads(o) @ w_out, c_kv, k_pe

def mla_latent(h, w_in, q_norm, kv_norm, w_uq, w_uk, w_uv, w_out, ckv_ctx, kpe_ctx):
    q_nope, q_pe, c_kv, k_pe = mla_project(h, w_in, q_norm, kv_norm, w_uq)
    k_nope = split_heads(c_kv @ w_uk, MLA_HEADS)
    v = split_heads(c_kv @ w_uv, MLA_HEADS)
    kc_nope = split_heads(ckv_ctx @ w_uk, MLA_HEADS)
    vc = split_heads(ckv_ctx @ w_uv, MLA_HEADS)
    q_lat = jnp.concatenate([q_nope, axial_rope(q_pe)], axis=-1)
    k_lat = jnp.concatenate([k_nope, bcast_heads(axial_rope(k_pe))], axis=-1)
    q_ctx = jnp.concatenate([q_nope, q_pe], axis=-1)
    k_ctx = jnp.concatenate([kc_nope, bcast_heads(kpe_ctx)], axis=-1)
    o = joint_attention([q_lat, q_ctx], [k_lat, k_ctx], [v, vc], MLA_SCALE)
    return merge_heads(o) @ w_out

def modulation(cond, w_ada, b_ada):
    m = jax.nn.silu(cond) @ w_ada + b_ada
    return m.reshape(cond.shape[0], 6, D_MODEL)

def modulate(x, g, shift, scale):
    return rms_norm(x, g) * (1 + scale[:, None, :]) + shift[:, None, :]

def gated_residual(x, y, g, gate):
    return x + gate[:, None, :] * rms_norm(y, g)

def channel_mixer(h, w1, w2):
    return jnp.square(jax.nn.relu(h @ w1)) @ w2

def setup_inputs(seed: int = 0) -> dict:
    key = jax.random.key(seed)
    ks = iter(jax.random.split(key, 40))
    f32 = jnp.float32

    def nrm(shape, scale=1.0):
        return jax.random.normal(next(ks), shape, f32) * scale

    base_decay = -5.0 - jnp.arange(H_RET, dtype=f32)
    return {
        'x_prompt': nrm((BATCH, SEQ, D_MODEL)),
        'x_sample': nrm((DEC_BATCH, DEC_SEQ, D_MODEL)),
        'state_ret_fwd': nrm((DEC_BATCH, N_A_LAYERS, H_RET, RET_DK, RET_DV), 0.5),
        'state_ret_bwd': nrm((DEC_BATCH, N_A_LAYERS, H_RET, RET_DK, RET_DV), 0.5),
        'cache_na_k': nrm((DEC_BATCH, N_A_LAYERS, H_NA, PAST_LEN, HEAD_DIM)),
        'cache_na_v': nrm((DEC_BATCH, N_A_LAYERS, H_NA, PAST_LEN, HEAD_DIM)),
        'cache_mla_ckv': nrm((DEC_BATCH, N_C_LAYERS, PAST_LEN, MLA_KV_LORA)),
        'cache_mla_kpe': nrm((DEC_BATCH, N_C_LAYERS, PAST_LEN, MLA_ROPE)),
        'c': nrm((DEC_BATCH, D_MODEL)),
        'c_ctx': nrm((D_MODEL,)),
        'w_ada': nrm((DEPTH, D_MODEL, 6 * D_MODEL), 0.5 * D_MODEL ** -0.5),
        'b_ada': nrm((DEPTH, 6 * D_MODEL), 0.1),
        'norm_gains': 1.0 + nrm((DEPTH, 4, D_MODEL), 0.05),
        'w_mlp_in': nrm((DEPTH, D_MODEL, D_FF), D_MODEL ** -0.5),
        'w_mlp_out': nrm((DEPTH, D_FF, D_MODEL), D_FF ** -0.5),
        'w_in_ac': nrm((N_A_LAYERS, D_MODEL, AC_IN), D_MODEL ** -0.5),
        'w_out_ac': nrm((N_A_LAYERS, AC_OUT, D_MODEL), AC_OUT ** -0.5),
        'ret_decay_fwd': base_decay + nrm((N_A_LAYERS, H_RET), 0.1),
        'ret_decay_bwd': base_decay + nrm((N_A_LAYERS, H_RET), 0.1),
        'na_rpb': nrm((N_A_LAYERS, H_NA, 2 * WIN_R - 1, 2 * WIN_C - 1), 0.1),
        'w_in_c': nrm((N_C_LAYERS, D_MODEL, C_IN), D_MODEL ** -0.5),
        'mla_q_norm': 1.0 + nrm((N_C_LAYERS, MLA_Q_LORA), 0.05),
        'mla_kv_norm': 1.0 + nrm((N_C_LAYERS, MLA_KV_LORA), 0.05),
        'w_uq': nrm((N_C_LAYERS, MLA_Q_LORA, MLA_HEADS * (MLA_NOPE + MLA_ROPE)), MLA_Q_LORA ** -0.5),
        'w_uk': nrm((N_C_LAYERS, MLA_KV_LORA, MLA_HEADS * MLA_NOPE), MLA_KV_LORA ** -0.5),
        'w_uv': nrm((N_C_LAYERS, MLA_KV_LORA, MLA_HEADS * MLA_V), MLA_KV_LORA ** -0.5),
        'w_out_c': nrm((N_C_LAYERS, MLA_HEADS * MLA_V, D_MODEL), (MLA_HEADS * MLA_V) ** -0.5),
    }

def reference(x_prompt, x_sample, state_ret_fwd, state_ret_bwd, cache_na_k, cache_na_v,
              cache_mla_ckv, cache_mla_kpe, c, c_ctx, w_ada, b_ada, norm_gains, w_mlp_in, w_mlp_out,
              w_in_ac, w_out_ac, ret_decay_fwd, ret_decay_bwd, na_rpb, w_in_c, mla_q_norm,
              mla_kv_norm, w_uq, w_uk, w_uv, w_out_c):
    xp, xs = x_prompt, x_sample
    ret_f, ret_b, na_k, na_v, mla_ckv, mla_kpe = [], [], [], [], [], []
    for layer in range(DEPTH):
        mc = modulation(c_ctx[None], w_ada[layer], b_ada[layer])
        ml = modulation(c, w_ada[layer], b_ada[layer])
        g = norm_gains[layer]
        hp = modulate(xp, g[0], mc[:, 0], mc[:, 1])
        hs = modulate(xs, g[0], ml[:, 0], ml[:, 1])
        if layer % 2 == 0:
            ia = layer // 2
            lg_f = log_decay(ret_decay_fwd[ia])
            lg_b = log_decay(ret_decay_bwd[ia])
            yp, s_f, s_b, nk, nv = mixer_ac_context(hp, w_in_ac[ia], w_out_ac[ia], lg_f, lg_b)
            ret_f.append(s_f)
            ret_b.append(s_b)
            na_k.append(nk)
            na_v.append(nv)
            ys = mixer_ac_latent(hs, w_in_ac[ia], w_out_ac[ia], lg_f, lg_b,
                                 state_ret_fwd[:, ia], state_ret_bwd[:, ia],
                                 cache_na_k[:, ia], cache_na_v[:, ia], na_rpb[ia])
        else:
            ic = layer // 2
            yp, ckv, kpe = mla_context(hp, w_in_c[ic], mla_q_norm[ic], mla_kv_norm[ic],
                                       w_uq[ic], w_uk[ic], w_uv[ic], w_out_c[ic])
            mla_ckv.append(ckv)
            mla_kpe.append(kpe)
            ys = mla_latent(hs, w_in_c[ic], mla_q_norm[ic], mla_kv_norm[ic], w_uq[ic], w_uk[ic],
                            w_uv[ic], w_out_c[ic], cache_mla_ckv[:, ic], cache_mla_kpe[:, ic])
        xp = gated_residual(xp, yp, g[1], mc[:, 2])
        xs = gated_residual(xs, ys, g[1], ml[:, 2])
        hp = modulate(xp, g[2], mc[:, 3], mc[:, 4])
        hs = modulate(xs, g[2], ml[:, 3], ml[:, 4])
        xp = gated_residual(xp, channel_mixer(hp, w_mlp_in[layer], w_mlp_out[layer]), g[3], mc[:, 5])
        xs = gated_residual(xs, channel_mixer(hs, w_mlp_in[layer], w_mlp_out[layer]), g[3], ml[:, 5])
    new_ret_fwd = jnp.stack(ret_f, axis=1)
    new_ret_bwd = jnp.stack(ret_b, axis=1)
    new_na_k = jnp.stack(na_k, axis=1)
    new_na_v = jnp.stack(na_v, axis=1)
    new_mla_ckv = jnp.stack(mla_ckv, axis=1)
    new_mla_kpe = jnp.stack(mla_kpe, axis=1)
    return (xp, xs, new_ret_fwd, new_ret_bwd, new_na_k, new_na_v, new_mla_ckv, new_mla_kpe)


_drawn_inputs = setup_inputs


def setup_inputs(seed=0):
    import zlib

    import numpy as np

    out = dict(_drawn_inputs(seed))
    spreads = {}
    factors = {'cache_mla_kpe': 3.166, 'na_rpb': 8.0, 'mla_q_norm': 8.0}
    for name, (base, spread) in spreads.items():
        noise = np.random.default_rng([zlib.crc32(name.encode()), seed]).standard_normal(out[name].shape)
        drawn = base * np.exp(spread * noise) if base else spread * noise
        out[name] = __import__('jax').numpy.asarray(drawn.astype(out[name].dtype))
    for name, factor in factors.items():
        out[name] = (out[name] * factor).astype(out[name].dtype)
    return out
```

```python
from contextlib import ExitStack

import concourse.bass as bass
from concourse import mybir

F32 = mybir.dt.float32
F32R = mybir.dt.float32r
ALU = mybir.AluOpType
ACT = mybir.ActivationFunctionType
AX = mybir.AxisListType

P = 128
D = 1024
KD = D // P
TL, TC = 512, 128
T = TL + TC
NP = 128
HALF = T // 2
ROWS, GRID_W = 8, 64
BLK = P // ROWS
NB = TL // P
HD = 64
NH = 8
NH_MLA = 16
KW = 32
NKEY = KW * ROWS
RPB_R, RPB_C = 15, 31
KQ, KKV = 3, 2
ROPE = 32
DFF = 4096
CH = 8
NCH = DFF // (CH * P)
EPS = 1e-6
MLA_SCALE = 96 ** -0.5
LN2 = 0.6931471805599453
LOWEST = -3.0e38

STAGE = 4
PIECE = 1024

SHIFT1, SCALE1, GATE1, SHIFT2, SCALE2, GATE2 = range(6)
A1, G1, A2, G2 = range(4)
ROW_GAIN, ROW_C, ROW_CTX, ROW_QN, ROW_KVN, VROWS = 0, 64, 72, 80, 83, 85

NORMS = (("in0", KD), ("y0a", KD), ("in0m", KD), ("y0m", KD), ("in1", KD), ("cq", KQ), ("ckv", KKV),
         ("y1a", KD), ("in1m", KD), ("y1m", KD))
PIECES = (("ac", 20), ("rv", 4), ("nv", 4), ("out0", 8), ("mlp0", 16 * NCH), ("in_c", 6),
          ("uq", 8), ("uk", 2), ("uv", 2), ("out1", 8), ("mlp1", 16 * NCH))
UNITS = (("ac", 20, "a"), ("out0", 8, "d"), ("mlp0", 16 * NCH, None), ("in_c", 6, "a"), ("uq", 16, "ad"),
         ("uk", 8, "a"), ("out1", 8, "d"), ("mlp1", 16 * NCH, None))


def first_of(table):
    out, at = {}, 0
    for row in table:
        out[row[0]] = at
        at += row[1]
    out["end"] = at
    return out


def evacuations():
    a = d = 0
    out = []
    for _, n, who in UNITS:
        for j in range(n):
            w = who or ("a" if j % 16 < 8 else "d")
            a += "a" in w
            d += "d" in w
            out.append((a if "a" in w else 0, d if "d" in w else 0))
    return out


NORM_AT = first_of(NORMS)
NORM_NO = {name: n for n, (name, _) in enumerate(NORMS)}
NORM_K = dict(NORMS)
PIECE_AT = first_of(PIECES)
UNIT_AT = first_of(UNITS)
EVAC = evacuations()
MOD_NO = {"in0": 0, "in0m": 1, "in1": 2, "in1m": 3}
N_NA = NH * (NB + 1)
N_MLA = NH_MLA * (NB + 1)
FIRST_KEY = (0, 64, 192, 256)
SPAN = ((0, TL), (TL, T))


def build(nc, i, o):
    top = ExitStack()
    with top:
        def sem(name):
            return top.enter_context(nc.semaphore(name))

        def sb(name, shape, dt=F32, stack=top):
            return stack.enter_context(nc.sbuf_tensor(name, shape, dt))

        def lay(offset, *rows):
            with ExitStack() as s:
                if offset:
                    sb(f"pad{len(pads)}", [P, offset * 256], stack=s)
                    pads.append(offset)
                return [sb(name, shape, dt, s) for name, shape, dt in rows]

        pads = []
        ps = top.enter_context(nc.psum_tensor("ps", [P, 8, 512], F32))

        def pair(g, rows=slice(0, P)):
            b = 2 * (g % 2)
            return ps[rows, b:b + 2, 0:HALF]

        def two(ap):
            return ap.rearrange("p (n c) -> p n c", n=2)

        xT = sb("xT", [P, KD, T])
        ident = sb("ident", [P, P])
        ones = sb("ones", [P, P])
        gnb = sb("gnb", [P, P])
        vecT = sb("vecT", [P, VROWS])
        badaT = sb("badaT", [P, 2, 48])
        mod = sb("mod", [P, 2, 48, 2])
        coef = sb("coef", [P, 2, 4, KD, 2])
        rstd = sb("rstd", [P, T])
        sq = sb("sq", [P, 2, T])
        nt = sb("nt", [P, 2, T])
        stage = sb("stage", [P, STAGE, PIECE])
        w_hi = sb("w_hi", [P, 2, PIECE], F32R)
        w_lo = sb("w_lo", [P, 2, PIECE], F32R)

        xtok, vrow, brow, csil, cexp, ada, modrow = lay(
            0, ("xtok", [P, 5, D], F32), ("vrow", [VROWS, P], F32), ("brow", [96, P], F32),
            ("csil", [P, KD, 2], F32), ("cexp", [P, 16], F32), ("ada", [P, 2, KD, 512], F32),
            ("modrow", [2, 2, 512], F32))
        oT, kz, gate, rv, kzn, nv, hA_hi, hA_lo = lay(
            0, ("oT", [P, KD, T], F32), ("kz", [P, NH, T], F32), ("gate", [P, 4, T], F32),
            ("rv", [P, 5, 512], F32), ("kzn", [P, NH, T + NP], F32), ("nv", [P, 5, 512], F32),
            ("hA_hi", [P, KD, T], F32R), ("hA_lo", [P, KD, T], F32R))
        dmat, dist, tpos, edec, qE, sd, state, dec, lg, kpos, kdec, kd, fin = lay(
            94, ("dmat", [P, 2, 1024], F32), ("dist", [P, 2, 1024], F32), ("tpos", [P, 2, TL], F32),
            ("edec", [P, 2, TL], F32), ("qE", [P, 2, TL], F32), ("sd", [P, 5, 512], F32),
            ("state", [P, NH, HD], F32), ("dec", [P, 16], F32), ("lg", [P, 8, 16], F32), ("kpos", [P, 2], F32),
            ("kdec", [P, 2, NH], F32), ("kd", [P, 2, P], F32), ("fin", [P, NH, HD], F32))
        bias, mask, bm, kpast, vpast, s32, pA, pTA, smA, nkt, nvs = lay(
            94, ("bias", [P, NH, ROWS, 48], F32), ("mask", [P, NB, NKEY], F32), ("bm", [P, 2, NKEY + NP], F32),
            ("kpast", [P, NH, HD], F32), ("vpast", [P, NH, HD], F32), ("s32", [P, 2, 384], F32),
            ("pA", [P, 2, 384], F32), ("pTA", [P, 2, 384], F32), ("smA", [P, 4, 2], F32),
            ("nkt", [P, NH, HD], F32), ("nvs", [P, 3, 512], F32))
        hM_hi, hM_lo, h2_hi, h2_lo, yT, r32, s2 = lay(
            0, ("hM_hi", [P, KD, T], F32R), ("hM_lo", [P, KD, T], F32R), ("h2_hi", [P, CH, T], F32R),
            ("h2_lo", [P, CH, T], F32R), ("yT", [P, KD, T], F32), ("r32", [P, 2, T], F32), ("s2", [P, 2, T], F32))
        qm, km, vm, ck_hi, ck_lo, kmas, rope, ckn = lay(
            0, ("qm", [P, NH_MLA, T], F32), ("km", [P, NH_MLA, T + NP], F32), ("vm", [P, 6, D], F32),
            ("ck_hi", [P, KKV, T + NP], F32R), ("ck_lo", [P, KKV, T + NP], F32R), ("kmas", [P, T + NP], F32),
            ("rope", [P, TL], F32), ("ckn", [P, KKV, T + NP], F32))
        [cT] = lay(40, ("cT", [P, 6, T], F32))
        pastc, tokc, rt = lay(60, ("pastc", [P, 288], F32), ("tokc", [P, 288], F32), ("rt", [P, 2, TL], F32))
        cq_hi, cq_lo = lay(88, ("cq_hi", [P, KQ, T], F32R), ("cq_lo", [P, KQ, T], F32R))
        pM, pTM, smM = lay(112, ("pM", [P, 2, T], F32), ("pTM", [P, 2, T], F32), ("smM", [P, 4, 2], F32))
        [ytok] = lay(0, ("ytok", [P, 5, D], F32))

        const_in, rows_in, x_in = sem("const_in"), sem("rows_in"), sem("x_in")
        ada_in = [sem(f"ada_in{n}") for n in range(2)]
        w_in = [sem(f"w_in{n}") for n in range(STAGE)]
        ret_in, na_in, na_bias_in, mla_in = sem("ret_in"), sem("na_in"), sem("na_bias_in"), sem("mla_in")
        stored = sem("stored")
        w_hi_done, w_lo_done = sem("w_hi_done"), sem("w_lo_done")
        unit_done, act_evac, dve_evac = sem("unit_done"), sem("act_evac"), sem("dve_evac")
        filled, rows_t, rows_out, x_t, x_out = [sem(n) for n in ("filled", "rows_t", "rows_out", "x_t", "x_out")]
        c_exp, c_ready = sem("c_exp"), sem("c_ready")
        ada_done, modrow_done, mod_t, mod_out = [sem(n) for n in ("ada_done", "modrow_done", "mod_t", "mod_out")]
        sq_done, sq_used, ms_out, root_done = [sem(n) for n in ("sq_done", "sq_used", "ms_out", "root_done")]
        x_done, h_full, h_hi_done, h_lo_done = [sem(n) for n in ("x_done", "h_full", "h_hi_done", "h_lo_done")]
        v_done, v_out = sem("v_done"), sem("v_out")
        decay_exp, decay_arg = sem("decay_exp"), sem("decay_arg")
        d_arg, d_exp, e_exp, qe_done = [sem(n) for n in ("d_arg", "d_exp", "e_exp", "qe_done")]
        rs_done, sd_done, ret_done, ret_out = [sem(n) for n in ("rs_done", "sd_done", "ret_done", "ret_out")]
        kd_t, kd_done, fin_done, fin_out = [sem(n) for n in ("kd_t", "kd_done", "fin_done", "fin_out")]
        g_exp, g_done, gn_mm, gn_cen, gn_sq, gn_var, gn_root, gn_done = [
            sem(n) for n in ("g_exp", "g_done", "gn_mm", "gn_cen", "gn_sq", "gn_var", "gn_root", "gn_done")]
        bias_zero, bm_done, past_t, past_out, nk_t, nk_out, nvs_done = [
            sem(n) for n in ("bias_zero", "bm_done", "past_t", "past_out", "nk_t", "nk_out", "nvs_done")]
        na_s, na_max, na_e, na_p, na_t, na_pt, na_pv, na_out = [
            sem(n) for n in ("na_s", "na_max", "na_e", "na_p", "na_t", "na_pt", "na_pv", "na_out")]
        o_hi_done, o_lo_done = sem("o_hi_done"), sem("o_lo_done")
        h2_hi_done, h2_lo_done, y_zero = sem("h2_hi_done"), sem("h2_lo_done"), sem("y_zero")
        cn_full, cn_hi, cn_lo = sem("cn_full"), sem("cn_hi"), sem("cn_lo")
        pc_t, pc_out, tok_t, tok_out, kmas_done, km_rope, qrope_done, vm_done, vm_out, km_zero, ctx_rope = [
            sem(n) for n in ("pc_t", "pc_out", "tok_t", "tok_out", "kmas_done", "km_rope", "qrope_done", "vm_done",
                             "vm_out", "km_zero", "ctx_rope")]
        m_s, m_max, m_e, m_p, m_t, m_pt, m_pv, m_out = [
            sem(n) for n in ("m_s", "m_max", "m_e", "m_p", "m_t", "m_pt", "m_pv", "m_out")]
        y_t, y_out = sem("y_t"), sem("y_out")

        class Chain:

            def __init__(self, engine, name):
                self.engine, self.sem, self.n, self.at = engine, sem(name), 0, 0

            def link(self, instruction):
                self.n += 1
                instruction.then_inc(self.sem, 1)
                self.engine.wait_ge(self.sem, self.at + self.n)

        w_ac = i["w_in_ac"][0].rearrange("(k p) m -> p k m", p=P)
        mats = {
            "out0": i["w_out_ac"][0].rearrange("(k p) m -> p k m", p=P),
            "in_c": i["w_in_c_swap"].rearrange("(k p) m -> p k m", p=P),
            "uq": i["w_uq_heads"].rearrange("(k p) m -> p k m", p=P),
            "uk": i["w_uk"][0].rearrange("(k p) m -> p k m", p=P),
            "uv": i["w_uv"][0].rearrange("(k p) m -> p k m", p=P),
            "out1": i["w_out_c"][0].rearrange("(k p) m -> p k m", p=P),
        }
        mlp_in = [i["w_mlp_in"][n].rearrange("(k p) m -> p k m", p=P) for n in range(2)]
        mlp_out = [i["w_mlp_out"][n].rearrange("(k p) m -> p k m", p=P) for n in range(2)]
        AC_COLS = [0, 512, 1536, 2048, 2560]
        RV_COL, NV_COL = 1024, 3072

        def piece_source(name, j):
            if name == "ac":
                c = AC_COLS[j // 4] + P * (j % 4)
                return w_ac[:, :, c:c + P]
            if name in ("rv", "nv"):
                c = RV_COL if name == "rv" else NV_COL
                return w_ac[:, 2 * j:2 * j + 2, c:c + 512]
            if name == "in_c":
                return mats[name][:, :, P * j:min(P * (j + 1), 704)]
            if name == "uq":
                return mats[name][:, :, 2 * P * j:2 * P * (j + 1)]
            if name in ("uk", "uv"):
                return mats[name][:, j:j + 1, :]
            if name.startswith("mlp"):
                layer, c, j = int(name[3]), j // 16, j % 16
                if j < CH:
                    return mlp_in[layer][:, :, P * (CH * c + j):P * (CH * c + j + 1)]
                return mlp_out[layer][:, CH * c:CH * (c + 1), P * (j - CH):P * (j - CH + 1)]
            return mats[name][:, :, P * j:P * (j + 1)]

        def piece_width(n):
            for name, k in PIECES:
                if PIECE_AT[name] <= n < PIECE_AT[name] + k:
                    if name == "in_c" and n - PIECE_AT[name] == 5:
                        return KD * 64
                    return 768 if name == "uq" else PIECE
            return PIECE


        def piece_used(n):
            name = [x for x, k in PIECES if PIECE_AT[x] <= n][-1]
            j = n - PIECE_AT[name]
            if name in ("rv", "nv"):
                return v_done, j + 1 + 4 * (name == "nv")
            if name == "uv":
                return vm_done, 12
            if name == "uk":
                return unit_done, UNIT_AT["uk"] + 8
            if name == "uq":
                return unit_done, UNIT_AT["uq"] + 2 * j + 2
            return unit_done, UNIT_AT[name] + j + 1

        def act_split(act, n, at=0):
            if isinstance(at, int) and n + at >= PIECE_AT["end"]:
                return
            width = piece_width(n)
            act.wait_ge(w_in[n % STAGE], 16 * (n // STAGE + 1) + at * (16 // STAGE))
            if n >= 2:
                used, count = piece_used(n - 2)
                act.wait_ge(used, count + at)
            nc.scalar.activation(w_hi[:, n % 2, 0:width], stage[:, n % STAGE, 0:width], ACT.Copy)\
                .then_inc(w_hi_done, 1)

        def dve_split(dve, n, at=0):
            if isinstance(at, int) and n + at >= PIECE_AT["end"]:
                return
            width = piece_width(n)
            dve.wait_ge(w_hi_done, n + 1 + at)
            nc.vector.tensor_tensor(w_lo[:, n % 2, 0:width], stage[:, n % STAGE, 0:width],
                                    w_hi[:, n % 2, 0:width].bitcast(F32), ALU.subtract).then_inc(w_lo_done, 1)

        block = top.enter_context(nc.Block())
        grid = lambda x: x.rearrange("(r c) d -> c r d", c=GRID_W)

        @block.sync
        def _(sp):
            def load_piece(name, j):
                n = PIECE_AT[name] + j
                src = piece_source(name, j)
                if n >= STAGE:
                    sp.wait_ge(w_lo_done, n - STAGE + 1)
                dst = stage[:, n % STAGE, 0:piece_width(n)].rearrange("p (k m) -> p k m", k=src.shape[1])
                sp.dma_start(dst, src).then_inc(w_in[n % STAGE], 16)

            def load_pieces(name):
                for j in range(dict(PIECES)[name]):
                    load_piece(name, j)

            def load_mlp(layer):
                first = PIECE_AT[f"mlp{layer}"]
                with sp.Fori(0, NCH) as c:
                    for j in range(2 * CH):
                        n = first + j
                        sp.wait_ge(w_lo_done, n - STAGE + 1 + c * (2 * CH))
                        if j < CH:
                            src = mlp_in[layer][:, :, bass.ds(c * (CH * P) + P * j, P)]
                        else:
                            src = mlp_out[layer][:, bass.ds(c * CH, CH), P * (j - CH):P * (j - CH + 1)]
                        sp.dma_start(stage[:, n % STAGE, :].rearrange("p (k m) -> p k m", k=KD), src)\
                            .then_inc(w_in[n % STAGE], 16)

            sp.dma_start(ident[:], i["c_ident"]).then_inc(const_in, 16)
            sp.dma_start(vrow[ROW_C:ROW_C + 8, :], i["c"][0].rearrange("(k p) -> k p", p=P)).then_inc(rows_in, 16)
            sp.dma_start(vrow[ROW_CTX:ROW_CTX + 8, :], i["c_ctx"].rearrange("(k p) -> k p", p=P)).then_inc(rows_in, 16)
            sp.dma_start(vrow[0:64, :], i["norm_gains"].rearrange("l g (k p) -> (l g k) p", p=P)).then_inc(rows_in, 16)
            sp.dma_start(vrow[ROW_QN:ROW_QN + KQ, :], i["mla_q_norm"][0].rearrange("(k p) -> k p", p=P))\
                .then_inc(rows_in, 16)
            sp.dma_start(vrow[ROW_KVN:VROWS, :], i["mla_kv_norm"][0].rearrange("(k p) -> k p", p=P))\
                .then_inc(rows_in, 16)
            sp.dma_start(brow[:], i["b_ada"].rearrange("l (f p) -> (l f) p", p=P)).then_inc(rows_in, 16)
            for r in range(ROWS):
                sp.dma_start(xtok[r:P:ROWS, 0:NB, :],
                             i["x_sample"][0, r * GRID_W:(r + 1) * GRID_W, :].rearrange("(b c) d -> c b d", b=NB))\
                    .then_inc(x_in, 16)
            sp.dma_start(xtok[:, NB, :], i["x_prompt"][0]).then_inc(x_in, 16)
            for n in range(24):
                if n >= 2:
                    sp.wait_ge(ada_done, n - 1)
                src = i["w_ada"][n // 12].rearrange("(k p) m -> p k m", p=P)
                sp.dma_start(ada[:, n % 2], src[:, :, 512 * (n % 12):512 * (n % 12 + 1)]).then_inc(ada_in[n % 2], 16)
                if n == 1:
                    for j in range(STAGE):
                        load_piece("ac", j)
            for j in range(STAGE, 20):
                load_piece("ac", j)
            load_pieces("rv")
            load_pieces("nv")
            sp.wait_ge(v_done, 8)
            sp.dma_start(dist[:], i["c_dist"]).then_inc(ret_in, 16)
            sp.dma_start(tpos[:], i["c_tpos"]).then_inc(ret_in, 16)
            sp.dma_start(kpos[:], i["c_kpos"]).then_inc(ret_in, 16)
            sp.dma_start(dec[:, 0:8], i["ret_decay_fwd"].to_broadcast([P, NH])).then_inc(ret_in, 16)
            sp.dma_start(dec[:, 8:16], i["ret_decay_bwd"].to_broadcast([P, NH])).then_inc(ret_in, 16)
            sp.dma_start(state[0:64], i["state_ret_fwd"][0, 0].rearrange("h k v -> k h v")).then_inc(ret_in, 16)
            sp.dma_start(state[64:P], i["state_ret_bwd"][0, 0].rearrange("h k v -> k h v")).then_inc(ret_in, 16)
            for j in range(STAGE):
                load_piece("out0", j)
            sp.wait_ge(fin_out, NH)
            sp.dma_start(o["new_ret_fwd"][0, 0].rearrange("h k v -> k h v"), fin[0:64]).then_inc(stored, 16)
            sp.dma_start(o["new_ret_bwd"][0, 0].rearrange("h k v -> k h v"), fin[64:P]).then_inc(stored, 16)
            sp.wait_ge(stored, 32)
            sp.wait_ge(ret_out, NH)
            sp.dma_start(mask[:], i["c_mask"]).then_inc(na_in, 16)
            sp.dma_start(kpast[:], i["cache_na_k"][0, 0].rearrange("h t d -> t h d")).then_inc(na_in, 16)
            sp.dma_start(vpast[:], i["cache_na_v"][0, 0].rearrange("h t d -> t h d")).then_inc(na_in, 16)
            sp.wait_ge(bias_zero, 1)
            rpb = i["na_rpb"]
            for c in range(BLK):
                for r in range(ROWS):
                    q = ROWS * c + r
                    sp.dma_start(bias[q:q + 1, :, :, c + 1:c + 1 + RPB_C],
                                 rpb[0:1, :, ROWS - 1 - r:2 * ROWS - 1 - r, :]).then_inc(na_bias_in, 16)
            sp.dma_start(o["new_na_v"][0, 0].rearrange("h t d -> t h d"),
                         nv[:, NB, :].rearrange("p (h d) -> p h d", h=NH)).then_inc(stored, 16)
            sp.wait_ge(nk_out, NH)
            sp.dma_start(o["new_na_k"][0, 0].rearrange("h t d -> t h d"), nkt[:]).then_inc(stored, 16)
            for j in range(STAGE, 8):
                load_piece("out0", j)
            load_mlp(0)
            load_pieces("in_c")
            sp.dma_start(pastc[:, 0:256], i["cache_mla_ckv"][0, 0]).then_inc(mla_in, 16)
            sp.dma_start(pastc[:, 256:288], i["cache_mla_kpe"][0, 0]).then_inc(mla_in, 16)
            sp.dma_start(rope[:], i["c_rope"]).then_inc(mla_in, 16)
            load_pieces("uq")
            load_pieces("uk")
            sp.wait_ge(tok_out, 1)
            sp.dma_start(o["new_mla_ckv"][0, 0], tokc[:, 0:256]).then_inc(stored, 16)
            sp.dma_start(o["new_mla_kpe"][0, 0], tokc[:, 256:288]).then_inc(stored, 16)
            load_pieces("uv")
            load_pieces("out1")
            load_mlp(1)
            for b in range(5):
                sp.wait_ge(y_out, 2 * b + 2)
            for r in range(ROWS):
                sp.dma_start(o["y_sample"][0, r * GRID_W:(r + 1) * GRID_W, :].rearrange("(b c) d -> c b d", b=NB),
                             ytok[r:P:ROWS, 0:NB, :]).then_inc(stored, 16)
            sp.dma_start(o["y_prompt"][0], ytok[:, NB, :]).then_inc(stored, 16)
            sp.wait_ge(stored, 16 * 15)

        @block.tensor
        def _(pe):
            mm = nc.tensor.matmul

            def free_pair(g, at=0):
                if g >= 2:
                    a, d = EVAC[g - 2]
                    if a:
                        pe.wait_ge(act_evac, a + at)
                    if d:
                        pe.wait_ge(dve_evac, d + at)

            def unit(g, n, k_tiles, m, x_hi, x_lo, at=0, half_at=0, ready=None, base=0, wide=None):
                wide = wide or m
                pe.wait_ge(w_lo_done, n + 1 + at)
                free_pair(g, half_at)
                hi, lo = [w[:, n % 2, 0:k_tiles * wide].rearrange("p (k m) -> p k m", k=k_tiles)[:, :, base:base + m]
                          for w in (w_hi, w_lo)]
                for k in range(k_tiles):
                    if ready:
                        ready(k)
                    for s in range(2):
                        out = ps[0:m, 2 * (g % 2) + s, 0:HALF]
                        xh, xl = [x[:, k, s * HALF:(s + 1) * HALF] for x in (x_hi, x_lo)]
                        mm(out, lo[:, k], xh, start=k == 0, stop=False)
                        mm(out, hi[:, k], xl, start=False, stop=False)
                        last = mm(out, hi[:, k], xh, start=False, stop=k == k_tiles - 1)
                last.then_inc(unit_done, 1)

            def mean_square(name):
                at, no = NORM_AT[name], NORM_NO[name]
                if no:
                    pe.wait_ge(ms_out, no)
                for k in range(NORM_K[name]):
                    pe.wait_ge(sq_done, at + k + 1)
                    for s in range(2):
                        last = mm(ps[:, 4 + s, 0:HALF], ones[:], sq[:, (at + k) % 2, s * HALF:(s + 1) * HALF],
                                  start=k == 0, stop=k == NORM_K[name] - 1)
                    last.then_inc(sq_used, 1)

            def h_ready(name):
                return lambda k: pe.wait_ge(h_lo_done, KD * MOD_NO[name] + k + 1)

            pe.wait_ge(const_in, 16)
            pe.wait_ge(filled, 4)
            pe.wait_ge(rows_in, 16 * 6)
            nc.tensor.transpose(ps[:, 0, 0:VROWS], vrow[:], ident[0:VROWS, 0:VROWS]).then_inc(rows_t, 1)
            nc.tensor.transpose(ps[:, 1, 0:96], brow[:], ident[0:96, 0:96]).then_inc(rows_t, 1)
            pe.wait_ge(x_in, 16 * (ROWS + 1))
            pe.wait_ge(rows_out, 2)
            for j in range(10):
                b, g = j // 2, j % 2
                if j >= 8:
                    pe.wait_ge(x_out, j - 7)
                for n in range(4):
                    last = nc.tensor.transpose(ps[:, j % 8, P * n:P * (n + 1)],
                                               xtok[:, b, P * (4 * g + n):P * (4 * g + n + 1)], ident[:])
                last.then_inc(x_t, 1)

            def turn_mod(n):
                pe.wait_ge(modrow_done, n + 1)
                if n >= 2:
                    pe.wait_ge(mod_out, n - 1)
                for j in range(4):
                    last = nc.tensor.transpose(ps[:, 6 + n % 2, 2 * j:2 * j + 2],
                                               modrow[:, n % 2, P * j:P * (j + 1)], ident[0:2, 0:2])
                last.then_inc(mod_t, 1)

            pe.wait_ge(c_ready, 1)
            pe.wait_ge(x_out, 10)
            for n in range(24):
                pe.wait_ge(ada_in[n % 2], 16 * (n // 2 + 1))
                if n >= 2:
                    pe.wait_ge(modrow_done, n - 1)
                for k in range(KD):
                    last = mm(ps[0:2, 4 + n % 2, :], csil[:, k, :], ada[:, n % 2, k, :],
                              start=k == 0, stop=k == KD - 1)
                last.then_inc(ada_done, 1)
                if n:
                    turn_mod(n - 1)
            turn_mod(23)
            pe.wait_ge(modrow_done, 24)

            mean_square("in0")
            for j in range(20):
                unit(j, j, KD, P, hA_hi, hA_lo, ready=h_ready("in0") if j == 0 else None)
            V_BANKS = (4, 5, 6, 7, 0)
            for part in range(2):
                if part:
                    pe.wait_ge(v_out, 5)
                else:
                    pe.wait_ge(act_evac, EVAC[18][0])
                for j in range(4):
                    n = PIECE_AT["rv"] + 4 * part + j
                    pe.wait_ge(w_lo_done, n + 1)
                    for b in range(5):
                        for kk in range(2):
                            k = 2 * j + kk
                            xh, xl = [x[:, k, P * b:P * (b + 1)] for x in (hA_hi, hA_lo)]
                            wh, wl = [w[:, n % 2, 512 * kk:512 * (kk + 1)] for w in (w_hi, w_lo)]
                            out = ps[:, V_BANKS[b], :]
                            mm(out, xh, wl, start=k == 0, stop=False)
                            mm(out, xl, wh, start=False, stop=False)
                            last = mm(out, xh, wh, start=False, stop=k == KD - 1)
                    last.then_inc(v_done, 1)

            def ret_scores(h):
                q = oT[:, h // 2, :]
                for kt in range(5):
                    if h:
                        pe.wait_ge(sd_done, 5 * (h - 1) + kt + 1)
                    if kt < NB:
                        mm(ps[:, kt, :], kz[:, h, P * kt:P * (kt + 1)], q[:, 0:TL], start=True, stop=True)\
                            .then_inc(rs_done, 1)
                    else:
                        mm(ps[:, 6, 0:P], kz[:, h, TL:T], q[:, TL:T], start=True, stop=True).then_inc(rs_done, 1)

            def ret_values(h):
                pe.wait_ge(qe_done, h + 1)
                pe.wait_ge(sd_done, 5 * h + 5)
                if h >= 2:
                    pe.wait_ge(ret_out, h - 1)
                out = ps[0:HD, 4 + h % 2, :]
                for kt in range(NB):
                    mm(out, rv[:, kt, HD * h:HD * (h + 1)], sd[:, kt, :], start=kt == 0, stop=False)
                mm(out, state[:, h, :], qE[:, h % 2, :], start=False, stop=True)
                if h:
                    pe.wait_ge(ret_out, h)
                mm(ps[0:HD, 7, 0:P], rv[:, NB, HD * h:HD * (h + 1)], sd[:, 4, 0:P],
                   start=True, stop=True).then_inc(ret_done, 1)

            pe.wait_ge(v_out, 10)
            pe.wait_ge(act_evac, 20)
            pe.wait_ge(ret_in, 16 * 7)
            ret_scores(0)
            for h in range(NH):
                if h < NH - 1:
                    ret_scores(h + 1)
                ret_values(h)
            for h in range(NH):
                if h >= 2:
                    pe.wait_ge(kd_done, h - 1)
                nc.tensor.transpose(ps[:, h % 2, 0:P], kz[:, h, TL:T], ident[:]).then_inc(kd_t, 1)
                if h:
                    pe.wait_ge(kd_done, h)
                    if h >= 3:
                        pe.wait_ge(fin_out, h - 2)
                    mm(ps[:, 2 + (h - 1) % 2, 0:HD], kd[:, (h - 1) % 2, :], rv[:, NB, HD * (h - 1):HD * h],
                       start=True, stop=True).then_inc(fin_done, 1)
            pe.wait_ge(kd_done, NH)
            pe.wait_ge(fin_out, NH - 2)
            mm(ps[:, 3, 0:HD], kd[:, 1, :], rv[:, NB, HD * (NH - 1):HD * NH], start=True, stop=True)\
                .then_inc(fin_done, 1)
            pe.wait_ge(ret_out, NH)
            for m in range(4):
                if m:
                    pe.wait_ge(gn_cen, m)
                for s in range(2):
                    last = mm(ps[:, 4 + s, 0:HALF], gnb[:], oT[:, m, s * HALF:(s + 1) * HALF], start=True, stop=True)
                last.then_inc(gn_mm, 1)
                pe.wait_ge(gn_sq, m + 1)
                if m:
                    pe.wait_ge(gn_var, m)
                for s in range(2):
                    last = mm(ps[:, 6 + s, 0:HALF], gnb[:], sq[:, 0, s * HALF:(s + 1) * HALF], start=True, stop=True)
                last.then_inc(gn_mm, 1)

            pe.wait_ge(na_in, 16 * 3)
            pe.wait_ge(fin_out, NH)
            for m in range(4):
                nc.tensor.transpose(ps[:, m, 0:P], kpast[:, 2 * m:2 * m + 2, :].rearrange("p h d -> p (h d)"),
                                    ident[:]).then_inc(past_t, 1)
            pe.wait_ge(gn_var, 4)
            for h in range(NH):
                if h >= 4:
                    pe.wait_ge(nk_out, h - 3)
                nc.tensor.transpose(ps[:, 4 + h % 4, 0:P], kzn[:, h, TL:T], ident[:]).then_inc(nk_t, 1)
            pe.wait_ge(past_out, 4)
            pe.wait_ge(nk_out, NH)
            pe.wait_ge(nvs_done, 1)

            def na_scores(t):
                m, b, h = t // 10, t % 10 // 2, 2 * (t // 10) + t % 2
                if t >= 2:
                    pe.wait_ge(na_max, t - 1)
                q = oT[:, 4 + m, P * b:P * (b + 1)]
                if b < NB:
                    mm(ps[:, t % 2, 0:NKEY], q, kzn[:, h, FIRST_KEY[b]:FIRST_KEY[b] + NKEY], start=True, stop=True)
                    mm(ps[:, t % 2, NKEY:NKEY + NP], q, kzn[:, h, T:T + NP], start=True, stop=True).then_inc(na_s, 1)
                else:
                    mm(ps[:, t % 2, 0:TC], q, kzn[:, h, TL:T], start=True, stop=True).then_inc(na_s, 1)

            def na_turn(t):
                pe.wait_ge(na_p, t + 1)
                if t >= 2:
                    pe.wait_ge(na_pt, t - 1)
                for kt in range(3 if t % 10 < 8 else 1):
                    last = nc.tensor.transpose(ps[:, 2 + t % 2, P * kt:P * (kt + 1)],
                                               pA[:, t % 2, P * kt:P * (kt + 1)], ident[:])
                last.then_inc(na_t, 1)

            def na_values(t):
                b, h = t % 10 // 2, 2 * (t // 10) + t % 2
                pe.wait_ge(na_pt, t + 1)
                if t >= 2:
                    pe.wait_ge(na_out, t - 1)
                hs = slice(HD * h, HD * (h + 1))
                if b < NB:
                    v = [(nv[:, 0], nv[:, 1]), (nvs[:, 0], nvs[:, 1]), (nvs[:, 1], nvs[:, 2]), (nv[:, 2], nv[:, 3])][b]
                    v = [v[0][:, hs], v[1][:, hs], vpast[:, h, :]]
                else:
                    v = [nv[:, NB, hs]]
                for kt in range(len(v)):
                    last = mm(ps[0:HD, 4 + t % 2, 0:P], v[kt], pTA[:, t % 2, P * kt:P * (kt + 1)],
                              start=kt == 0, stop=kt == len(v) - 1)
                last.then_inc(na_pv, 1)

            for t in range(N_NA + 2):
                if t < N_NA:
                    na_scores(t)
                if 1 <= t <= N_NA:
                    na_turn(t - 1)
                if t >= 2:
                    na_values(t - 2)

            def project_out(layer):
                name = f"out{layer}"
                for j in range(8):
                    unit(UNIT_AT[name] + j, PIECE_AT[name] + j, KD, P, h2_hi, h2_lo,
                         ready=(lambda k: pe.wait_ge(o_lo_done, KD * layer + k + 1)) if j == 0 else None)

            def mlp(layer):
                g0, n0 = UNIT_AT[f"mlp{layer}"], PIECE_AT[f"mlp{layer}"]
                with pe.Fori(0, NCH) as c:
                    for j in range(2 * CH):
                        if j < CH:
                            ready = h_ready("in0m" if layer == 0 else "in1m") if j == 0 else None
                            unit(g0 + j, n0 + j, KD, P, hM_hi, hM_lo, at=c * (2 * CH), half_at=c * CH, ready=ready)
                        else:
                            ready = (lambda k: pe.wait_ge(h2_lo_done, layer * NCH * CH + k + 1 + c * CH)) \
                                if j == CH else None
                            unit(g0 + j, n0 + j, CH, P, h2_hi, h2_lo, at=c * (2 * CH), half_at=c * CH, ready=ready)

            pe.wait_ge(na_max, N_NA)
            pe.wait_ge(na_pt, N_NA)
            pe.wait_ge(na_out, N_NA)
            project_out(0)
            mean_square("y0a")
            mean_square("in0m")
            mlp(0)
            mean_square("y0m")
            mean_square("in1")

            g0, n0 = UNIT_AT["in_c"], PIECE_AT["in_c"]
            for j in range(6):
                unit(g0 + j, n0 + j, KD, P if j < 5 else 64, hM_hi, hM_lo, ready=h_ready("in1") if j == 0 else None)
            pe.wait_ge(mla_in, 16 * 3)
            for k in range(KKV):
                nc.tensor.transpose(ps[:, 6, P * k:P * (k + 1)], pastc[:, P * k:P * (k + 1)], ident[:])
            nc.tensor.transpose(ps[0:ROPE, 7, 0:P], pastc[:, 256:288], ident[:]).then_inc(pc_t, 1)
            mean_square("cq")
            mean_square("ckv")
            g0, n0 = UNIT_AT["uq"], PIECE_AT["uq"]
            for h in range(NH_MLA):
                ready = (lambda k: pe.wait_ge(cn_lo, k + 1)) if h == 0 else None
                unit(g0 + h, n0 + h // 2, KQ, P, cq_hi, cq_lo, ready=ready, base=P * (h % 2), wide=2 * P)
            pe.wait_ge(cn_lo, KQ + KKV)
            pe.wait_ge(pc_out, 1)
            for k in range(KKV):
                nc.tensor.transpose(ps[:, 6, P * k:P * (k + 1)], ckn[:, k, TL + NP:T + NP], ident[:])
            nc.tensor.transpose(ps[:, 7, 0:ROPE], cT[0:ROPE, 5, TL:T], ident[0:ROPE, 0:ROPE]).then_inc(tok_t, 1)
            pe.wait_ge(tok_out, 1)
            g0, n0 = UNIT_AT["uk"], PIECE_AT["uk"]
            pe.wait_ge(w_lo_done, n0 + 2)
            for m in range(8):
                g = g0 + m
                free_pair(g)
                for k in range(KKV):
                    wh, wl = [w[:, (n0 + k) % 2, P * m:P * (m + 1)] for w in (w_hi, w_lo)]
                    for s in range(2):
                        out = ps[:, 2 * (g % 2) + s, 0:384]
                        xh, xl = [x[:, k, 384 * s:384 * (s + 1)] for x in (ck_hi, ck_lo)]
                        mm(out, wl, xh, start=k == 0, stop=False)
                        mm(out, wh, xl, start=False, stop=False)
                        last = mm(out, wh, xh, start=False, stop=k == KKV - 1)
                last.then_inc(unit_done, 1)
            n0 = PIECE_AT["uv"]
            pe.wait_ge(w_lo_done, n0 + 2)
            for j in range(12):
                b, s = j // 2, j % 2
                if j >= 4:
                    pe.wait_ge(vm_out, j - 3)
                for k in range(KKV):
                    wh, wl = [w[:, (n0 + k) % 2, 512 * s:512 * (s + 1)] for w in (w_hi, w_lo)]
                    xh, xl = [x[:, k, P * b:P * (b + 1)] for x in (ck_hi, ck_lo)]
                    out = ps[:, 4 + j % 4, :]
                    mm(out, xh, wl, start=k == 0, stop=False)
                    mm(out, xl, wh, start=False, stop=False)
                    last = mm(out, xh, wh, start=False, stop=k == KKV - 1)
                last.then_inc(vm_done, 1)

            def mla_scores(t):
                h, b = t // 5, t % 5
                if t >= 2:
                    pe.wait_ge(m_e, t - 1)
                q = qm[:, h, P * b:P * (b + 1)]
                if b < NB:
                    for s in range(2):
                        last = mm(ps[:, 2 * (t % 2) + s, 0:HALF], q, km[:, h, HALF * s:HALF * (s + 1)],
                                  start=True, stop=True)
                else:
                    last = mm(ps[:, 2 * (t % 2), 0:TC], q, km[:, h, TL + NP:T + NP], start=True, stop=True)
                last.then_inc(m_s, 1)

            def mla_turn(t):
                pe.wait_ge(m_p, t + 1)
                if t:
                    pe.wait_ge(m_pt, t)
                for kt in range(5 if t % 5 < NB else 1):
                    last = nc.tensor.transpose(ps[:, 4 + kt // 4, P * (kt % 4):P * (kt % 4 + 1)],
                                               pM[:, t % 2, P * kt:P * (kt + 1)], ident[:])
                last.then_inc(m_t, 1)

            def mla_values(t):
                h, b = t // 5, t % 5
                pe.wait_ge(m_pt, t + 1)
                if t >= 2:
                    pe.wait_ge(m_out, t - 1)
                tiles = range(5) if b < NB else (5,)
                for j, kt in enumerate(tiles):
                    last = mm(ps[0:HD, 6 + t % 2, 0:P], vm[:, kt, HD * h:HD * (h + 1)],
                              pTM[:, t % 2, P * j:P * (j + 1)], start=j == 0, stop=j == len(tiles) - 1)
                last.then_inc(m_pv, 1)

            pe.wait_ge(act_evac, EVAC[UNIT_AT["uk"] + 7][0])
            pe.wait_ge(vm_out, 12)
            pe.wait_ge(kmas_done, NH_MLA)
            pe.wait_ge(ctx_rope, 1)
            for t in range(N_MLA + 2):
                if t < N_MLA:
                    mla_scores(t)
                if 1 <= t <= N_MLA:
                    mla_turn(t - 1)
                if t >= 2:
                    mla_values(t - 2)
            pe.wait_ge(m_e, N_MLA)
            project_out(1)
            mean_square("y1a")
            mean_square("in1m")
            mlp(1)
            mean_square("y1m")

            pe.wait_ge(dve_evac, EVAC[-1][1])
            pe.wait_ge(ms_out, len(NORMS))
            pe.wait_ge(x_done, 4 * KD)
            for j in range(10):
                b, g = j // 2, j % 2
                if j >= 8:
                    pe.wait_ge(y_out, j - 7)
                for n in range(4):
                    last = nc.tensor.transpose(ps[:, j % 8, P * n:P * (n + 1)],
                                               xT[:, 4 * g + n, P * b:P * (b + 1)], ident[:])
                last.then_inc(y_t, 1)

        @block.scalar
        def _(act):
            chain = Chain(act, "act_chain")
            f = nc.scalar.activation

            def squares(name, src, ready):
                at, no = NORM_AT[name], NORM_NO[name]
                for k in range(NORM_K[name]):
                    ready(k)
                    if at + k >= 2:
                        act.wait_ge(sq_used, at + k - 1)
                    f(sq[:, (at + k) % 2, :], src(k), ACT.Square).then_inc(sq_done, 1)
                act.wait_ge(ms_out, no + 1)
                f(rstd[:], rstd[:], ACT.Sqrt).then_inc(root_done, 1)

            def operand(name, out):
                for k in range(KD):
                    act.wait_ge(h_full, KD * MOD_NO[name] + k + 1)
                    f(out[:, k, :], nt[:, k % 2, :], ACT.Copy).then_inc(h_hi_done, 1)

            def residual_norms(yname, src, xcount, ready):
                squares(yname, lambda k: src[:, k, :], ready)
                if xcount is not None:
                    squares(xcount[0], lambda k: xT[:, k, :], lambda k: act.wait_ge(x_done, xcount[1] + k + 1))

            act.wait_ge(rows_out, 1)
            f(cexp[:], vecT[:, ROW_C:ROW_C + 16], ACT.Exp, scale=-1.0).then_inc(c_exp, 1)
            for n in range(24):
                act.wait_ge(ada_done, n + 1)
                if n >= 2:
                    act.wait_ge(mod_t, n - 1)
                f(modrow[:, n % 2, :], ps[0:2, 4 + n % 2, :], ACT.Copy).then_inc(modrow_done, 1)
            squares("in0", lambda k: xT[:, k, :], lambda k: act.wait_ge(x_out, 10))
            operand("in0", hA_hi)
            act_split(act, 0)
            act.wait_ge(filled, 6)
            for j in range(20):
                act_split(act, j + 1)
                act.wait_ge(unit_done, j + 1)
                kind, m, src = j // 4, j % 4, pair(j)
                if kind == 0:
                    last = f(two(oT[:, m, :]), src, ACT.Copy)
                elif kind == 1:
                    f(two(kz[0:64, 2 * m, :]), pair(j, slice(0, 64)), ACT.Copy, scale=HD ** -0.5)
                    last = f(two(kz[64:P, 2 * m + 1, :]), pair(j, slice(64, P)), ACT.Copy, scale=HD ** -0.5)
                elif kind == 2:
                    last = f(two(gate[:, m, :]), src, ACT.Copy)
                elif kind == 3:
                    last = f(two(oT[:, 4 + m, :]), src, ACT.Copy, scale=HD ** -0.5)
                else:
                    f(two(kzn[0:64, 2 * m, 0:T]), pair(j, slice(0, 64)), ACT.Copy)
                    last = f(two(kzn[64:P, 2 * m + 1, 0:T]), pair(j, slice(64, P)), ACT.Copy)
                last.then_inc(act_evac, 1)
            for n in range(21, 29):
                act_split(act, n)

            act.wait_ge(ret_in, 16 * 7)
            f(lg[:, 0, :], dec[:], ACT.Exp, scale=LN2).then_inc(decay_exp, 1)
            act.wait_ge(decay_arg, 1)
            f(lg[:, 2, :], lg[:, 1, :], ACT.Ln).then_inc(decay_exp, 1)
            act.wait_ge(decay_arg, 2)
            f(kdec[:], kdec[:], ACT.Exp).then_inc(decay_exp, 1)
            act.wait_ge(v_out, 10)

            def ret_copy(h):
                act.wait_ge(ret_done, h + 1)
                rows = slice(64 * (h % 2), 64 * (h % 2) + 64)
                f(oT[rows, h // 2, 0:TL], ps[0:64, 4 + h % 2, :], ACT.Copy)
                f(oT[rows, h // 2, TL:T], ps[0:64, 7, 0:P], ACT.Copy).then_inc(ret_out, 1)

            for h in range(NH):
                rows = slice(64 * (h % 2), 64 * (h % 2) + 64)
                if h >= 2:
                    act.wait_ge(qe_done, h - 1)
                for s in range(2):
                    last = f(edec[rows, s, :], tpos[rows, s, :], ACT.Exp, scale=lg[rows, 7, 8 * s + h:8 * s + h + 1])
                last.then_inc(e_exp, 1)
                act.wait_ge(d_arg, h + 1)
                f(dmat[:, h % 2, :], dmat[:, h % 2, :], ACT.Exp).then_inc(d_exp, 1)
                if h:
                    ret_copy(h - 1)
            ret_copy(NH - 1)
            for h in range(NH):
                act.wait_ge(fin_done, h + 1)
                f(fin[:, h, :], ps[:, 2 + h % 2, 0:HD], ACT.Copy).then_inc(fin_out, 1)
            for m in range(4):
                if m >= 2:
                    act.wait_ge(g_done, m - 1)
                f(nt[:, m % 2, :], gate[:, m, :], ACT.Exp, scale=-1.0).then_inc(g_exp, 1)
            for m in range(4):
                act.wait_ge(gn_cen, m + 1)
                f(sq[:, 0, :], nt[:, 0, :], ACT.Square).then_inc(gn_sq, 1)
                act.wait_ge(gn_var, m + 1)
                f(rstd[:], rstd[:], ACT.Sqrt).then_inc(gn_root, 1)

            for m in range(4):
                act.wait_ge(past_t, m + 1)
                f(kzn[0:64, 2 * m, T:T + NP], ps[0:64, m, 0:P], ACT.Copy)
                f(kzn[64:P, 2 * m + 1, T:T + NP], ps[64:P, m, 0:P], ACT.Copy).then_inc(past_out, 1)
            for h in range(NH):
                act.wait_ge(nk_t, h + 1)
                c = HD * (h % 2)
                f(nkt[:, h, :], ps[:, 4 + h % 4, c:c + HD], ACT.Copy).then_inc(nk_out, 1)

            def na_exp(t):
                w = 384 if t % 10 < 8 else TC
                act.wait_ge(na_max, t + 1)
                if t >= 2:
                    act.wait_ge(na_t, t - 1)
                f(pA[:, t % 2, 0:w], s32[:, t % 2, 0:w], ACT.Exp, bias=smA[:, 1, t % 2:t % 2 + 1],
                  accum_out=smA[:, 2, t % 2:t % 2 + 1]).then_inc(na_e, 1)

            def na_copy(t):
                w = 384 if t % 10 < 8 else TC
                act.wait_ge(na_t, t + 1)
                if t >= 2:
                    act.wait_ge(na_pv, t - 1)
                f(pTA[:, t % 2, 0:w], ps[:, 2 + t % 2, 0:w], ACT.Copy).then_inc(na_pt, 1)

            for t in range(N_NA + 1):
                if t < N_NA:
                    na_exp(t)
                if t:
                    na_copy(t - 1)

            def mlp(layer):
                g0, n0 = UNIT_AT[f"mlp{layer}"], PIECE_AT[f"mlp{layer}"]
                base = layer * NCH * CH

                def chunk(c):
                    at, half = c * (2 * CH), c * CH
                    for j in range(2 * CH):
                        act_split(act, n0 + j + 1, at)
                        if j < CH:
                            act.wait_ge(unit_done, g0 + j + 1 + at)
                            if not isinstance(c, int) or base + j - 1 + half > 0:
                                act.wait_ge(h2_lo_done, base + j - 1 + half)
                            f(two(r32[:, j % 2, :]), pair(g0 + j), ACT.Relu).then_inc(act_evac, 1)
                            act.wait_ge(act_evac, EVAC[g0][0] + j + half)
                            f(h2_hi[:, j, :], r32[:, j % 2, :], ACT.Square).then_inc(h2_hi_done, 1)

                chunk(0)
                with act.Fori(1, NCH - 1) as c:
                    chunk(c)
                chunk(NCH - 1)

            act.wait_ge(na_out, N_NA)
            for k in range(KD):
                f(h2_hi[:, k, :], oT[:, k, :], ACT.Copy).then_inc(o_hi_done, 1)
            for j in range(8):
                act_split(act, PIECE_AT["out0"] + j + 1)
            e0 = EVAC[UNIT_AT["out0"]][1]
            residual_norms("y0a", yT, ("in0m", 0), lambda k: act.wait_ge(dve_evac, e0 + k))
            operand("in0m", hM_hi)
            mlp(0)
            e1 = EVAC[UNIT_AT["in_c"] - 1][1]
            residual_norms("y0m", yT, ("in1", KD), lambda k: act.wait_ge(dve_evac, e1))
            operand("in1", hM_hi)

            for j in range(6):
                g, n = UNIT_AT["in_c"] + j, PIECE_AT["in_c"] + j
                act_split(act, n + 1)
                act.wait_ge(unit_done, g + 1)
                m = P if j < 5 else 64
                f(two(cT[0:m, j, :]), pair(g, slice(0, m)), ACT.Copy).then_inc(act_evac, 1)
            e2 = EVAC[UNIT_AT["in_c"]][0]
            act.wait_ge(pc_t, 1)
            for k in range(KKV):
                f(ckn[:, k, TL:TL + NP], ps[:, 6, P * k:P * (k + 1)], ACT.Copy)
            act.wait_ge(km_zero, 1)
            f(kmas[96:P, TL:TL + NP], ps[0:ROPE, 7, 0:P], ACT.Copy).then_inc(pc_out, 1)
            squares("cq", lambda k: cT[:, k, :], lambda k: act.wait_ge(act_evac, e2 + k))
            for k in range(KQ):
                act.wait_ge(cn_full, k + 1)
                f(cq_hi[:, k, :], nt[:, k % 2, :], ACT.Copy).then_inc(cn_hi, 1)
            squares("ckv", lambda k: cT[:, KQ + k, :], lambda k: act.wait_ge(act_evac, e2 + KQ + k))
            act.wait_ge(pc_out, 1)
            for k in range(KKV):
                act.wait_ge(cn_full, KQ + k + 1)
                f(ck_hi[:, k, :], ckn[:, k, :], ACT.Copy).then_inc(cn_hi, 1)
            f(kmas[96:P, TL + NP:T + NP], cT[0:ROPE, 5, TL:T], ACT.Copy).then_inc(km_rope, 1)
            for h in range(NH_MLA):
                g = UNIT_AT["uq"] + h
                if h % 2 == 0:
                    act_split(act, PIECE_AT["uq"] + h // 2 + 1)
                act.wait_ge(unit_done, g + 1)
                if h == 0:
                    act.wait_ge(cn_lo, KQ)
                f(two(qm[0:64, h, :]), pair(g, slice(0, 64)), ACT.Copy, scale=MLA_SCALE)
                f(two(qm[96:P, h, :]), pair(g, slice(64, 96)), ACT.Copy, scale=MLA_SCALE).then_inc(act_evac, 1)
            act.wait_ge(tok_t, 1)
            f(tokc[:, 0:256], ps[:, 6, 0:256], ACT.Copy)
            f(tokc[:, 256:288], ps[:, 7, 0:ROPE], ACT.Copy).then_inc(tok_out, 1)
            act_split(act, PIECE_AT["uk"] + 1)
            act.wait_ge(tok_out, 1)
            act.wait_ge(stored, 16 * 6)
            act.wait_ge(qrope_done, NH_MLA)
            act.wait_ge(km_rope, 2)
            for m in range(8):
                g = UNIT_AT["uk"] + m
                act.wait_ge(unit_done, g + 1)
                for s in range(2):
                    src = ps[64 * s:64 * s + 64, 2 * (g % 2):2 * (g % 2) + 2, 0:384]
                    last = f(km[0:64, 2 * m + s, :].rearrange("p (n c) -> p n c", n=2), src, ACT.Copy)
                last.then_inc(act_evac, 1)
            act_split(act, PIECE_AT["uv"])
            act_split(act, PIECE_AT["uv"] + 1)
            act.wait_ge(vm_done, 12)

            def mla_exp(t):
                act.wait_ge(m_max, t + 1)
                if t >= 2:
                    act.wait_ge(m_t, t - 1)
                b2 = 2 * (t % 2)
                if t % 5 < NB:
                    src, dst = ps[:, b2:b2 + 2, 0:HALF], two(pM[:, t % 2, :])
                else:
                    src, dst = ps[:, b2, 0:TC], pM[:, t % 2, 0:TC]
                f(dst, src, ACT.Exp, bias=smM[:, 0, t % 2:t % 2 + 1], accum_out=smM[:, 1, t % 2:t % 2 + 1])\
                    .then_inc(m_e, 1)

            def mla_copy(t):
                act.wait_ge(m_t, t + 1)
                if t >= 2:
                    act.wait_ge(m_pv, t - 1)
                w = T if t % 5 < NB else TC
                src = ps[:, 4:6, :].rearrange("p n c -> p (n c)")
                f(pTM[:, t % 2, 0:w], src[:, 0:w], ACT.Copy).then_inc(m_pt, 1)

            for t in range(N_MLA + 1):
                if t < N_MLA:
                    mla_exp(t)
                if t:
                    mla_copy(t - 1)
            act_split(act, PIECE_AT["out1"])
            act.wait_ge(m_out, N_MLA)
            act.wait_ge(m_pv, N_MLA)
            for k in range(KD):
                for s in range(2):
                    rows = slice(64 * s, 64 * s + 64)
                    last = f(h2_hi[rows, k, :], qm[rows, 2 * k + s, :], ACT.Copy)
                last.then_inc(o_hi_done, 1)
            for j in range(8):
                act_split(act, PIECE_AT["out1"] + j + 1)
            e3 = EVAC[UNIT_AT["out1"]][1]
            residual_norms("y1a", yT, ("in1m", 2 * KD), lambda k: act.wait_ge(dve_evac, e3 + k))
            operand("in1m", hM_hi)
            mlp(1)
            residual_norms("y1m", yT, None, lambda k: act.wait_ge(dve_evac, EVAC[-1][1]))
            for j in range(10):
                b, g = j // 2, j % 2
                act.wait_ge(y_t, j + 1)
                f(ytok[:, b, 512 * g:512 * (g + 1)], ps[:, j % 8, :], ACT.Copy).then_inc(y_out, 1)

        @block.vector
        def _(dve):
            chain = Chain(dve, "dve_chain")
            link = chain.link
            tt, ts, stt = nc.vector.tensor_tensor, nc.vector.tensor_scalar, nc.vector.scalar_tensor_tensor

            def root(name, features):
                at, no = NORM_AT[name], NORM_NO[name]
                dve.wait_ge(sq_used, at + NORM_K[name])
                ts(two(rstd[:]), ps[:, 4:6, 0:HALF], 1.0 / features, EPS, ALU.mult, ALU.add).then_inc(ms_out, 1)
                dve.wait_ge(root_done, no + 1)
                link(nc.vector.reciprocal(rstd[:], rstd[:]))

            def add_residual(name, layer, which):
                root(name, D)
                first = KD * (2 * layer + (which == G2))
                for k in range(KD):
                    if k >= 2:
                        dve.wait_ge(x_done, first + k - 1)
                    link(tt(nt[:, k % 2, :], yT[:, k, :], rstd[:], ALU.mult))
                    for g, (a, b) in enumerate(SPAN):
                        last = stt(xT[:, k, a:b], nt[:, k % 2, a:b], coef[:, layer, which, k, g:g + 1],
                                   xT[:, k, a:b], ALU.mult, ALU.add)
                    last.then_inc(x_done, 1)

            def modulate(name, layer, which, shift):
                root(name, D)
                for k in range(KD):
                    if k >= 2:
                        dve.wait_ge(h_lo_done, KD * MOD_NO[name] + k - 1)
                    link(tt(nt[:, k % 2, :], xT[:, k, :], rstd[:], ALU.mult))
                    for g, (a, b) in enumerate(SPAN):
                        last = ts(nt[:, k % 2, a:b], nt[:, k % 2, a:b], coef[:, layer, which, k, g:g + 1],
                                  mod[:, layer, 8 * shift + k, g:g + 1], ALU.mult, ALU.add)
                    last.then_inc(h_full, 1)

            def coefficients(layer):
                for g in range(2):
                    for which, part in ((A1, SCALE1), (G1, GATE1), (A2, SCALE2), (G2, GATE2)):
                        gain = vecT[:, ROW_GAIN + 32 * layer + 8 * which:ROW_GAIN + 32 * layer + 8 * which + 8]
                        m = mod[:, layer, 8 * part:8 * part + 8, g]
                        last = stt(coef[:, layer, which, :, g], m, 1.0 if which in (A1, A2) else 0.0, gain,
                                   ALU.add, ALU.mult)
                link(last)

            dve.wait_ge(rows_t, 1)
            nc.vector.tensor_copy(vecT[:], ps[:, 0, 0:VROWS]).then_inc(rows_out, 1)
            dve.wait_ge(rows_t, 2)
            nc.vector.tensor_copy(badaT[:].rearrange("p l f -> p (l f)"), ps[:, 1, 0:96]).then_inc(rows_out, 1)
            dve.wait_ge(c_exp, 1)
            link(ts(cexp[:], cexp[:], 1.0, None, ALU.add))
            link(nc.vector.reciprocal(cexp[:], cexp[:]))
            for g in range(2):
                last = tt(csil[:, :, g], vecT[:, ROW_C + 8 * g:ROW_C + 8 * g + 8], cexp[:, 8 * g:8 * g + 8], ALU.mult)
            last.then_inc(c_ready, 1)
            for j in range(10):
                b, g = j // 2, j % 2
                dve.wait_ge(x_t, j + 1)
                nc.vector.tensor_copy(xT[:, 4 * g:4 * g + 4, P * b:P * (b + 1)],
                                      ps[:, j % 8, :].rearrange("p (k t) -> p k t", k=4)).then_inc(x_out, 1)
            for n in range(24):
                layer, c = n // 12, n % 12
                dve.wait_ge(mod_t, n + 1)
                cols = ps[:, 6 + n % 2, 0:8].rearrange("p (j g) -> p j g", g=2)
                for g in range(2):
                    last = tt(mod[:, layer, 4 * c:4 * c + 4, g], cols[:, :, g], badaT[:, layer, 4 * c:4 * c + 4],
                              ALU.add)
                last.then_inc(mod_out, 1)
                if c == 11:
                    dve.wait_ge(mod_out, n + 1)
                    coefficients(layer)

            modulate("in0", 0, A1, SHIFT1)
            dve_split(dve, 0)
            for n in range(1, 24):
                dve_split(dve, n)
            dve_split(dve, 24)
            for part in range(2):
                if part:
                    for n in range(25, 29):
                        dve_split(dve, n)
                dve.wait_ge(v_done, 4 * part + 4)
                for b in range(5):
                    nc.vector.tensor_copy((nv if part else rv)[:, b, :], ps[:, (4, 5, 6, 7, 0)[b], :])\
                        .then_inc(v_out, 1)

            dve.wait_ge(decay_exp, 1)
            y, w, ln, z, z2, s, big, out = [lg[:, n, :] for n in range(8)]
            link(ts(w, y, -1.0, 1.0, ALU.mult, ALU.add))
            ts(w, w, 1e-30, None, ALU.max).then_inc(decay_arg, 1)
            ts(big, y, 0.5, None, ALU.is_gt)
            link(ts(y, y, 0.5, None, ALU.min))
            link(ts(z, y, -1.0, 2.0, ALU.mult, ALU.add))
            link(nc.vector.reciprocal(z, z))
            link(tt(z, z, y, ALU.mult))
            link(tt(z2, z, z, ALU.mult))
            link(ts(s, z2, 1.0 / 21, 1.0 / 19, ALU.mult, ALU.add))
            for d in range(17, 0, -2):
                link(tt(s, s, z2, ALU.mult))
                link(ts(s, s, 1.0 / d, None, ALU.add))
            link(tt(s, s, z, ALU.mult))
            link(ts(s, s, -2.0, None, ALU.mult))
            dve.wait_ge(decay_exp, 2)
            link(tt(ln, ln, s, ALU.subtract))
            link(tt(ln, ln, big, ALU.mult))
            link(tt(out, ln, s, ALU.add))
            for s_ in range(2):
                last = ts(kdec[:, s_, :], out[:, 8 * s_:8 * s_ + 8], kpos[:, s_:s_ + 1], None, ALU.mult)
            last.then_inc(decay_arg, 1)

            def decay_args(h):
                link(ts(dmat[:, h % 2, :], dist[:, 1, :], out[:, 8 + h:9 + h], None, ALU.mult))
                stt(dmat[:, h % 2, :], dist[:, 0, :], out[:, h:h + 1], dmat[:, h % 2, :], ALU.mult, ALU.add)\
                    .then_inc(d_arg, 1)

            dve.wait_ge(decay_arg, 2)
            decay_args(0)
            for h in range(NH):
                rows = slice(64 * (h % 2), 64 * (h % 2) + 64)
                dve.wait_ge(e_exp, h + 1)
                if h >= 2:
                    dve.wait_ge(ret_done, h - 1)
                for s_ in range(2):
                    last = tt(qE[64 * s_:64 * s_ + 64, h % 2, :], oT[rows, h // 2, 0:TL], edec[rows, s_, :], ALU.mult)
                last.then_inc(qe_done, 1)
                dve.wait_ge(d_exp, h + 1)
                for c in (384, 896):
                    last = tt(dmat[:, h % 2, c:c + P], dmat[:, h % 2, c:c + P], ident[:], ALU.add)
                link(last)
                if h < NH - 1:
                    decay_args(h + 1)
                if h:
                    dve.wait_ge(ret_done, h)
                for kt in range(5):
                    dve.wait_ge(rs_done, 5 * h + kt + 1)
                    if kt < NB:
                        c = ROWS * (48 - BLK * kt)
                        tt(sd[:, kt, :], ps[:, kt, :], dmat[:, h % 2, c:c + TL], ALU.mult).then_inc(sd_done, 1)
                    else:
                        tt(sd[:, 4, 0:P], ps[:, 6, 0:P], dmat[:, h % 2, 896:1024], ALU.mult).then_inc(sd_done, 1)
            dve.wait_ge(decay_exp, 3)
            for h in range(NH):
                dve.wait_ge(kd_t, h + 1)
                if h >= 2:
                    dve.wait_ge(fin_done, h - 1)
                c = HD * (h % 2)
                for s_ in range(2):
                    last = ts(kd[:, h % 2, HD * s_:HD * (s_ + 1)], ps[:, h % 2, c:c + HD], kdec[:, s_, h:h + 1], None,
                              ALU.mult)
                last.then_inc(kd_done, 1)
            for m in range(4):
                dve.wait_ge(g_exp, m + 1)
                link(ts(nt[:, m % 2, :], nt[:, m % 2, :], 1.0, None, ALU.add))
                link(nc.vector.reciprocal(nt[:, m % 2, :], nt[:, m % 2, :]))
                tt(gate[:, m, :], gate[:, m, :], nt[:, m % 2, :], ALU.mult).then_inc(g_done, 1)
            dve.wait_ge(g_done, 4)
            for m in range(4):
                if m:
                    dve.wait_ge(gn_done, m)
                dve.wait_ge(gn_mm, 2 * m + 1)
                tt(two(nt[:, 0, :]), two(oT[:, m, :]), ps[:, 4:6, 0:HALF], ALU.subtract).then_inc(gn_cen, 1)
                dve.wait_ge(gn_mm, 2 * m + 2)
                ts(two(rstd[:]), ps[:, 6:8, 0:HALF], EPS, None, ALU.add).then_inc(gn_var, 1)
                dve.wait_ge(gn_root, m + 1)
                link(nc.vector.reciprocal(rstd[:], rstd[:]))
                link(tt(nt[:, 0, :], nt[:, 0, :], rstd[:], ALU.mult))
                tt(oT[:, m, :], nt[:, 0, :], gate[:, m, :], ALU.mult).then_inc(gn_done, 1)

            dve.wait_ge(na_in, 16 * 3)
            for j in range(3):
                nc.vector.tensor_copy(nvs[0:64, j, :], nv[64:P, j, :])
                last = nc.vector.tensor_copy(nvs[64:P, j, :], nv[0:64, j + 1, :])
            last.then_inc(nvs_done, 1)

            def na_rowmax(t):
                w = 384 if t % 10 < 8 else TC
                n = 8 * (t // 10) + t % 10
                dve.wait_ge(na_s, t + 1)
                if t % 10 < 8:
                    dve.wait_ge(bm_done, n + 1)
                    add = bm[:, n % 2, :]
                else:
                    add = bm[:, 0, NKEY:NKEY + NP]
                if t >= 2:
                    dve.wait_ge(na_e, t - 1)
                e = t % 2
                link(nc.vector.tensor_tensor_reduce(s32[:, e, 0:w], ps[:, e, 0:w], add, 1.0, LOWEST, ALU.add, ALU.max,
                                                    smA[:, 0, e:e + 1]))
                ts(smA[:, 1, e:e + 1], smA[:, 0, e:e + 1], -1.0, None, ALU.mult).then_inc(na_max, 1)

            def na_norm(t):
                w = 384 if t % 10 < 8 else TC
                e = t % 2
                dve.wait_ge(na_e, t + 1)
                link(nc.vector.reciprocal(smA[:, 3, e:e + 1], smA[:, 2, e:e + 1]))
                ts(pA[:, e, 0:w], pA[:, e, 0:w], smA[:, 3, e:e + 1], None, ALU.mult).then_inc(na_p, 1)

            def na_store(t):
                m, b = t // 10, t % 10 // 2
                rows = slice(64 * (t % 2), 64 * (t % 2) + 64)
                dve.wait_ge(na_pv, t + 1)
                nc.vector.tensor_copy(oT[rows, 4 + m, P * b:P * (b + 1)], ps[0:64, 4 + t % 2, 0:P])\
                    .then_inc(na_out, 1)

            for t in range(N_NA + 3):
                if t < N_NA:
                    na_rowmax(t)
                if 1 <= t <= N_NA:
                    na_norm(t - 1)
                if t >= 3:
                    na_store(t - 3)

            def project_out(layer):
                for j in range(8):
                    dve_split(dve, PIECE_AT[f"out{layer}"] + j + 1)
                    g = UNIT_AT[f"out{layer}"] + j
                    dve.wait_ge(unit_done, g + 1)
                    nc.vector.tensor_copy(two(yT[:, j, :]), pair(g)).then_inc(dve_evac, 1)

            def mlp(layer):
                g0, n0 = UNIT_AT[f"mlp{layer}"], PIECE_AT[f"mlp{layer}"]
                base = layer * NCH * CH
                dve.wait_ge(y_zero, layer + 1)

                def chunk(c):
                    at, half = c * (2 * CH), c * CH
                    for j in range(2 * CH):
                        dve_split(dve, n0 + j + 1, at)
                        if j < CH:
                            dve.wait_ge(act_evac, EVAC[g0][0] + j + half)
                            tt(s2[:, j % 2, :], r32[:, j % 2, :], r32[:, j % 2, :], ALU.mult)\
                                .then_inc(chain.sem, 1)
                            dve.wait_ge(chain.sem, chain.n + j + 1 + half)
                            dve.wait_ge(h2_hi_done, base + j + 1 + half)
                            tt(h2_lo[:, j, :], s2[:, j % 2, :], h2_hi[:, j, :].bitcast(F32), ALU.subtract)\
                                .then_inc(h2_lo_done, 1)
                        else:
                            dve.wait_ge(unit_done, g0 + j + 1 + at)
                            y = two(yT[:, j - CH, :])
                            tt(y, y, pair(g0 + j), ALU.add).then_inc(dve_evac, 1)

                with dve.Fori(0, NCH - 1) as c:
                    chunk(c)
                chunk(NCH - 1)
                chain.n += NCH * CH

            project_out(0)
            add_residual("y0a", 0, G1)
            modulate("in0m", 0, A2, SHIFT2)
            mlp(0)
            add_residual("y0m", 0, G2)
            modulate("in1", 1, A1, SHIFT1)

            for j in range(6):
                dve_split(dve, PIECE_AT["in_c"] + j + 1)
            root("cq", KQ * P)
            for k in range(KQ):
                if k >= 2:
                    dve.wait_ge(cn_lo, k - 1)
                link(tt(nt[:, k % 2, :], cT[:, k, :], rstd[:], ALU.mult))
                ts(nt[:, k % 2, :], nt[:, k % 2, :], vecT[:, ROW_QN + k:ROW_QN + k + 1], None, ALU.mult)\
                    .then_inc(cn_full, 1)
            root("ckv", KKV * P)
            dve.wait_ge(cn_lo, KQ)
            dve.wait_ge(pc_out, 1)
            for k in range(KKV):
                link(tt(nt[:, k, :], cT[:, KQ + k, :], rstd[:], ALU.mult))
                gain = vecT[:, ROW_KVN + k:ROW_KVN + k + 1]
                ts(ckn[:, k, 0:TL], nt[:, k, 0:TL], gain, None, ALU.mult)
                ts(ckn[:, k, TL + NP:T + NP], nt[:, k, TL:T], gain, None, ALU.mult).then_inc(cn_full, 1)
            dve.wait_ge(act_evac, EVAC[UNIT_AT["in_c"] + 5][0])
            tt(rt[0:ROPE, 0, :], cT[0:ROPE, 5, 0:TL], rope[0:ROPE, :], ALU.mult)
            link(tt(rt[0:ROPE, 1, :], cT[ROPE:64, 5, 0:TL], rope[ROPE:64, :], ALU.mult))
            tt(kmas[64:96, 0:TL], rt[0:ROPE, 0, :], rt[0:ROPE, 1, :], ALU.add).then_inc(km_rope, 1)
            for h in range(NH_MLA):
                g = UNIT_AT["uq"] + h
                if h % 2 == 0:
                    dve_split(dve, PIECE_AT["uq"] + h // 2 + 1)
                dve.wait_ge(act_evac, EVAC[g][0])
                if h:
                    dve.wait_ge(qrope_done, h)
                for s_, (a, b) in enumerate(((0, HALF), (HALF, TL))):
                    bank = 2 * (g % 2) + s_
                    tt(rt[64:96, 0, a:b], ps[64:96, bank, 0:b - a], rope[64:96, a:b], ALU.mult)
                    last = tt(rt[64:96, 1, a:b], ps[96:P, bank, 0:b - a], rope[96:P, a:b], ALU.mult)
                last.then_inc(dve_evac, 1)
                dve.wait_ge(dve_evac, EVAC[g][1])
                tt(qm[64:96, h, 0:TL], rt[64:96, 0, :], rt[64:96, 1, :], ALU.add).then_inc(qrope_done, 1)
            dve_split(dve, PIECE_AT["uk"] + 1)
            dve_split(dve, PIECE_AT["uv"])
            dve_split(dve, PIECE_AT["uv"] + 1)
            for j in range(12):
                dve.wait_ge(vm_done, j + 1)
                if j == 0:
                    dve.wait_ge(unit_done, UNIT_AT["uq"] + NH_MLA)
                nc.vector.tensor_copy(vm[:, j // 2, 512 * (j % 2):512 * (j % 2 + 1)], ps[:, 4 + j % 4, :])\
                    .then_inc(vm_out, 1)

            def mla_rowmax(t):
                e, b2 = t % 2, 2 * (t % 2)
                dve.wait_ge(m_s, t + 1)
                if t >= 2:
                    dve.wait_ge(m_e, t - 1)
                src = ps[:, b2:b2 + 2, 0:HALF] if t % 5 < NB else ps[:, b2, 0:TC]
                nc.vector.tensor_reduce(smM[:, 0, e:e + 1], src, AX.XY if t % 5 < NB else AX.X, ALU.max,
                                        negate=True).then_inc(m_max, 1)

            def mla_norm(t):
                w, e = (T if t % 5 < NB else TC), t % 2
                dve.wait_ge(m_e, t + 1)
                link(nc.vector.reciprocal(smM[:, 2, e:e + 1], smM[:, 1, e:e + 1]))
                ts(pM[:, e, 0:w], pM[:, e, 0:w], smM[:, 2, e:e + 1], None, ALU.mult).then_inc(m_p, 1)

            def mla_store(t):
                h, b = t // 5, t % 5
                dve.wait_ge(m_pv, t + 1)
                rows = slice(64 * (h % 2), 64 * (h % 2) + 64)
                nc.vector.tensor_copy(qm[rows, h, P * b:P * (b + 1)], ps[0:64, 6 + t % 2, 0:P]).then_inc(m_out, 1)

            for t in range(N_MLA + 3):
                if t < N_MLA:
                    mla_rowmax(t)
                if 1 <= t <= N_MLA:
                    mla_norm(t - 1)
                if t >= 3:
                    mla_store(t - 3)
            dve_split(dve, PIECE_AT["out1"])
            project_out(1)
            add_residual("y1a", 1, G1)
            modulate("in1m", 1, A2, SHIFT2)
            mlp(1)
            add_residual("y1m", 1, G2)

        @block.gpsimd
        def _(pool):
            sub = nc.gpsimd.tensor_tensor
            nc.gpsimd.memset(ones[:], 1.0).then_inc(filled, 1)
            nc.gpsimd.memset(gnb[:], 0.0).then_inc(filled, 1)
            pool.wait_ge(filled, 2)
            nc.gpsimd.memset(gnb[0:64, 0:64], 1.0 / HD).then_inc(filled, 1)
            nc.gpsimd.memset(gnb[64:P, 64:P], 1.0 / HD).then_inc(filled, 1)
            pool.wait_ge(filled, 4)
            pool.wait_ge(x_out, 10)
            pool.wait_ge(ada_done, 24)
            pool.wait_ge(mod_t, 24)
            nc.gpsimd.memset(kz[:], 0.0).then_inc(filled, 1)
            pool.wait_ge(filled, 5)
            nc.gpsimd.memset(kzn[:], 0.0).then_inc(filled, 1)

            def low_parts(name, hi, lo):
                for k in range(KD):
                    pool.wait_ge(h_hi_done, KD * MOD_NO[name] + k + 1)
                    sub(lo[:, k, :], nt[:, k % 2, :], hi[:, k, :].bitcast(F32), ALU.subtract).then_inc(h_lo_done, 1)

            low_parts("in0", hA_hi, hA_lo)
            pool.wait_ge(stored, 32)
            pool.wait_ge(ret_out, NH)
            pool.wait_ge(fin_out, NH)
            nc.gpsimd.memset(bm[:], 0.0)
            nc.gpsimd.memset(bias[:], 0.0).then_inc(bias_zero, 1)
            pool.wait_ge(na_in, 16 * 3)
            pool.wait_ge(na_bias_in, 16 * BLK * ROWS)
            for n in range(8 * 4):
                m, b, h = n // 8, n % 8 // 2, 2 * (n // 8) + n % 2
                if n >= 2:
                    pool.wait_ge(na_max, 10 * ((n - 2) // 8) + (n - 2) % 8 + 1)
                u = (16, 8, 8, 0)[b]
                sub(bm[:, n % 2, 0:NKEY].rearrange("p (c r) -> p c r", r=ROWS),
                    bias[:, h, :, u:u + KW].rearrange("p r c -> p c r"),
                    mask[:, b, :].rearrange("p (c r) -> p c r", r=ROWS), ALU.add).then_inc(bm_done, 1)

            def output_low(layer, src):
                for k in range(KD):
                    pool.wait_ge(o_hi_done, KD * layer + k + 1)
                    src(k).then_inc(o_lo_done, 1)

            output_low(0, lambda k: sub(h2_lo[:, k, :], oT[:, k, :], h2_hi[:, k, :].bitcast(F32), ALU.subtract))
            pool.wait_ge(ms_out, NORM_NO["y0a"] + 1)
            pool.wait_ge(x_done, KD)
            nc.gpsimd.memset(yT[:], 0.0).then_inc(y_zero, 1)
            low_parts("in0m", hM_hi, hM_lo)
            low_parts("in1", hM_hi, hM_lo)
            pool.wait_ge(h_lo_done, 3 * KD)
            nc.gpsimd.memset(kmas[64:P, :], 0.0).then_inc(km_zero, 1)
            pool.wait_ge(km_zero, 1)
            for k in range(KQ):
                pool.wait_ge(cn_hi, k + 1)
                sub(cq_lo[:, k, :], nt[:, k % 2, :], cq_hi[:, k, :].bitcast(F32), ALU.subtract).then_inc(cn_lo, 1)
            for k in range(KKV):
                pool.wait_ge(cn_hi, KQ + k + 1)
                sub(ck_lo[:, k, :], ckn[:, k, :], ck_hi[:, k, :].bitcast(F32), ALU.subtract).then_inc(cn_lo, 1)
            pool.wait_ge(cn_lo, KQ + KKV)
            nc.gpsimd.memset(qm[64:96, :, TL:T], 0.0).then_inc(ctx_rope, 1)
            pool.wait_ge(ctx_rope, 1)
            pool.wait_ge(km_rope, 2)
            pool.wait_ge(pc_out, 1)
            pool.wait_ge(tok_out, 1)
            pool.wait_ge(stored, 16 * 6)
            pool.wait_ge(qrope_done, NH_MLA)
            for h in range(NH_MLA):
                nc.gpsimd.tensor_copy(km[64:P, h, :], kmas[64:P, :]).then_inc(kmas_done, 1)

            pool.wait_ge(kmas_done, NH_MLA)
            chain = Chain(pool, "pool_chain")

            def heads_low(k):
                for s in range(2):
                    rows = slice(64 * s, 64 * s + 64)
                    if s:
                        chain.link(last)
                    elif k:
                        pool.wait_ge(o_lo_done, KD + k)
                    last = sub(h2_lo[rows, k, :], qm[rows, 2 * k + s, :], h2_hi[rows, k, :].bitcast(F32), ALU.subtract)
                return last

            output_low(1, heads_low)
            pool.wait_ge(x_done, 3 * KD)
            nc.gpsimd.memset(yT[:], 0.0).then_inc(y_zero, 1)
            low_parts("in1m", hM_hi, hM_lo)


_INS = ["x_prompt", "x_sample", "state_ret_fwd", "state_ret_bwd", "cache_na_k", "cache_na_v", "cache_mla_ckv",
        "cache_mla_kpe", "c", "c_ctx", "w_ada", "b_ada", "norm_gains", "w_mlp_in", "w_mlp_out", "w_in_ac",
        "w_out_ac", "ret_decay_fwd", "ret_decay_bwd", "na_rpb", "mla_q_norm", "mla_kv_norm", "w_uk", "w_uv",
        "w_out_c"]
_OUTS = [("y_prompt", (1, 128, 1024)), ("y_sample", (1, 512, 1024)), ("new_ret_fwd", (1, 1, 8, 64, 64)),
         ("new_ret_bwd", (1, 1, 8, 64, 64)), ("new_na_k", (1, 1, 8, 128, 64)), ("new_na_v", (1, 1, 8, 128, 64)),
         ("new_mla_ckv", (1, 1, 128, 256)), ("new_mla_kpe", (1, 1, 128, 32))]


def shape_constants():
    import numpy as np

    part = np.arange(P)
    col, row = part // ROWS, part % ROWS
    u, rq = np.divmod(np.arange(112 * ROWS), ROWS)
    lat = (rq[None, :] - row[:, None]) * GRID_W + (u[None, :] - 48 - col[:, None])
    ctx = part[None, :] - part[:, None]
    d = np.concatenate([lat, ctx], axis=1)
    dist = np.stack([np.maximum(d, 0), np.maximum(-d, 0)], axis=1).astype(np.float32)
    token = np.arange(TL)
    time = (token % ROWS) * GRID_W + token // ROWS
    tpos = np.broadcast_to(np.stack([time + 1, TL - time]), (P, 2, TL)).astype(np.float32)
    kpos = np.stack([P - 1 - part, part], axis=1).astype(np.float32)
    mask = np.zeros((P, NB, KW, ROWS), np.float32)
    for b in range(NB):
        first = int(np.clip(b * BLK - 8, 0, GRID_W - KW))
        qc = b * BLK + col
        start = np.clip(qc - 8, 0, GRID_W - 16)
        kc = first + np.arange(KW)
        ok = (kc[None, :] >= start[:, None]) & (kc[None, :] < start[:, None] + 16)
        mask[:, b] = np.where(ok, 0.0, -1e30)[:, :, None]
    nf = ROPE // 4
    inv = (np.float32(10000.0) ** (-np.arange(nf, dtype=np.float32) / np.float32(nf))).astype(np.float32)
    ang = np.concatenate([(time // GRID_W).astype(np.float32)[:, None] * inv,
                          (time % GRID_W).astype(np.float32)[:, None] * inv], axis=-1)
    cos = np.repeat(np.cos(ang), 2, axis=1).T
    sin = np.repeat(np.sin(ang), 2, axis=1).T * np.where(np.arange(ROPE) % 2 == 0, -1.0, 1.0)[:, None]
    rope = np.concatenate([cos, sin, cos * MLA_SCALE, sin * MLA_SCALE]).astype(np.float32)
    return {"c_ident": np.eye(P, dtype=np.float32), "c_dist": dist, "c_tpos": tpos, "c_kpos": kpos,
            "c_mask": mask.reshape(P, NB, NKEY), "c_rope": rope}


def kernel(**inputs):
    import concourse.bacc as bacc
    import numpy as np
    from concourse.bass_utils import run_bass_kernel_spmd as run

    nc = bacc.Bacc("TRN2", target_bir_lowering=False, num_devices=1)
    arrays = {name: np.ascontiguousarray(inputs[name]) for name in _INS}
    swap = np.arange(ROPE) ^ 1
    w = np.asarray(inputs["w_in_c"])[0]
    arrays["w_in_c_swap"] = np.ascontiguousarray(np.concatenate([w, w[:, 640 + swap]], axis=1))
    w = np.asarray(inputs["w_uq"])[0].reshape(KQ * P, NH_MLA, 96)
    arrays["w_uq_heads"] = np.ascontiguousarray(
        np.concatenate([w, w[:, :, 64 + swap]], axis=2).reshape(KQ * P, NH_MLA * P))
    arrays.update(shape_constants())
    ins, feed = {}, {}
    for name, a in arrays.items():
        feed[f"in_{name}"] = a
        ins[name] = nc.dram_tensor(f"in_{name}", a.shape, mybir.dt.from_np(a.dtype), kind="ExternalInput").ap()
    outs = {name: nc.dram_tensor(f"out_{name}", shape, F32, kind="ExternalOutput").ap() for name, shape in _OUTS}
    build(nc, ins, outs)
    r = run(nc, [feed], core_ids=[0])
    return tuple(r.results[0][f"out_{name}"] for name, _ in _OUTS)
```

```python
from contextlib import ExitStack

import concourse.bass as bass
from concourse import mybir

F32 = mybir.dt.float32
F32R = mybir.dt.float32r
ALU = mybir.AluOpType
ACT = mybir.ActivationFunctionType
AX = mybir.AxisListType

P = 128
D = 1024
KD = D // P
TL, TC = 512, 128
T = TL + TC
NP = 128
HALF = T // 2
ROWS, GRID_W = 8, 64
BLK = P // ROWS
NB = TL // P
HD = 64
NH = 8
NH_MLA = 16
KW = 32
NKEY = KW * ROWS
RPB_R, RPB_C = 15, 31
KQ, KKV = 3, 2
ROPE = 32
DFF = 4096
CH = 8
NCH = DFF // (CH * P)
EPS = 1e-6
MLA_SCALE = 96 ** -0.5
LN2 = 0.6931471805599453
LOWEST = -3.0e38

STAGE = 4
PIECE = 1024

SHIFT1, SCALE1, GATE1, SHIFT2, SCALE2, GATE2 = range(6)
A1, G1, A2, G2 = range(4)
ROW_GAIN, ROW_C, ROW_CTX, ROW_QN, ROW_KVN, VROWS = 0, 64, 72, 80, 83, 85

NORMS = (("in0", KD), ("y0a", KD), ("in0m", KD), ("y0m", KD), ("in1", KD), ("cq", KQ), ("ckv", KKV),
         ("y1a", KD), ("in1m", KD), ("y1m", KD))
PIECES = (("ac", 20), ("rv", 4), ("nv", 4), ("out0", 8), ("mlp0", 16 * NCH), ("in_c", 6),
          ("uq", 8), ("uk", 2), ("uv", 2), ("out1", 8), ("mlp1", 16 * NCH))
UNITS = (("ac", 20, "a"), ("out0", 8, "d"), ("mlp0", 16 * NCH, None), ("in_c", 6, "a"), ("uq", 16, "ad"),
         ("uk", 8, "a"), ("out1", 8, "d"), ("mlp1", 16 * NCH, None))


def first_of(table):
    out, at = {}, 0
    for row in table:
        out[row[0]] = at
        at += row[1]
    out["end"] = at
    return out


def evacuations():
    a = d = 0
    out = []
    for _, n, who in UNITS:
        for j in range(n):
            w = who or ("a" if j % 16 < 8 else "d")
            a += "a" in w
            d += "d" in w
            out.append((a if "a" in w else 0, d if "d" in w else 0))
    return out


NORM_AT = first_of(NORMS)
NORM_NO = {name: n for n, (name, _) in enumerate(NORMS)}
NORM_K = dict(NORMS)
PIECE_AT = first_of(PIECES)
UNIT_AT = first_of(UNITS)
EVAC = evacuations()
MOD_NO = {"in0": 0, "in0m": 1, "in1": 2, "in1m": 3}
N_NA = NH * (NB + 1)
N_MLA = NH_MLA * (NB + 1)
ADA_W = 256
N_ADA = 2 * 6 * D // ADA_W
ADA_RING = 3
ADA_SPLIT = 13
FIRST_KEY = (0, 64, 192, 256)
SPAN = ((0, TL), (TL, T))


def build(nc, i, o):
    top = ExitStack()
    with top:
        def sem(name):
            return top.enter_context(nc.semaphore(name))

        def sb(name, shape, dt=F32, stack=top):
            return stack.enter_context(nc.sbuf_tensor(name, shape, dt))

        def lay(offset, *rows):
            with ExitStack() as s:
                if offset:
                    sb(f"pad{len(pads)}", [P, offset * 256], stack=s)
                    pads.append(offset)
                return [sb(name, shape, dt, s) for name, shape, dt in rows]

        pads = []
        ps = top.enter_context(nc.psum_tensor("ps", [P, 8, 512], F32))

        def pair(g, rows=slice(0, P)):
            b = 2 * (g % 2)
            return ps[rows, b:b + 2, 0:HALF]

        def two(ap):
            return ap.rearrange("p (n c) -> p n c", n=2)

        xT = sb("xT", [P, KD, T])
        ident = sb("ident", [P, P])
        ones = sb("ones", [P, P])
        gnb = sb("gnb", [P, P])
        vecT = sb("vecT", [P, VROWS])
        badaT = sb("badaT", [P, 2, 48])
        mod = sb("mod", [P, 2, 48, 2])
        coef = sb("coef", [P, 2, 4, KD, 2])
        csil, cexp = sb("csil", [P, KD, 2]), sb("cexp", [P, 16])
        dec, lg, kpos, kdec = sb("dec", [P, 16]), sb("lg", [P, 8, 16]), sb("kpos", [P, 2]), sb("kdec", [P, 2, NH])
        rstd = sb("rstd", [P, T])
        sq = sb("sq", [P, 2, T])
        nt = sb("nt", [P, 2, T])
        stage = sb("stage", [P, STAGE, PIECE])
        w_hi = sb("w_hi", [P, 2, PIECE], F32R)
        w_lo = sb("w_lo", [P, 2, PIECE], F32R)

        xtok, vrow, brow = lay(0, ("xtok", [P, 5, D], F32), ("vrow", [VROWS, P], F32), ("brow", [96, P], F32))
        ada_a, modrow_a = lay(64, ("ada_a", [P, ADA_RING, KD, ADA_W], F32), ("modrow_a", [2, 2, ADA_W], F32))
        ada_b, modrow_b = lay(44, ("ada_b", [P, ADA_RING, KD, ADA_W], F32), ("modrow_b", [2, 2, ADA_W], F32))
        oT, kzn, kz, rv, gate, nv, hA_hi, hA_lo = lay(
            0, ("oT", [P, KD, T], F32), ("kzn", [P, NH, T + NP], F32), ("kz", [P, NH, T], F32),
            ("rv", [P, 5, 512], F32), ("gate", [P, 4, T], F32), ("nv", [P, 5, 512], F32),
            ("hA_hi", [P, KD, T], F32R), ("hA_lo", [P, KD, T], F32R))
        dmat, tpos, edec, qE, sd, state, kd, fin = lay(
            94, ("dmat", [P, 2, 1024], F32), ("tpos", [P, 2, TL], F32),
            ("edec", [P, 2, TL], F32), ("qE", [P, 2, TL], F32), ("sd", [P, 5, 512], F32),
            ("state", [P, NH, HD], F32), ("kd", [P, 2, P], F32), ("fin", [P, NH, HD], F32))
        [dist] = lay(134, ("dist", [P, 1024], F32))
        bias, mask, bm, kpast, vpast, s32, pA, pTA, smA, nkt, nvs = lay(
            94, ("bias", [P, NH, ROWS, 48], F32), ("mask", [P, NB, NKEY], F32), ("bm", [P, 2, NKEY + NP], F32),
            ("kpast", [P, NH, HD], F32), ("vpast", [P, NH, HD], F32), ("s32", [P, 2, 384], F32),
            ("pA", [P, 3, 384], F32), ("pTA", [P, 2, 384], F32), ("smA", [P, 4, 3], F32),
            ("nkt", [P, NH, HD], F32), ("nvs", [P, 3, 512], F32))
        hM_hi, hM_lo, h2_hi, h2_lo, yT, r32, s2 = lay(
            0, ("hM_hi", [P, KD, T], F32R), ("hM_lo", [P, KD, T], F32R), ("h2_hi", [P, CH, T], F32R),
            ("h2_lo", [P, CH, T], F32R), ("yT", [P, KD, T], F32), ("r32", [P, 2, T], F32), ("s2", [P, 2, T], F32))
        qm, km, vm, ck_hi, ck_lo, kmas, rope, ckn = lay(
            0, ("qm", [P, NH_MLA, T], F32), ("km", [P, NH_MLA, T + NP], F32), ("vm", [P, 6, D], F32),
            ("ck_hi", [P, KKV, T + NP], F32R), ("ck_lo", [P, KKV, T + NP], F32R), ("kmas", [P, T + NP], F32),
            ("rope", [P, TL], F32), ("ckn", [P, KKV, T + NP], F32))
        [cT] = lay(40, ("cT", [P, 6, T], F32))
        pastc, tokc, rt = lay(60, ("pastc", [P, 288], F32), ("tokc", [P, 288], F32), ("rt", [P, 2, TL], F32))
        cq_hi, cq_lo = lay(88, ("cq_hi", [P, KQ, T], F32R), ("cq_lo", [P, KQ, T], F32R))
        pM, pTM, smM = lay(112, ("pM", [P, 3, T], F32), ("pTM", [P, 2, T], F32), ("smM", [P, 3, 3], F32))
        [ytok] = lay(0, ("ytok", [P, 5, D], F32))

        const_in, rows_in, x_in = sem("const_in"), sem("rows_in"), sem("x_in")
        ada_in = [sem(f"ada_in{n}") for n in range(ADA_RING)]
        decay_in, dist_in = sem("decay_in"), sem("dist_in")
        w_in = [sem(f"w_in{n}") for n in range(STAGE)]
        ret_in, na_in, na_bias_in, mla_in = sem("ret_in"), sem("na_in"), sem("na_bias_in"), sem("mla_in")
        stored = sem("stored")
        w_hi_done, w_lo_done = sem("w_hi_done"), sem("w_lo_done")
        unit_done, act_evac, dve_evac = sem("unit_done"), sem("act_evac"), sem("dve_evac")
        filled, rows_t, rows_out, x_t, x_out = [sem(n) for n in ("filled", "rows_t", "rows_out", "x_t", "x_out")]
        c_exp, c_ready = sem("c_exp"), sem("c_ready")
        ada_done, modrow_done, mod_t, mod_out = [sem(n) for n in ("ada_done", "modrow_done", "mod_t", "mod_out")]
        sq_done, sq_used, ms_out, root_done = [sem(n) for n in ("sq_done", "sq_used", "ms_out", "root_done")]
        x_done, h_full, h_hi_done, h_lo_done = [sem(n) for n in ("x_done", "h_full", "h_hi_done", "h_lo_done")]
        v_done, v_out = sem("v_done"), sem("v_out")
        decay_exp, decay_arg = sem("decay_exp"), sem("decay_arg")
        d_arg, d_exp, e_exp, qe_done = [sem(n) for n in ("d_arg", "d_exp", "e_exp", "qe_done")]
        rs_done, sd_done, ret_done, ret_out = [sem(n) for n in ("rs_done", "sd_done", "ret_done", "ret_out")]
        kd_t, kd_done, fin_done, fin_out = [sem(n) for n in ("kd_t", "kd_done", "fin_done", "fin_out")]
        g_exp, g_done, gn_mm, gn_cen, gn_sq, gn_var, gn_root, gn_done = [
            sem(n) for n in ("g_exp", "g_done", "gn_mm", "gn_cen", "gn_sq", "gn_var", "gn_root", "gn_done")]
        bias_zero, bm_done, past_t, past_out, nk_t, nk_out, nvs_done = [
            sem(n) for n in ("bias_zero", "bm_done", "past_t", "past_out", "nk_t", "nk_out", "nvs_done")]
        na_s, na_max, na_e, na_p, na_t, na_pt, na_pv, na_out = [
            sem(n) for n in ("na_s", "na_max", "na_e", "na_p", "na_t", "na_pt", "na_pv", "na_out")]
        o_hi_done, o_lo_done = sem("o_hi_done"), sem("o_lo_done")
        h2_hi_done, h2_lo_done, y_zero = sem("h2_hi_done"), sem("h2_lo_done"), sem("y_zero")
        cn_full, cn_hi, cn_lo = sem("cn_full"), sem("cn_hi"), sem("cn_lo")
        pc_t, pc_out, tok_t, tok_out, kmas_done, km_rope, qrope_done, vm_done, vm_out, km_zero, ctx_rope = [
            sem(n) for n in ("pc_t", "pc_out", "tok_t", "tok_out", "kmas_done", "km_rope", "qrope_done", "vm_done",
                             "vm_out", "km_zero", "ctx_rope")]
        m_s, m_max, m_e, m_p, m_t, m_pt, m_pv, m_out = [
            sem(n) for n in ("m_s", "m_max", "m_e", "m_p", "m_t", "m_pt", "m_pv", "m_out")]
        y_t, y_out = sem("y_t"), sem("y_out")

        class Chain:

            def __init__(self, engine, name):
                self.engine, self.sem, self.n, self.at = engine, sem(name), 0, 0

            def link(self, instruction):
                self.n += 1
                instruction.then_inc(self.sem, 1)
                self.engine.wait_ge(self.sem, self.at + self.n)

        w_ac = i["w_in_ac"][0].rearrange("(k p) m -> p k m", p=P)
        mats = {
            "out0": i["w_out_ac"][0].rearrange("(k p) m -> p k m", p=P),
            "in_c": i["w_in_c_swap"].rearrange("(k p) m -> p k m", p=P),
            "uq": i["w_uq_heads"].rearrange("(k p) m -> p k m", p=P),
            "uk": i["w_uk"][0].rearrange("(k p) m -> p k m", p=P),
            "uv": i["w_uv"][0].rearrange("(k p) m -> p k m", p=P),
            "out1": i["w_out_c"][0].rearrange("(k p) m -> p k m", p=P),
        }
        mlp_in = [i["w_mlp_in"][n].rearrange("(k p) m -> p k m", p=P) for n in range(2)]
        mlp_out = [i["w_mlp_out"][n].rearrange("(k p) m -> p k m", p=P) for n in range(2)]
        AC_COLS = [0, 512, 1536, 2048, 2560]
        RV_COL, NV_COL = 1024, 3072

        def piece_source(name, j):
            if name == "ac":
                c = AC_COLS[j // 4] + P * (j % 4)
                return w_ac[:, :, c:c + P]
            if name in ("rv", "nv"):
                c = RV_COL if name == "rv" else NV_COL
                return w_ac[:, 2 * j:2 * j + 2, c:c + 512]
            if name == "in_c":
                return mats[name][:, :, P * j:min(P * (j + 1), 704)]
            if name == "uq":
                return mats[name][:, :, 2 * P * j:2 * P * (j + 1)]
            if name in ("uk", "uv"):
                return mats[name][:, j:j + 1, :]
            if name.startswith("mlp"):
                layer, c, j = int(name[3]), j // 16, j % 16
                if j < CH:
                    return mlp_in[layer][:, :, P * (CH * c + j):P * (CH * c + j + 1)]
                return mlp_out[layer][:, CH * c:CH * (c + 1), P * (j - CH):P * (j - CH + 1)]
            return mats[name][:, :, P * j:P * (j + 1)]

        def piece_width(n):
            for name, k in PIECES:
                if PIECE_AT[name] <= n < PIECE_AT[name] + k:
                    if name == "in_c" and n - PIECE_AT[name] == 5:
                        return KD * 64
                    return 768 if name == "uq" else PIECE
            return PIECE


        def piece_used(n):
            name = [x for x, k in PIECES if PIECE_AT[x] <= n][-1]
            j = n - PIECE_AT[name]
            if name in ("rv", "nv"):
                return v_done, j + 1 + 4 * (name == "nv")
            if name == "uv":
                return vm_done, 12
            if name == "uk":
                return unit_done, UNIT_AT["uk"] + 8
            if name == "uq":
                return unit_done, UNIT_AT["uq"] + 2 * j + 2
            return unit_done, UNIT_AT[name] + j + 1

        def act_split(act, n, at=0):
            if isinstance(at, int) and n + at >= PIECE_AT["end"]:
                return
            width = piece_width(n)
            act.wait_ge(w_in[n % STAGE], 16 * (n // STAGE + 1) + at * (16 // STAGE))
            if n >= 2:
                used, count = piece_used(n - 2)
                act.wait_ge(used, count + at)
            nc.scalar.activation(w_hi[:, n % 2, 0:width], stage[:, n % STAGE, 0:width], ACT.Copy)\
                .then_inc(w_hi_done, 1)

        def dve_split(dve, n, at=0):
            if isinstance(at, int) and n + at >= PIECE_AT["end"]:
                return
            width = piece_width(n)
            dve.wait_ge(w_hi_done, n + 1 + at)
            nc.vector.tensor_tensor(w_lo[:, n % 2, 0:width], stage[:, n % STAGE, 0:width],
                                    w_hi[:, n % 2, 0:width].bitcast(F32), ALU.subtract).then_inc(w_lo_done, 1)

        def load_ada(queue, n):
            src = i["w_ada"][n // (N_ADA // 2)].rearrange("(k p) m -> p k m", p=P)
            c = ADA_W * (n % (N_ADA // 2))
            ring = ada_a if n < ADA_SPLIT else ada_b
            queue.dma_start(ring[:, n % ADA_RING], src[:, :, c:c + ADA_W]).then_inc(ada_in[n % ADA_RING], 16)

        def gn_step(n):
            s, odd = divmod(n - ADA_SPLIT - 4, 2)
            return s if 0 <= s < 8 and not odd else None

        block = top.enter_context(nc.Block())
        grid = lambda x: x.rearrange("(r c) d -> c r d", c=GRID_W)

        @block.sync
        def _(sp):
            def load_piece(name, j):
                n = PIECE_AT[name] + j
                src = piece_source(name, j)
                if n >= STAGE:
                    sp.wait_ge(w_lo_done, n - STAGE + 1)
                dst = stage[:, n % STAGE, 0:piece_width(n)].rearrange("p (k m) -> p k m", k=src.shape[1])
                sp.dma_start(dst, src).then_inc(w_in[n % STAGE], 16)

            def load_pieces(name):
                for j in range(dict(PIECES)[name]):
                    load_piece(name, j)

            def load_mlp(layer):
                first = PIECE_AT[f"mlp{layer}"]
                with sp.Fori(0, NCH) as c:
                    for j in range(2 * CH):
                        n = first + j
                        sp.wait_ge(w_lo_done, n - STAGE + 1 + c * (2 * CH))
                        if j < CH:
                            src = mlp_in[layer][:, :, bass.ds(c * (CH * P) + P * j, P)]
                        else:
                            src = mlp_out[layer][:, bass.ds(c * CH, CH), P * (j - CH):P * (j - CH + 1)]
                        sp.dma_start(stage[:, n % STAGE, :].rearrange("p (k m) -> p k m", k=KD), src)\
                            .then_inc(w_in[n % STAGE], 16)

            sp.dma_start(ident[:], i["c_ident"]).then_inc(const_in, 16)
            sp.dma_start(vrow[ROW_C:ROW_C + 8, :], i["c"][0].rearrange("(k p) -> k p", p=P)).then_inc(rows_in, 16)
            sp.dma_start(vrow[ROW_CTX:ROW_CTX + 8, :], i["c_ctx"].rearrange("(k p) -> k p", p=P)).then_inc(rows_in, 16)
            sp.dma_start(vrow[0:64, :], i["norm_gains"].rearrange("l g (k p) -> (l g k) p", p=P)).then_inc(rows_in, 16)
            sp.dma_start(vrow[ROW_QN:ROW_QN + KQ, :], i["mla_q_norm"][0].rearrange("(k p) -> k p", p=P))\
                .then_inc(rows_in, 16)
            sp.dma_start(vrow[ROW_KVN:VROWS, :], i["mla_kv_norm"][0].rearrange("(k p) -> k p", p=P))\
                .then_inc(rows_in, 16)
            sp.dma_start(brow[:], i["b_ada"].rearrange("l (f p) -> (l f) p", p=P)).then_inc(rows_in, 16)
            for n in range(ADA_RING):
                load_ada(sp, n)
            for r in range(ROWS):
                sp.dma_start(xtok[r:P:ROWS, 0:NB, :],
                             i["x_sample"][0, r * GRID_W:(r + 1) * GRID_W, :].rearrange("(b c) d -> c b d", b=NB))\
                    .then_inc(x_in, 16)
            sp.dma_start(xtok[:, NB, :], i["x_prompt"][0]).then_inc(x_in, 16)
            sp.dma_start(kpos[:], i["c_kpos"]).then_inc(decay_in, 16)
            sp.dma_start(dec[:, 0:8], i["ret_decay_fwd"].to_broadcast([P, NH])).then_inc(decay_in, 16)
            sp.dma_start(dec[:, 8:16], i["ret_decay_bwd"].to_broadcast([P, NH])).then_inc(decay_in, 16)
            for n in range(ADA_RING, ADA_SPLIT):
                sp.wait_ge(ada_done, n - ADA_RING + 1)
                load_ada(sp, n)
                if n == 8:
                    for j in range(STAGE):
                        load_piece("ac", j)
            sp.dma_start(dist[:], i["c_dist"]).then_inc(dist_in, 16)
            for j in range(STAGE, 20):
                load_piece("ac", j)
            load_pieces("rv")
            load_pieces("nv")
            sp.wait_ge(v_done, 8)
            sp.dma_start(tpos[:], i["c_tpos"]).then_inc(ret_in, 16)
            sp.dma_start(state[0:64], i["state_ret_fwd"][0, 0].rearrange("h k v -> k h v")).then_inc(ret_in, 16)
            sp.dma_start(state[64:P], i["state_ret_bwd"][0, 0].rearrange("h k v -> k h v")).then_inc(ret_in, 16)
            for j in range(STAGE):
                load_piece("out0", j)
            sp.wait_ge(fin_out, NH)
            sp.dma_start(o["new_ret_fwd"][0, 0].rearrange("h k v -> k h v"), fin[0:64]).then_inc(stored, 16)
            sp.dma_start(o["new_ret_bwd"][0, 0].rearrange("h k v -> k h v"), fin[64:P]).then_inc(stored, 16)
            sp.wait_ge(stored, 32)
            sp.wait_ge(ret_out, NH)
            sp.dma_start(mask[:], i["c_mask"]).then_inc(na_in, 16)
            sp.dma_start(kpast[:], i["cache_na_k"][0, 0].rearrange("h t d -> t h d")).then_inc(na_in, 16)
            sp.dma_start(vpast[:], i["cache_na_v"][0, 0].rearrange("h t d -> t h d")).then_inc(na_in, 16)
            sp.wait_ge(bias_zero, 1)
            rpb = i["na_rpb"]
            for c in range(BLK):
                for r in range(ROWS):
                    q = ROWS * c + r
                    sp.dma_start(bias[q:q + 1, :, :, c + 1:c + 1 + RPB_C],
                                 rpb[0:1, :, ROWS - 1 - r:2 * ROWS - 1 - r, :]).then_inc(na_bias_in, 16)
            sp.dma_start(o["new_na_v"][0, 0].rearrange("h t d -> t h d"),
                         nv[:, NB, :].rearrange("p (h d) -> p h d", h=NH)).then_inc(stored, 16)
            sp.wait_ge(nk_out, NH)
            sp.dma_start(o["new_na_k"][0, 0].rearrange("h t d -> t h d"), nkt[:]).then_inc(stored, 16)
            for j in range(STAGE, 8):
                load_piece("out0", j)
            load_mlp(0)
            load_pieces("in_c")
            sp.dma_start(pastc[:, 0:256], i["cache_mla_ckv"][0, 0]).then_inc(mla_in, 16)
            sp.dma_start(pastc[:, 256:288], i["cache_mla_kpe"][0, 0]).then_inc(mla_in, 16)
            sp.dma_start(rope[:], i["c_rope"]).then_inc(mla_in, 16)
            load_pieces("uq")
            load_pieces("uk")
            sp.wait_ge(tok_out, 1)
            sp.dma_start(o["new_mla_ckv"][0, 0], tokc[:, 0:256]).then_inc(stored, 16)
            sp.dma_start(o["new_mla_kpe"][0, 0], tokc[:, 256:288]).then_inc(stored, 16)
            load_pieces("uv")
            load_pieces("out1")
            load_mlp(1)
            for b in range(5):
                sp.wait_ge(y_out, 2 * b + 2)
            for r in range(ROWS):
                sp.dma_start(o["y_sample"][0, r * GRID_W:(r + 1) * GRID_W, :].rearrange("(b c) d -> c b d", b=NB),
                             ytok[r:P:ROWS, 0:NB, :]).then_inc(stored, 16)
            sp.dma_start(o["y_prompt"][0], ytok[:, NB, :]).then_inc(stored, 16)
            sp.wait_ge(stored, 16 * 15)

        @block.tensor
        def _(pe):
            mm = nc.tensor.matmul

            def free_pair(g, at=0):
                if g >= 2:
                    a, d = EVAC[g - 2]
                    if a:
                        pe.wait_ge(act_evac, a + at)
                    if d:
                        pe.wait_ge(dve_evac, d + at)

            def unit(g, n, k_tiles, m, x_hi, x_lo, at=0, half_at=0, ready=None, base=0, wide=None):
                wide = wide or m
                pe.wait_ge(w_lo_done, n + 1 + at)
                free_pair(g, half_at)
                hi, lo = [w[:, n % 2, 0:k_tiles * wide].rearrange("p (k m) -> p k m", k=k_tiles)[:, :, base:base + m]
                          for w in (w_hi, w_lo)]
                for k in range(k_tiles):
                    if ready:
                        ready(k)
                    for s in range(2):
                        out = ps[0:m, 2 * (g % 2) + s, 0:HALF]
                        xh, xl = [x[:, k, s * HALF:(s + 1) * HALF] for x in (x_hi, x_lo)]
                        mm(out, lo[:, k], xh, start=k == 0, stop=False)
                        mm(out, hi[:, k], xl, start=False, stop=False)
                        last = mm(out, hi[:, k], xh, start=False, stop=k == k_tiles - 1)
                last.then_inc(unit_done, 1)

            def mean_square(name):
                at, no = NORM_AT[name], NORM_NO[name]
                if no:
                    pe.wait_ge(ms_out, no)
                for k in range(NORM_K[name]):
                    pe.wait_ge(sq_done, at + k + 1)
                    for s in range(2):
                        last = mm(ps[:, 4 + s, 0:HALF], ones[:], sq[:, (at + k) % 2, s * HALF:(s + 1) * HALF],
                                  start=k == 0, stop=k == NORM_K[name] - 1)
                    last.then_inc(sq_used, 1)

            def h_ready(name):
                return lambda k: pe.wait_ge(h_lo_done, KD * MOD_NO[name] + k + 1)

            pe.wait_ge(const_in, 16)
            pe.wait_ge(filled, 4)
            pe.wait_ge(rows_in, 16 * 6)
            nc.tensor.transpose(ps[:, 3, 0:VROWS], vrow[:], ident[0:VROWS, 0:VROWS]).then_inc(rows_t, 1)
            nc.tensor.transpose(ps[:, 4, 0:96], brow[:], ident[0:96, 0:96]).then_inc(rows_t, 1)

            def turn_mod(n):
                pe.wait_ge(modrow_done, n + 1)
                if n:
                    pe.wait_ge(mod_out, n)
                modrow = modrow_a if n < ADA_SPLIT else modrow_b
                for j in range(2):
                    last = nc.tensor.transpose(ps[:, 2, 2 * j:2 * j + 2],
                                               modrow[:, n % 2, P * j:P * (j + 1)], ident[0:2, 0:2])
                last.then_inc(mod_t, 1)

            def ada_step(n):
                pe.wait_ge(ada_in[n % ADA_RING], 16 * (n // ADA_RING + 1))
                if n >= 2:
                    pe.wait_ge(modrow_done, n - 1)
                ring = ada_a if n < ADA_SPLIT else ada_b
                for k in range(KD):
                    last = mm(ps[0:2, n % 2, 0:ADA_W], csil[:, k, :], ring[:, n % ADA_RING, k, :],
                              start=k == 0, stop=k == KD - 1)
                last.then_inc(ada_done, 1)
                if n not in (0, 8, ADA_SPLIT):
                    turn_mod(n - 1)
                if n in (7, ADA_SPLIT - 1, N_ADA - 1):
                    turn_mod(n)

            pe.wait_ge(c_ready, 1)
            for n in range(3):
                ada_step(n)
            pe.wait_ge(x_in, 16 * (ROWS + 1))
            pe.wait_ge(rows_out, 2)
            for j in range(10):
                b, g = j // 2, j % 2
                if j >= 5:
                    pe.wait_ge(x_out, j - 4)
                for n in range(4):
                    last = nc.tensor.transpose(ps[:, 3 + j % 5, P * n:P * (n + 1)],
                                               xtok[:, b, P * (4 * g + n):P * (4 * g + n + 1)], ident[:])
                last.then_inc(x_t, 1)
            ada_step(3)
            ada_step(4)
            mean_square("in0")
            for n in range(5, ADA_SPLIT):
                ada_step(n)

            pe.wait_ge(mod_out, ADA_SPLIT)
            for j in range(20):
                unit(j, j, KD, P, hA_hi, hA_lo, ready=h_ready("in0") if j == 0 else None)
            V_BANKS = (4, 5, 6, 7, 0)
            for part in range(2):
                if part:
                    pe.wait_ge(v_out, 5)
                else:
                    pe.wait_ge(act_evac, EVAC[18][0])
                for j in range(4):
                    n = PIECE_AT["rv"] + 4 * part + j
                    pe.wait_ge(w_lo_done, n + 1)
                    for b in range(5):
                        for kk in range(2):
                            k = 2 * j + kk
                            xh, xl = [x[:, k, P * b:P * (b + 1)] for x in (hA_hi, hA_lo)]
                            wh, wl = [w[:, n % 2, 512 * kk:512 * (kk + 1)] for w in (w_hi, w_lo)]
                            out = ps[:, V_BANKS[b], :]
                            mm(out, xh, wl, start=k == 0, stop=False)
                            mm(out, xl, wh, start=False, stop=False)
                            last = mm(out, xh, wh, start=False, stop=k == KD - 1)
                    last.then_inc(v_done, 1)

            def ret_scores(h):
                q = oT[:, h // 2, :]
                for kt in range(5):
                    if h:
                        pe.wait_ge(sd_done, 5 * (h - 1) + kt + 1)
                    if kt < NB:
                        mm(ps[:, kt, :], kz[:, h, P * kt:P * (kt + 1)], q[:, 0:TL], start=True, stop=True)\
                            .then_inc(rs_done, 1)
                    else:
                        mm(ps[:, 6, 0:P], kz[:, h, TL:T], q[:, TL:T], start=True, stop=True).then_inc(rs_done, 1)

            def ret_values(h):
                pe.wait_ge(qe_done, h + 1)
                pe.wait_ge(sd_done, 5 * h + 5)
                if h >= 2:
                    pe.wait_ge(ret_out, h - 1)
                out = ps[0:HD, 4 + h % 2, :]
                for kt in range(NB):
                    mm(out, rv[:, kt, HD * h:HD * (h + 1)], sd[:, kt, :], start=kt == 0, stop=False)
                mm(out, state[:, h, :], qE[:, h % 2, :], start=False, stop=True)
                if h:
                    pe.wait_ge(ret_out, h)
                mm(ps[0:HD, 7, 0:P], rv[:, NB, HD * h:HD * (h + 1)], sd[:, 4, 0:P],
                   start=True, stop=True).then_inc(ret_done, 1)

            pe.wait_ge(v_out, 10)
            pe.wait_ge(act_evac, 20)
            pe.wait_ge(ret_in, 16 * 3)
            ret_scores(0)
            for h in range(NH):
                if h < NH - 1:
                    ret_scores(h + 1)
                ret_values(h)
            for h in range(NH):
                if h >= 2:
                    pe.wait_ge(kd_done, h - 1)
                nc.tensor.transpose(ps[:, h % 2, 0:P], kz[:, h, TL:T], ident[:]).then_inc(kd_t, 1)
                if h:
                    pe.wait_ge(kd_done, h)
                    if h >= 3:
                        pe.wait_ge(fin_out, h - 2)
                    mm(ps[:, 2 + (h - 1) % 2, 0:HD], kd[:, (h - 1) % 2, :], rv[:, NB, HD * (h - 1):HD * h],
                       start=True, stop=True).then_inc(fin_done, 1)
            pe.wait_ge(kd_done, NH)
            pe.wait_ge(fin_out, NH - 2)
            mm(ps[:, 3, 0:HD], kd[:, 1, :], rv[:, NB, HD * (NH - 1):HD * NH], start=True, stop=True)\
                .then_inc(fin_done, 1)
            pe.wait_ge(ret_out, NH)
            for n in range(ADA_SPLIT, N_ADA):
                ada_step(n)
                s = gn_step(n)
                if s is None:
                    continue
                m = s // 2
                if s % 2 == 0:
                    if m:
                        pe.wait_ge(gn_cen, m)
                    for s in range(2):
                        last = mm(ps[:, 4 + s, 0:HALF], gnb[:], oT[:, m, s * HALF:(s + 1) * HALF],
                                  start=True, stop=True)
                else:
                    pe.wait_ge(gn_sq, m + 1)
                    if m:
                        pe.wait_ge(gn_var, m)
                    for s in range(2):
                        last = mm(ps[:, 6 + s, 0:HALF], gnb[:], sq[:, 0, s * HALF:(s + 1) * HALF],
                                  start=True, stop=True)
                last.then_inc(gn_mm, 1)

            pe.wait_ge(mod_out, N_ADA)
            pe.wait_ge(na_in, 16 * 3)
            pe.wait_ge(fin_out, NH)
            for m in range(4):
                nc.tensor.transpose(ps[:, m, 0:P], kpast[:, 2 * m:2 * m + 2, :].rearrange("p h d -> p (h d)"),
                                    ident[:]).then_inc(past_t, 1)
            pe.wait_ge(gn_var, 4)
            for h in range(NH):
                if h >= 4:
                    pe.wait_ge(nk_out, h - 3)
                nc.tensor.transpose(ps[:, 4 + h % 4, 0:P], kzn[:, h, TL:T], ident[:]).then_inc(nk_t, 1)
            pe.wait_ge(past_out, 4)
            pe.wait_ge(nk_out, NH)
            pe.wait_ge(nvs_done, 1)

            def na_scores(t):
                m, b, h = t // 10, t % 10 // 2, 2 * (t // 10) + t % 2
                if t >= 2:
                    pe.wait_ge(na_max, t - 1)
                q = oT[:, 4 + m, P * b:P * (b + 1)]
                if b < NB:
                    mm(ps[:, t % 2, 0:NKEY], q, kzn[:, h, FIRST_KEY[b]:FIRST_KEY[b] + NKEY], start=True, stop=True)
                    mm(ps[:, t % 2, NKEY:NKEY + NP], q, kzn[:, h, T:T + NP], start=True, stop=True).then_inc(na_s, 1)
                else:
                    mm(ps[:, t % 2, 0:TC], q, kzn[:, h, TL:T], start=True, stop=True).then_inc(na_s, 1)

            def na_turn(t):
                pe.wait_ge(na_p, t + 1)
                if t >= 2:
                    pe.wait_ge(na_pt, t - 1)
                for kt in range(3 if t % 10 < 8 else 1):
                    last = nc.tensor.transpose(ps[:, 2 + t % 2, P * kt:P * (kt + 1)],
                                               pA[:, t % 3, P * kt:P * (kt + 1)], ident[:])
                last.then_inc(na_t, 1)

            def na_values(t):
                b, h = t % 10 // 2, 2 * (t // 10) + t % 2
                pe.wait_ge(na_pt, t + 1)
                if t >= 2:
                    pe.wait_ge(na_out, t - 1)
                hs = slice(HD * h, HD * (h + 1))
                if b < NB:
                    v = [(nv[:, 0], nv[:, 1]), (nvs[:, 0], nvs[:, 1]), (nvs[:, 1], nvs[:, 2]), (nv[:, 2], nv[:, 3])][b]
                    v = [v[0][:, hs], v[1][:, hs], vpast[:, h, :]]
                else:
                    v = [nv[:, NB, hs]]
                for kt in range(len(v)):
                    last = mm(ps[0:HD, 4 + t % 2, 0:P], v[kt], pTA[:, t % 2, P * kt:P * (kt + 1)],
                              start=kt == 0, stop=kt == len(v) - 1)
                last.then_inc(na_pv, 1)

            for t in range(N_NA + 3):
                if t < N_NA:
                    na_scores(t)
                if 2 <= t < N_NA + 2:
                    na_turn(t - 2)
                if t >= 3:
                    na_values(t - 3)

            def project_out(layer):
                name = f"out{layer}"
                for j in range(8):
                    unit(UNIT_AT[name] + j, PIECE_AT[name] + j, KD, P, h2_hi, h2_lo,
                         ready=(lambda k: pe.wait_ge(o_lo_done, KD * layer + k + 1)) if j == 0 else None)

            def mlp(layer):
                g0, n0 = UNIT_AT[f"mlp{layer}"], PIECE_AT[f"mlp{layer}"]
                with pe.Fori(0, NCH) as c:
                    for j in range(2 * CH):
                        if j < CH:
                            ready = h_ready("in0m" if layer == 0 else "in1m") if j == 0 else None
                            unit(g0 + j, n0 + j, KD, P, hM_hi, hM_lo, at=c * (2 * CH), half_at=c * CH, ready=ready)
                        else:
                            ready = (lambda k: pe.wait_ge(h2_lo_done, layer * NCH * CH + k + 1 + c * CH)) \
                                if j == CH else None
                            unit(g0 + j, n0 + j, CH, P, h2_hi, h2_lo, at=c * (2 * CH), half_at=c * CH, ready=ready)

            pe.wait_ge(na_max, N_NA)
            pe.wait_ge(na_pt, N_NA)
            pe.wait_ge(na_out, N_NA)
            project_out(0)
            mean_square("y0a")
            mean_square("in0m")
            mlp(0)
            mean_square("y0m")
            mean_square("in1")

            g0, n0 = UNIT_AT["in_c"], PIECE_AT["in_c"]
            for j in range(6):
                unit(g0 + j, n0 + j, KD, P if j < 5 else 64, hM_hi, hM_lo, ready=h_ready("in1") if j == 0 else None)
            pe.wait_ge(mla_in, 16 * 3)
            for k in range(KKV):
                nc.tensor.transpose(ps[:, 6, P * k:P * (k + 1)], pastc[:, P * k:P * (k + 1)], ident[:])
            nc.tensor.transpose(ps[0:ROPE, 7, 0:P], pastc[:, 256:288], ident[:]).then_inc(pc_t, 1)
            mean_square("cq")
            mean_square("ckv")
            g0, n0 = UNIT_AT["uq"], PIECE_AT["uq"]
            for h in range(NH_MLA):
                ready = (lambda k: pe.wait_ge(cn_lo, k + 1)) if h == 0 else None
                unit(g0 + h, n0 + h // 2, KQ, P, cq_hi, cq_lo, ready=ready, base=P * (h % 2), wide=2 * P)
            pe.wait_ge(cn_lo, KQ + KKV)
            pe.wait_ge(pc_out, 1)
            for k in range(KKV):
                nc.tensor.transpose(ps[:, 6, P * k:P * (k + 1)], ckn[:, k, TL + NP:T + NP], ident[:])
            nc.tensor.transpose(ps[:, 7, 0:ROPE], cT[0:ROPE, 5, TL:T], ident[0:ROPE, 0:ROPE]).then_inc(tok_t, 1)
            pe.wait_ge(tok_out, 1)
            g0, n0 = UNIT_AT["uk"], PIECE_AT["uk"]
            pe.wait_ge(w_lo_done, n0 + 2)
            for m in range(8):
                g = g0 + m
                free_pair(g)
                for k in range(KKV):
                    wh, wl = [w[:, (n0 + k) % 2, P * m:P * (m + 1)] for w in (w_hi, w_lo)]
                    for s in range(2):
                        out = ps[:, 2 * (g % 2) + s, 0:384]
                        xh, xl = [x[:, k, 384 * s:384 * (s + 1)] for x in (ck_hi, ck_lo)]
                        mm(out, wl, xh, start=k == 0, stop=False)
                        mm(out, wh, xl, start=False, stop=False)
                        last = mm(out, wh, xh, start=False, stop=k == KKV - 1)
                last.then_inc(unit_done, 1)
            n0 = PIECE_AT["uv"]
            pe.wait_ge(w_lo_done, n0 + 2)
            for j in range(12):
                b, s = j // 2, j % 2
                if j >= 4:
                    pe.wait_ge(vm_out, j - 3)
                for k in range(KKV):
                    wh, wl = [w[:, (n0 + k) % 2, 512 * s:512 * (s + 1)] for w in (w_hi, w_lo)]
                    xh, xl = [x[:, k, P * b:P * (b + 1)] for x in (ck_hi, ck_lo)]
                    out = ps[:, 4 + j % 4, :]
                    mm(out, xh, wl, start=k == 0, stop=False)
                    mm(out, xl, wh, start=False, stop=False)
                    last = mm(out, xh, wh, start=False, stop=k == KKV - 1)
                last.then_inc(vm_done, 1)

            def mla_scores(t):
                h, b = t // 5, t % 5
                if t >= 2:
                    pe.wait_ge(m_e, t - 1)
                q = qm[:, h, P * b:P * (b + 1)]
                if b < NB:
                    for s in range(2):
                        last = mm(ps[:, 2 * (t % 2) + s, 0:HALF], q, km[:, h, HALF * s:HALF * (s + 1)],
                                  start=True, stop=True)
                else:
                    last = mm(ps[:, 2 * (t % 2), 0:TC], q, km[:, h, TL + NP:T + NP], start=True, stop=True)
                last.then_inc(m_s, 1)

            def mla_turn(t):
                pe.wait_ge(m_p, t + 1)
                if t:
                    pe.wait_ge(m_pt, t)
                for kt in range(5 if t % 5 < NB else 1):
                    last = nc.tensor.transpose(ps[:, 4 + kt // 4, P * (kt % 4):P * (kt % 4 + 1)],
                                               pM[:, t % 3, P * kt:P * (kt + 1)], ident[:])
                last.then_inc(m_t, 1)

            def mla_values(t):
                h, b = t // 5, t % 5
                pe.wait_ge(m_pt, t + 1)
                if t >= 2:
                    pe.wait_ge(m_out, t - 1)
                tiles = range(5) if b < NB else (5,)
                for j, kt in enumerate(tiles):
                    last = mm(ps[0:HD, 6 + t % 2, 0:P], vm[:, kt, HD * h:HD * (h + 1)],
                              pTM[:, t % 2, P * j:P * (j + 1)], start=j == 0, stop=j == len(tiles) - 1)
                last.then_inc(m_pv, 1)

            pe.wait_ge(act_evac, EVAC[UNIT_AT["uk"] + 7][0])
            pe.wait_ge(vm_out, 12)
            pe.wait_ge(kmas_done, NH_MLA)
            pe.wait_ge(ctx_rope, 1)
            for t in range(N_MLA + 3):
                if t < N_MLA:
                    mla_scores(t)
                if 2 <= t < N_MLA + 2:
                    mla_turn(t - 2)
                if t >= 3:
                    mla_values(t - 3)
            pe.wait_ge(m_e, N_MLA)
            project_out(1)
            mean_square("y1a")
            mean_square("in1m")
            mlp(1)
            mean_square("y1m")

            pe.wait_ge(dve_evac, EVAC[-1][1])
            pe.wait_ge(ms_out, len(NORMS))
            pe.wait_ge(x_done, 4 * KD)
            for j in range(10):
                b, g = j // 2, j % 2
                if j >= 8:
                    pe.wait_ge(y_out, j - 7)
                for n in range(4):
                    last = nc.tensor.transpose(ps[:, j % 8, P * n:P * (n + 1)],
                                               xT[:, 4 * g + n, P * b:P * (b + 1)], ident[:])
                last.then_inc(y_t, 1)

        @block.scalar
        def _(act):
            chain = Chain(act, "act_chain")
            f = nc.scalar.activation

            def squares(name, src, ready):
                at, no = NORM_AT[name], NORM_NO[name]
                for k in range(NORM_K[name]):
                    ready(k)
                    if at + k >= 2:
                        act.wait_ge(sq_used, at + k - 1)
                    f(sq[:, (at + k) % 2, :], src(k), ACT.Square).then_inc(sq_done, 1)
                act.wait_ge(ms_out, no + 1)
                f(rstd[:], rstd[:], ACT.Sqrt).then_inc(root_done, 1)

            def operand(name, out, beside=None):
                for k in range(KD):
                    act.wait_ge(h_full, KD * MOD_NO[name] + k + 1)
                    f(out[:, k, :], nt[:, k % 2, :], ACT.Copy).then_inc(h_hi_done, 1)
                    if beside:
                        beside(k)

            def mod_rows(n):
                act.wait_ge(ada_done, n + 1)
                if n >= 2:
                    act.wait_ge(mod_t, n - 1)
                modrow = modrow_a if n < ADA_SPLIT else modrow_b
                f(modrow[:, n % 2, :], ps[0:2, n % 2, 0:ADA_W], ACT.Copy).then_inc(modrow_done, 1)

            def residual_norms(yname, src, xcount, ready):
                squares(yname, lambda k: src[:, k, :], ready)
                if xcount is not None:
                    squares(xcount[0], lambda k: xT[:, k, :], lambda k: act.wait_ge(x_done, xcount[1] + k + 1))

            act.wait_ge(rows_out, 1)
            f(cexp[:], vecT[:, ROW_C:ROW_C + 16], ACT.Exp, scale=-1.0).then_inc(c_exp, 1)
            act.wait_ge(decay_in, 16 * 3)
            f(lg[:, 0, :], dec[:], ACT.Exp, scale=LN2).then_inc(decay_exp, 1)
            act.wait_ge(decay_arg, 1)
            f(lg[:, 2, :], lg[:, 1, :], ACT.Ln).then_inc(decay_exp, 1)
            act.wait_ge(decay_arg, 2)
            f(kdec[:], kdec[:], ACT.Exp).then_inc(decay_exp, 1)
            for n in range(5):
                mod_rows(n)
            squares("in0", lambda k: xT[:, k, :], lambda k: act.wait_ge(x_out, 10))
            for n in range(5, 8):
                mod_rows(n)
            operand("in0", hA_hi, lambda k: mod_rows(7 + k // 2) if k in (2, 4, 6) else None)
            for n in range(11, ADA_SPLIT):
                mod_rows(n)
            act_split(act, 0)
            act.wait_ge(filled, 6)
            for j in range(20):
                act_split(act, j + 1)
                act.wait_ge(unit_done, j + 1)
                kind, m, src = j // 4, j % 4, pair(j)
                if kind == 0:
                    last = f(two(oT[:, m, :]), src, ACT.Copy)
                elif kind == 1:
                    f(two(kz[0:64, 2 * m, :]), pair(j, slice(0, 64)), ACT.Copy, scale=HD ** -0.5)
                    last = f(two(kz[64:P, 2 * m + 1, :]), pair(j, slice(64, P)), ACT.Copy, scale=HD ** -0.5)
                elif kind == 2:
                    last = f(two(gate[:, m, :]), src, ACT.Copy)
                elif kind == 3:
                    last = f(two(oT[:, 4 + m, :]), src, ACT.Copy, scale=HD ** -0.5)
                else:
                    f(two(kzn[0:64, 2 * m, 0:T]), pair(j, slice(0, 64)), ACT.Copy)
                    last = f(two(kzn[64:P, 2 * m + 1, 0:T]), pair(j, slice(64, P)), ACT.Copy)
                last.then_inc(act_evac, 1)
            for n in range(21, 29):
                act_split(act, n)

            act.wait_ge(ret_in, 16 * 3)
            act.wait_ge(v_out, 10)

            def ret_copy(h):
                act.wait_ge(ret_done, h + 1)
                rows = slice(64 * (h % 2), 64 * (h % 2) + 64)
                f(oT[rows, h // 2, 0:TL], ps[0:64, 4 + h % 2, :], ACT.Copy)
                f(oT[rows, h // 2, TL:T], ps[0:64, 7, 0:P], ACT.Copy).then_inc(ret_out, 1)

            for h in range(NH):
                rows = slice(64 * (h % 2), 64 * (h % 2) + 64)
                if h >= 2:
                    act.wait_ge(qe_done, h - 1)
                for s in range(2):
                    last = f(edec[rows, s, :], tpos[rows, s, :], ACT.Exp, scale=lg[rows, 7, 8 * s + h:8 * s + h + 1])
                last.then_inc(e_exp, 1)
                act.wait_ge(d_arg, h + 1)
                f(dmat[:, h % 2, :], dmat[:, h % 2, :], ACT.Exp).then_inc(d_exp, 1)
                if h:
                    ret_copy(h - 1)
            ret_copy(NH - 1)
            for h in range(NH):
                act.wait_ge(fin_done, h + 1)
                f(fin[:, h, :], ps[:, 2 + h % 2, 0:HD], ACT.Copy).then_inc(fin_out, 1)
            act.wait_ge(kd_done, NH)
            for n in range(ADA_SPLIT, ADA_SPLIT + ADA_RING):
                load_ada(nc.scalar, n)
            for n in range(ADA_SPLIT, N_ADA):
                m = n - ADA_SPLIT
                if m < 4:
                    if m >= 2:
                        act.wait_ge(g_done, m - 1)
                    f(nt[:, m % 2, :], gate[:, m, :], ACT.Exp, scale=-1.0).then_inc(g_exp, 1)
                mod_rows(n)
                if n + ADA_RING < N_ADA:
                    load_ada(nc.scalar, n + ADA_RING)
                s = gn_step(n)
                if s is None:
                    continue
                if s % 2 == 0:
                    act.wait_ge(gn_cen, s // 2 + 1)
                    f(sq[:, 0, :], nt[:, 0, :], ACT.Square).then_inc(gn_sq, 1)
                else:
                    act.wait_ge(gn_var, s // 2 + 1)
                    f(rstd[:], rstd[:], ACT.Sqrt).then_inc(gn_root, 1)

            for m in range(4):
                act.wait_ge(past_t, m + 1)
                f(kzn[0:64, 2 * m, T:T + NP], ps[0:64, m, 0:P], ACT.Copy)
                f(kzn[64:P, 2 * m + 1, T:T + NP], ps[64:P, m, 0:P], ACT.Copy).then_inc(past_out, 1)
            for h in range(NH):
                act.wait_ge(nk_t, h + 1)
                c = HD * (h % 2)
                f(nkt[:, h, :], ps[:, 4 + h % 4, c:c + HD], ACT.Copy).then_inc(nk_out, 1)

            def na_exp(t):
                w = 384 if t % 10 < 8 else TC
                act.wait_ge(na_max, t + 1)
                if t >= 3:
                    act.wait_ge(na_t, t - 2)
                e = t % 3
                f(pA[:, e, 0:w], s32[:, t % 2, 0:w], ACT.Exp, bias=smA[:, 1, e:e + 1],
                  accum_out=smA[:, 2, e:e + 1]).then_inc(na_e, 1)

            def na_copy(t):
                w = 384 if t % 10 < 8 else TC
                act.wait_ge(na_t, t + 1)
                if t >= 2:
                    act.wait_ge(na_pv, t - 1)
                f(pTA[:, t % 2, 0:w], ps[:, 2 + t % 2, 0:w], ACT.Copy).then_inc(na_pt, 1)

            for t in range(N_NA + 2):
                if t < N_NA:
                    na_exp(t)
                if t >= 2:
                    na_copy(t - 2)

            def mlp(layer):
                g0, n0 = UNIT_AT[f"mlp{layer}"], PIECE_AT[f"mlp{layer}"]
                base = layer * NCH * CH

                def chunk(c):
                    at, half = c * (2 * CH), c * CH
                    for j in range(2 * CH):
                        act_split(act, n0 + j + 1, at)
                        if j < CH:
                            act.wait_ge(unit_done, g0 + j + 1 + at)
                            if not isinstance(c, int) or base + j - 1 + half > 0:
                                act.wait_ge(h2_lo_done, base + j - 1 + half)
                            f(two(r32[:, j % 2, :]), pair(g0 + j), ACT.Relu).then_inc(act_evac, 1)
                            act.wait_ge(act_evac, EVAC[g0][0] + j + half)
                            f(h2_hi[:, j, :], r32[:, j % 2, :], ACT.Square).then_inc(h2_hi_done, 1)

                chunk(0)
                with act.Fori(1, NCH - 1) as c:
                    chunk(c)
                chunk(NCH - 1)

            act.wait_ge(na_out, N_NA)
            for k in range(KD):
                f(h2_hi[:, k, :], oT[:, k, :], ACT.Copy).then_inc(o_hi_done, 1)
            for j in range(8):
                act_split(act, PIECE_AT["out0"] + j + 1)
            e0 = EVAC[UNIT_AT["out0"]][1]
            residual_norms("y0a", yT, ("in0m", 0), lambda k: act.wait_ge(dve_evac, e0 + k))
            operand("in0m", hM_hi)
            mlp(0)
            e1 = EVAC[UNIT_AT["in_c"] - 1][1]
            residual_norms("y0m", yT, ("in1", KD), lambda k: act.wait_ge(dve_evac, e1))
            operand("in1", hM_hi)

            for j in range(6):
                g, n = UNIT_AT["in_c"] + j, PIECE_AT["in_c"] + j
                act_split(act, n + 1)
                act.wait_ge(unit_done, g + 1)
                m = P if j < 5 else 64
                f(two(cT[0:m, j, :]), pair(g, slice(0, m)), ACT.Copy).then_inc(act_evac, 1)
            e2 = EVAC[UNIT_AT["in_c"]][0]
            act.wait_ge(pc_t, 1)
            for k in range(KKV):
                f(ckn[:, k, TL:TL + NP], ps[:, 6, P * k:P * (k + 1)], ACT.Copy)
            act.wait_ge(km_zero, 1)
            f(kmas[96:P, TL:TL + NP], ps[0:ROPE, 7, 0:P], ACT.Copy).then_inc(pc_out, 1)
            squares("cq", lambda k: cT[:, k, :], lambda k: act.wait_ge(act_evac, e2 + k))
            for k in range(KQ):
                act.wait_ge(cn_full, k + 1)
                f(cq_hi[:, k, :], nt[:, k % 2, :], ACT.Copy).then_inc(cn_hi, 1)
            squares("ckv", lambda k: cT[:, KQ + k, :], lambda k: act.wait_ge(act_evac, e2 + KQ + k))
            act.wait_ge(pc_out, 1)
            for k in range(KKV):
                act.wait_ge(cn_full, KQ + k + 1)
                f(ck_hi[:, k, :], ckn[:, k, :], ACT.Copy).then_inc(cn_hi, 1)
            f(kmas[96:P, TL + NP:T + NP], cT[0:ROPE, 5, TL:T], ACT.Copy).then_inc(km_rope, 1)
            for h in range(NH_MLA):
                g = UNIT_AT["uq"] + h
                if h % 2 == 0:
                    act_split(act, PIECE_AT["uq"] + h // 2 + 1)
                act.wait_ge(unit_done, g + 1)
                if h == 0:
                    act.wait_ge(cn_lo, KQ)
                f(two(qm[0:64, h, :]), pair(g, slice(0, 64)), ACT.Copy, scale=MLA_SCALE)
                f(two(qm[96:P, h, :]), pair(g, slice(64, 96)), ACT.Copy, scale=MLA_SCALE).then_inc(act_evac, 1)
            act.wait_ge(tok_t, 1)
            f(tokc[:, 0:256], ps[:, 6, 0:256], ACT.Copy)
            f(tokc[:, 256:288], ps[:, 7, 0:ROPE], ACT.Copy).then_inc(tok_out, 1)
            act_split(act, PIECE_AT["uk"] + 1)
            act.wait_ge(tok_out, 1)
            act.wait_ge(stored, 16 * 6)
            act.wait_ge(qrope_done, NH_MLA)
            act.wait_ge(km_rope, 2)
            for m in range(8):
                g = UNIT_AT["uk"] + m
                act.wait_ge(unit_done, g + 1)
                for s in range(2):
                    src = ps[64 * s:64 * s + 64, 2 * (g % 2):2 * (g % 2) + 2, 0:384]
                    last = f(km[0:64, 2 * m + s, :].rearrange("p (n c) -> p n c", n=2), src, ACT.Copy)
                last.then_inc(act_evac, 1)
            act_split(act, PIECE_AT["uv"])
            act_split(act, PIECE_AT["uv"] + 1)
            act.wait_ge(vm_done, 12)

            def mla_exp(t):
                act.wait_ge(m_max, t + 1)
                if t >= 3:
                    act.wait_ge(m_t, t - 2)
                b2, e = 2 * (t % 2), t % 3
                if t % 5 < NB:
                    src, dst = ps[:, b2:b2 + 2, 0:HALF], two(pM[:, e, :])
                else:
                    src, dst = ps[:, b2, 0:TC], pM[:, e, 0:TC]
                f(dst, src, ACT.Exp, bias=smM[:, 0, e:e + 1], accum_out=smM[:, 1, e:e + 1])\
                    .then_inc(m_e, 1)

            def mla_copy(t):
                act.wait_ge(m_t, t + 1)
                if t >= 2:
                    act.wait_ge(m_pv, t - 1)
                w = T if t % 5 < NB else TC
                src = ps[:, 4:6, :].rearrange("p n c -> p (n c)")
                f(pTM[:, t % 2, 0:w], src[:, 0:w], ACT.Copy).then_inc(m_pt, 1)

            for t in range(N_MLA + 2):
                if t < N_MLA:
                    mla_exp(t)
                if t >= 2:
                    mla_copy(t - 2)
            act_split(act, PIECE_AT["out1"])
            act.wait_ge(m_out, N_MLA)
            act.wait_ge(m_pv, N_MLA)
            for k in range(KD):
                for s in range(2):
                    rows = slice(64 * s, 64 * s + 64)
                    last = f(h2_hi[rows, k, :], qm[rows, 2 * k + s, :], ACT.Copy)
                last.then_inc(o_hi_done, 1)
            for j in range(8):
                act_split(act, PIECE_AT["out1"] + j + 1)
            e3 = EVAC[UNIT_AT["out1"]][1]
            residual_norms("y1a", yT, ("in1m", 2 * KD), lambda k: act.wait_ge(dve_evac, e3 + k))
            operand("in1m", hM_hi)
            mlp(1)
            residual_norms("y1m", yT, None, lambda k: act.wait_ge(dve_evac, EVAC[-1][1]))
            for j in range(10):
                b, g = j // 2, j % 2
                act.wait_ge(y_t, j + 1)
                f(ytok[:, b, 512 * g:512 * (g + 1)], ps[:, j % 8, :], ACT.Copy).then_inc(y_out, 1)

        @block.vector
        def _(dve):
            chain = Chain(dve, "dve_chain")
            link = chain.link
            tt, ts, stt = nc.vector.tensor_tensor, nc.vector.tensor_scalar, nc.vector.scalar_tensor_tensor

            def root(name, features):
                at, no = NORM_AT[name], NORM_NO[name]
                dve.wait_ge(sq_used, at + NORM_K[name])
                ts(two(rstd[:]), ps[:, 4:6, 0:HALF], 1.0 / features, EPS, ALU.mult, ALU.add).then_inc(ms_out, 1)
                dve.wait_ge(root_done, no + 1)
                link(nc.vector.reciprocal(rstd[:], rstd[:]))

            def add_residual(name, layer, which):
                root(name, D)
                first = KD * (2 * layer + (which == G2))
                for k in range(KD):
                    if k >= 2:
                        dve.wait_ge(x_done, first + k - 1)
                    link(tt(nt[:, k % 2, :], yT[:, k, :], rstd[:], ALU.mult))
                    for g, (a, b) in enumerate(SPAN):
                        last = stt(xT[:, k, a:b], nt[:, k % 2, a:b], coef[:, layer, which, k, g:g + 1],
                                   xT[:, k, a:b], ALU.mult, ALU.add)
                    last.then_inc(x_done, 1)

            def modulate(name, layer, which, shift, beside=None):
                if not beside:
                    root(name, D)
                for k in range(KD):
                    if k >= 2:
                        dve.wait_ge(h_lo_done, KD * MOD_NO[name] + k - 1)
                    link(tt(nt[:, k % 2, :], xT[:, k, :], rstd[:], ALU.mult))
                    for g, (a, b) in enumerate(SPAN):
                        last = ts(nt[:, k % 2, a:b], nt[:, k % 2, a:b], coef[:, layer, which, k, g:g + 1],
                                  mod[:, layer, 8 * shift + k, g:g + 1], ALU.mult, ALU.add)
                    last.then_inc(h_full, 1)
                    if beside:
                        beside(k)

            def mod_columns(n):
                layer, c = divmod(n, N_ADA // 2)
                dve.wait_ge(mod_t, n + 1)
                cols = ps[:, 2, 0:4].rearrange("p (j g) -> p j g", g=2)
                for g in range(2):
                    last = tt(mod[:, layer, 2 * c:2 * c + 2, g], cols[:, :, g], badaT[:, layer, 2 * c:2 * c + 2],
                              ALU.add)
                last.then_inc(mod_out, 1)
                which = {SCALE1: A1, GATE1: G1, SCALE2: A2, GATE2: G2}.get(c // 4)
                if c % 4 == 3 and which is not None:
                    dve.wait_ge(mod_out, n + 1)
                    part = c // 4
                    for g in range(2):
                        gain = vecT[:, ROW_GAIN + 32 * layer + 8 * which:ROW_GAIN + 32 * layer + 8 * which + 8]
                        m = mod[:, layer, 8 * part:8 * part + 8, g]
                        last = stt(coef[:, layer, which, :, g], m, 1.0 if which in (A1, A2) else 0.0, gain,
                                   ALU.add, ALU.mult)
                    link(last)

            dve.wait_ge(rows_t, 1)
            nc.vector.tensor_copy(vecT[:], ps[:, 3, 0:VROWS]).then_inc(rows_out, 1)
            dve.wait_ge(rows_t, 2)
            nc.vector.tensor_copy(badaT[:].rearrange("p l f -> p (l f)"), ps[:, 4, 0:96]).then_inc(rows_out, 1)
            dve.wait_ge(c_exp, 1)
            link(ts(cexp[:], cexp[:], 1.0, None, ALU.add))
            link(nc.vector.reciprocal(cexp[:], cexp[:]))
            for g in range(2):
                last = tt(csil[:, :, g], vecT[:, ROW_C + 8 * g:ROW_C + 8 * g + 8], cexp[:, 8 * g:8 * g + 8], ALU.mult)
            last.then_inc(c_ready, 1)
            dve.wait_ge(decay_exp, 1)
            y, w, ln, z, z2, s, big, out = [lg[:, n, :] for n in range(8)]
            link(ts(w, y, -1.0, 1.0, ALU.mult, ALU.add))
            ts(w, w, 1e-30, None, ALU.max).then_inc(decay_arg, 1)
            ts(big, y, 0.5, None, ALU.is_gt)
            link(ts(y, y, 0.5, None, ALU.min))
            link(ts(z, y, -1.0, 2.0, ALU.mult, ALU.add))
            link(nc.vector.reciprocal(z, z))
            link(tt(z, z, y, ALU.mult))
            link(tt(z2, z, z, ALU.mult))
            link(ts(s, z2, 1.0 / 21, 1.0 / 19, ALU.mult, ALU.add))
            for d in range(17, 0, -2):
                link(tt(s, s, z2, ALU.mult))
                link(ts(s, s, 1.0 / d, None, ALU.add))
            link(tt(s, s, z, ALU.mult))
            link(ts(s, s, -2.0, None, ALU.mult))
            dve.wait_ge(decay_exp, 2)
            link(tt(ln, ln, s, ALU.subtract))
            link(tt(ln, ln, big, ALU.mult))
            link(tt(out, ln, s, ALU.add))
            for s_ in range(2):
                last = ts(kdec[:, s_, :], out[:, 8 * s_:8 * s_ + 8], kpos[:, s_:s_ + 1], None, ALU.mult)
            last.then_inc(decay_arg, 1)
            back = lg[:, 0, 0:8]
            link(ts(back, out[:, 8:16], -1.0, None, ALU.mult))

            mod_columns(0)
            mod_columns(1)
            for j in range(10):
                b, g = j // 2, j % 2
                dve.wait_ge(x_t, j + 1)
                nc.vector.tensor_copy(xT[:, 4 * g:4 * g + 4, P * b:P * (b + 1)],
                                      ps[:, 3 + j % 5, :].rearrange("p (k t) -> p k t", k=4)).then_inc(x_out, 1)
            mod_columns(2)
            mod_columns(3)

            root("in0", D)
            for n in range(4, 8):
                mod_columns(n)
            modulate("in0", 0, A1, SHIFT1, lambda k: mod_columns(7 + k // 2) if k in (2, 4, 6) else None)
            for n in range(11, ADA_SPLIT):
                mod_columns(n)
            dve_split(dve, 0)
            for n in range(1, 24):
                dve_split(dve, n)
            dve_split(dve, 24)
            for part in range(2):
                if part:
                    for n in range(25, 29):
                        dve_split(dve, n)
                dve.wait_ge(v_done, 4 * part + 4)
                for b in range(5):
                    nc.vector.tensor_copy((nv if part else rv)[:, b, :], ps[:, (4, 5, 6, 7, 0)[b], :])\
                        .then_inc(v_out, 1)

            def decay_args(h):
                link(ts(dmat[:, h % 2, :], dist[:], back[:, h:h + 1], None, ALU.mult))
                stt(dmat[:, h % 2, :], dist[:], out[:, h:h + 1], dmat[:, h % 2, :], ALU.mult, ALU.min)\
                    .then_inc(d_arg, 1)

            dve.wait_ge(dist_in, 16)
            decay_args(0)
            for h in range(NH):
                rows = slice(64 * (h % 2), 64 * (h % 2) + 64)
                dve.wait_ge(e_exp, h + 1)
                if h >= 2:
                    dve.wait_ge(ret_done, h - 1)
                for s_ in range(2):
                    last = tt(qE[64 * s_:64 * s_ + 64, h % 2, :], oT[rows, h // 2, 0:TL], edec[rows, s_, :], ALU.mult)
                last.then_inc(qe_done, 1)
                dve.wait_ge(d_exp, h + 1)
                for c in (384, 896):
                    last = tt(dmat[:, h % 2, c:c + P], dmat[:, h % 2, c:c + P], ident[:], ALU.add)
                link(last)
                if h < NH - 1:
                    decay_args(h + 1)
                if h:
                    dve.wait_ge(ret_done, h)
                for kt in range(5):
                    dve.wait_ge(rs_done, 5 * h + kt + 1)
                    if kt < NB:
                        c = ROWS * (48 - BLK * kt)
                        tt(sd[:, kt, :], ps[:, kt, :], dmat[:, h % 2, c:c + TL], ALU.mult).then_inc(sd_done, 1)
                    else:
                        tt(sd[:, 4, 0:P], ps[:, 6, 0:P], dmat[:, h % 2, 896:1024], ALU.mult).then_inc(sd_done, 1)
            dve.wait_ge(decay_exp, 3)
            for h in range(NH):
                dve.wait_ge(kd_t, h + 1)
                if h >= 2:
                    dve.wait_ge(fin_done, h - 1)
                c = HD * (h % 2)
                for s_ in range(2):
                    last = ts(kd[:, h % 2, HD * s_:HD * (s_ + 1)], ps[:, h % 2, c:c + HD], kdec[:, s_, h:h + 1], None,
                              ALU.mult)
                last.then_inc(kd_done, 1)
            for n in range(ADA_SPLIT, N_ADA):
                m = n - ADA_SPLIT
                if m < 4:
                    dve.wait_ge(g_exp, m + 1)
                    link(ts(nt[:, m % 2, :], nt[:, m % 2, :], 1.0, None, ALU.add))
                    link(nc.vector.reciprocal(nt[:, m % 2, :], nt[:, m % 2, :]))
                    tt(gate[:, m, :], gate[:, m, :], nt[:, m % 2, :], ALU.mult).then_inc(g_done, 1)
                if n > ADA_SPLIT:
                    mod_columns(n - 1)
                s = gn_step(n)
                if s is None:
                    continue
                m = s // 2
                if s % 2 == 0:
                    if m:
                        dve.wait_ge(gn_done, m)
                    else:
                        dve.wait_ge(g_done, 4)
                    dve.wait_ge(gn_mm, 2 * m + 1)
                    tt(two(nt[:, 0, :]), two(oT[:, m, :]), ps[:, 4:6, 0:HALF], ALU.subtract).then_inc(gn_cen, 1)
                else:
                    dve.wait_ge(gn_mm, 2 * m + 2)
                    ts(two(rstd[:]), ps[:, 6:8, 0:HALF], EPS, None, ALU.add).then_inc(gn_var, 1)
                    dve.wait_ge(gn_root, m + 1)
                    link(nc.vector.reciprocal(rstd[:], rstd[:]))
                    link(tt(nt[:, 0, :], nt[:, 0, :], rstd[:], ALU.mult))
                    tt(oT[:, m, :], nt[:, 0, :], gate[:, m, :], ALU.mult).then_inc(gn_done, 1)
            mod_columns(N_ADA - 1)

            dve.wait_ge(na_in, 16 * 3)
            for j in range(3):
                nc.vector.tensor_copy(nvs[0:64, j, :], nv[64:P, j, :])
                last = nc.vector.tensor_copy(nvs[64:P, j, :], nv[0:64, j + 1, :])
            last.then_inc(nvs_done, 1)

            def na_rowmax(t):
                w = 384 if t % 10 < 8 else TC
                n = 8 * (t // 10) + t % 10
                dve.wait_ge(na_s, t + 1)
                if t % 10 < 8:
                    dve.wait_ge(bm_done, n + 1)
                    add = bm[:, n % 2, :]
                else:
                    add = bm[:, 0, NKEY:NKEY + NP]
                if t >= 2:
                    dve.wait_ge(na_e, t - 1)
                e, f = t % 3, t % 2
                link(nc.vector.tensor_tensor_reduce(s32[:, f, 0:w], ps[:, f, 0:w], add, 1.0, LOWEST, ALU.add, ALU.max,
                                                    smA[:, 0, e:e + 1]))
                ts(smA[:, 1, e:e + 1], smA[:, 0, e:e + 1], -1.0, None, ALU.mult).then_inc(na_max, 1)

            def na_norm(t):
                w = 384 if t % 10 < 8 else TC
                e = t % 3
                dve.wait_ge(na_e, t + 1)
                link(nc.vector.reciprocal(smA[:, 3, e:e + 1], smA[:, 2, e:e + 1]))
                ts(pA[:, e, 0:w], pA[:, e, 0:w], smA[:, 3, e:e + 1], None, ALU.mult).then_inc(na_p, 1)

            def na_store(t):
                m, b = t // 10, t % 10 // 2
                rows = slice(64 * (t % 2), 64 * (t % 2) + 64)
                dve.wait_ge(na_pv, t + 1)
                nc.vector.tensor_copy(oT[rows, 4 + m, P * b:P * (b + 1)], ps[0:64, 4 + t % 2, 0:P])\
                    .then_inc(na_out, 1)

            for t in range(N_NA + 4):
                if t < N_NA:
                    na_rowmax(t)
                if 1 <= t <= N_NA:
                    na_norm(t - 1)
                if t >= 4:
                    na_store(t - 4)

            def project_out(layer):
                for j in range(8):
                    dve_split(dve, PIECE_AT[f"out{layer}"] + j + 1)
                    g = UNIT_AT[f"out{layer}"] + j
                    dve.wait_ge(unit_done, g + 1)
                    nc.vector.tensor_copy(two(yT[:, j, :]), pair(g)).then_inc(dve_evac, 1)

            def mlp(layer):
                g0, n0 = UNIT_AT[f"mlp{layer}"], PIECE_AT[f"mlp{layer}"]
                base = layer * NCH * CH
                dve.wait_ge(y_zero, layer + 1)

                def chunk(c):
                    at, half = c * (2 * CH), c * CH
                    for j in range(2 * CH):
                        dve_split(dve, n0 + j + 1, at)
                        if j < CH:
                            dve.wait_ge(act_evac, EVAC[g0][0] + j + half)
                            tt(s2[:, j % 2, :], r32[:, j % 2, :], r32[:, j % 2, :], ALU.mult)\
                                .then_inc(chain.sem, 1)
                            dve.wait_ge(chain.sem, chain.n + j + 1 + half)
                            dve.wait_ge(h2_hi_done, base + j + 1 + half)
                            tt(h2_lo[:, j, :], s2[:, j % 2, :], h2_hi[:, j, :].bitcast(F32), ALU.subtract)\
                                .then_inc(h2_lo_done, 1)
                        else:
                            dve.wait_ge(unit_done, g0 + j + 1 + at)
                            y = two(yT[:, j - CH, :])
                            tt(y, y, pair(g0 + j), ALU.add).then_inc(dve_evac, 1)

                with dve.Fori(0, NCH - 1) as c:
                    chunk(c)
                chunk(NCH - 1)
                chain.n += NCH * CH

            project_out(0)
            add_residual("y0a", 0, G1)
            modulate("in0m", 0, A2, SHIFT2)
            mlp(0)
            add_residual("y0m", 0, G2)
            modulate("in1", 1, A1, SHIFT1)

            for j in range(6):
                dve_split(dve, PIECE_AT["in_c"] + j + 1)
            root("cq", KQ * P)
            for k in range(KQ):
                if k >= 2:
                    dve.wait_ge(cn_lo, k - 1)
                link(tt(nt[:, k % 2, :], cT[:, k, :], rstd[:], ALU.mult))
                ts(nt[:, k % 2, :], nt[:, k % 2, :], vecT[:, ROW_QN + k:ROW_QN + k + 1], None, ALU.mult)\
                    .then_inc(cn_full, 1)
            root("ckv", KKV * P)
            dve.wait_ge(cn_lo, KQ)
            dve.wait_ge(pc_out, 1)
            for k in range(KKV):
                link(tt(nt[:, k, :], cT[:, KQ + k, :], rstd[:], ALU.mult))
                gain = vecT[:, ROW_KVN + k:ROW_KVN + k + 1]
                ts(ckn[:, k, 0:TL], nt[:, k, 0:TL], gain, None, ALU.mult)
                ts(ckn[:, k, TL + NP:T + NP], nt[:, k, TL:T], gain, None, ALU.mult).then_inc(cn_full, 1)
            dve.wait_ge(act_evac, EVAC[UNIT_AT["in_c"] + 5][0])
            tt(rt[0:ROPE, 0, :], cT[0:ROPE, 5, 0:TL], rope[0:ROPE, :], ALU.mult)
            link(tt(rt[0:ROPE, 1, :], cT[ROPE:64, 5, 0:TL], rope[ROPE:64, :], ALU.mult))
            tt(kmas[64:96, 0:TL], rt[0:ROPE, 0, :], rt[0:ROPE, 1, :], ALU.add).then_inc(km_rope, 1)
            for h in range(NH_MLA):
                g = UNIT_AT["uq"] + h
                if h % 2 == 0:
                    dve_split(dve, PIECE_AT["uq"] + h // 2 + 1)
                dve.wait_ge(act_evac, EVAC[g][0])
                if h:
                    dve.wait_ge(qrope_done, h)
                for s_, (a, b) in enumerate(((0, HALF), (HALF, TL))):
                    bank = 2 * (g % 2) + s_
                    tt(rt[64:96, 0, a:b], ps[64:96, bank, 0:b - a], rope[64:96, a:b], ALU.mult)
                    last = tt(rt[64:96, 1, a:b], ps[96:P, bank, 0:b - a], rope[96:P, a:b], ALU.mult)
                last.then_inc(dve_evac, 1)
                dve.wait_ge(dve_evac, EVAC[g][1])
                tt(qm[64:96, h, 0:TL], rt[64:96, 0, :], rt[64:96, 1, :], ALU.add).then_inc(qrope_done, 1)
            dve_split(dve, PIECE_AT["uk"] + 1)
            dve_split(dve, PIECE_AT["uv"])
            dve_split(dve, PIECE_AT["uv"] + 1)
            for j in range(12):
                dve.wait_ge(vm_done, j + 1)
                if j == 0:
                    dve.wait_ge(unit_done, UNIT_AT["uq"] + NH_MLA)
                nc.vector.tensor_copy(vm[:, j // 2, 512 * (j % 2):512 * (j % 2 + 1)], ps[:, 4 + j % 4, :])\
                    .then_inc(vm_out, 1)

            def mla_rowmax(t):
                e, b2 = t % 3, 2 * (t % 2)
                dve.wait_ge(m_s, t + 1)
                if t >= 2:
                    dve.wait_ge(m_e, t - 1)
                src = ps[:, b2:b2 + 2, 0:HALF] if t % 5 < NB else ps[:, b2, 0:TC]
                nc.vector.tensor_reduce(smM[:, 0, e:e + 1], src, AX.XY if t % 5 < NB else AX.X, ALU.max,
                                        negate=True).then_inc(m_max, 1)

            def mla_norm(t):
                w, e = (T if t % 5 < NB else TC), t % 3
                dve.wait_ge(m_e, t + 1)
                link(nc.vector.reciprocal(smM[:, 2, e:e + 1], smM[:, 1, e:e + 1]))
                ts(pM[:, e, 0:w], pM[:, e, 0:w], smM[:, 2, e:e + 1], None, ALU.mult).then_inc(m_p, 1)

            def mla_store(t):
                h, b = t // 5, t % 5
                dve.wait_ge(m_pv, t + 1)
                rows = slice(64 * (h % 2), 64 * (h % 2) + 64)
                nc.vector.tensor_copy(qm[rows, h, P * b:P * (b + 1)], ps[0:64, 6 + t % 2, 0:P]).then_inc(m_out, 1)

            for t in range(N_MLA + 4):
                if t < N_MLA:
                    mla_rowmax(t)
                if 1 <= t <= N_MLA:
                    mla_norm(t - 1)
                if t >= 4:
                    mla_store(t - 4)
            dve_split(dve, PIECE_AT["out1"])
            project_out(1)
            add_residual("y1a", 1, G1)
            modulate("in1m", 1, A2, SHIFT2)
            mlp(1)
            add_residual("y1m", 1, G2)

        @block.gpsimd
        def _(pool):
            sub = nc.gpsimd.tensor_tensor
            nc.gpsimd.memset(ones[:], 1.0).then_inc(filled, 1)
            nc.gpsimd.memset(gnb[:], 0.0).then_inc(filled, 1)
            pool.wait_ge(filled, 2)
            nc.gpsimd.memset(gnb[0:64, 0:64], 1.0 / HD).then_inc(filled, 1)
            nc.gpsimd.memset(gnb[64:P, 64:P], 1.0 / HD).then_inc(filled, 1)
            pool.wait_ge(filled, 4)
            pool.wait_ge(x_out, 10)
            pool.wait_ge(rows_out, 2)
            nc.gpsimd.memset(kz[:], 0.0).then_inc(filled, 1)
            pool.wait_ge(filled, 5)
            nc.gpsimd.memset(kzn[:], 0.0).then_inc(filled, 1)

            def low_parts(name, hi, lo):
                for k in range(KD):
                    pool.wait_ge(h_hi_done, KD * MOD_NO[name] + k + 1)
                    sub(lo[:, k, :], nt[:, k % 2, :], hi[:, k, :].bitcast(F32), ALU.subtract).then_inc(h_lo_done, 1)

            low_parts("in0", hA_hi, hA_lo)
            pool.wait_ge(stored, 32)
            pool.wait_ge(ret_out, NH)
            pool.wait_ge(fin_out, NH)
            nc.gpsimd.memset(bm[:], 0.0)
            nc.gpsimd.memset(bias[:], 0.0).then_inc(bias_zero, 1)
            pool.wait_ge(na_in, 16 * 3)
            pool.wait_ge(na_bias_in, 16 * BLK * ROWS)
            for n in range(8 * 4):
                m, b, h = n // 8, n % 8 // 2, 2 * (n // 8) + n % 2
                if n >= 2:
                    pool.wait_ge(na_max, 10 * ((n - 2) // 8) + (n - 2) % 8 + 1)
                u = (16, 8, 8, 0)[b]
                sub(bm[:, n % 2, 0:NKEY].rearrange("p (c r) -> p c r", r=ROWS),
                    bias[:, h, :, u:u + KW].rearrange("p r c -> p c r"),
                    mask[:, b, :].rearrange("p (c r) -> p c r", r=ROWS), ALU.add).then_inc(bm_done, 1)

            def output_low(layer, src):
                for k in range(KD):
                    pool.wait_ge(o_hi_done, KD * layer + k + 1)
                    src(k).then_inc(o_lo_done, 1)

            output_low(0, lambda k: sub(h2_lo[:, k, :], oT[:, k, :], h2_hi[:, k, :].bitcast(F32), ALU.subtract))
            pool.wait_ge(ms_out, NORM_NO["y0a"] + 1)
            pool.wait_ge(x_done, KD)
            nc.gpsimd.memset(yT[:], 0.0).then_inc(y_zero, 1)
            low_parts("in0m", hM_hi, hM_lo)
            low_parts("in1", hM_hi, hM_lo)
            pool.wait_ge(h_lo_done, 3 * KD)
            nc.gpsimd.memset(kmas[64:P, :], 0.0).then_inc(km_zero, 1)
            pool.wait_ge(km_zero, 1)
            for k in range(KQ):
                pool.wait_ge(cn_hi, k + 1)
                sub(cq_lo[:, k, :], nt[:, k % 2, :], cq_hi[:, k, :].bitcast(F32), ALU.subtract).then_inc(cn_lo, 1)
            for k in range(KKV):
                pool.wait_ge(cn_hi, KQ + k + 1)
                sub(ck_lo[:, k, :], ckn[:, k, :], ck_hi[:, k, :].bitcast(F32), ALU.subtract).then_inc(cn_lo, 1)
            pool.wait_ge(cn_lo, KQ + KKV)
            nc.gpsimd.memset(qm[64:96, :, TL:T], 0.0).then_inc(ctx_rope, 1)
            pool.wait_ge(ctx_rope, 1)
            pool.wait_ge(km_rope, 2)
            pool.wait_ge(pc_out, 1)
            pool.wait_ge(tok_out, 1)
            pool.wait_ge(stored, 16 * 6)
            pool.wait_ge(qrope_done, NH_MLA)
            for h in range(NH_MLA):
                nc.gpsimd.tensor_copy(km[64:P, h, :], kmas[64:P, :]).then_inc(kmas_done, 1)

            pool.wait_ge(kmas_done, NH_MLA)
            chain = Chain(pool, "pool_chain")

            def heads_low(k):
                for s in range(2):
                    rows = slice(64 * s, 64 * s + 64)
                    if s:
                        chain.link(last)
                    elif k:
                        pool.wait_ge(o_lo_done, KD + k)
                    last = sub(h2_lo[rows, k, :], qm[rows, 2 * k + s, :], h2_hi[rows, k, :].bitcast(F32), ALU.subtract)
                return last

            output_low(1, heads_low)
            pool.wait_ge(x_done, 3 * KD)
            nc.gpsimd.memset(yT[:], 0.0).then_inc(y_zero, 1)
            low_parts("in1m", hM_hi, hM_lo)


_INS = ["x_prompt", "x_sample", "state_ret_fwd", "state_ret_bwd", "cache_na_k", "cache_na_v", "cache_mla_ckv",
        "cache_mla_kpe", "c", "c_ctx", "w_ada", "b_ada", "norm_gains", "w_mlp_in", "w_mlp_out", "w_in_ac",
        "w_out_ac", "ret_decay_fwd", "ret_decay_bwd", "na_rpb", "mla_q_norm", "mla_kv_norm", "w_uk", "w_uv",
        "w_out_c"]
_OUTS = [("y_prompt", (1, 128, 1024)), ("y_sample", (1, 512, 1024)), ("new_ret_fwd", (1, 1, 8, 64, 64)),
         ("new_ret_bwd", (1, 1, 8, 64, 64)), ("new_na_k", (1, 1, 8, 128, 64)), ("new_na_v", (1, 1, 8, 128, 64)),
         ("new_mla_ckv", (1, 1, 128, 256)), ("new_mla_kpe", (1, 1, 128, 32))]


def shape_constants():
    import numpy as np

    part = np.arange(P)
    col, row = part // ROWS, part % ROWS
    u, rq = np.divmod(np.arange(112 * ROWS), ROWS)
    lat = (rq[None, :] - row[:, None]) * GRID_W + (u[None, :] - 48 - col[:, None])
    ctx = part[None, :] - part[:, None]
    d = np.concatenate([lat, ctx], axis=1)
    dist = d.astype(np.float32)
    token = np.arange(TL)
    time = (token % ROWS) * GRID_W + token // ROWS
    tpos = np.broadcast_to(np.stack([time + 1, TL - time]), (P, 2, TL)).astype(np.float32)
    kpos = np.stack([P - 1 - part, part], axis=1).astype(np.float32)
    mask = np.zeros((P, NB, KW, ROWS), np.float32)
    for b in range(NB):
        first = int(np.clip(b * BLK - 8, 0, GRID_W - KW))
        qc = b * BLK + col
        start = np.clip(qc - 8, 0, GRID_W - 16)
        kc = first + np.arange(KW)
        ok = (kc[None, :] >= start[:, None]) & (kc[None, :] < start[:, None] + 16)
        mask[:, b] = np.where(ok, 0.0, -1e30)[:, :, None]
    nf = ROPE // 4
    inv = (np.float32(10000.0) ** (-np.arange(nf, dtype=np.float32) / np.float32(nf))).astype(np.float32)
    ang = np.concatenate([(time // GRID_W).astype(np.float32)[:, None] * inv,
                          (time % GRID_W).astype(np.float32)[:, None] * inv], axis=-1)
    cos = np.repeat(np.cos(ang), 2, axis=1).T
    sin = np.repeat(np.sin(ang), 2, axis=1).T * np.where(np.arange(ROPE) % 2 == 0, -1.0, 1.0)[:, None]
    rope = np.concatenate([cos, sin, cos * MLA_SCALE, sin * MLA_SCALE]).astype(np.float32)
    return {"c_ident": np.eye(P, dtype=np.float32), "c_dist": dist, "c_tpos": tpos, "c_kpos": kpos,
            "c_mask": mask.reshape(P, NB, NKEY), "c_rope": rope}


def kernel(**inputs):
    import concourse.bacc as bacc
    import numpy as np
    from concourse.bass_utils import run_bass_kernel_spmd as run

    nc = bacc.Bacc("TRN2", target_bir_lowering=False, num_devices=1)
    arrays = {name: np.ascontiguousarray(inputs[name]) for name in _INS}
    swap = np.arange(ROPE) ^ 1
    w = np.asarray(inputs["w_in_c"])[0]
    arrays["w_in_c_swap"] = np.ascontiguousarray(np.concatenate([w, w[:, 640 + swap]], axis=1))
    w = np.asarray(inputs["w_uq"])[0].reshape(KQ * P, NH_MLA, 96)
    arrays["w_uq_heads"] = np.ascontiguousarray(
        np.concatenate([w, w[:, :, 64 + swap]], axis=2).reshape(KQ * P, NH_MLA * P))
    arrays.update(shape_constants())
    ins, feed = {}, {}
    for name, a in arrays.items():
        feed[f"in_{name}"] = a
        ins[name] = nc.dram_tensor(f"in_{name}", a.shape, mybir.dt.from_np(a.dtype), kind="ExternalInput").ap()
    outs = {name: nc.dram_tensor(f"out_{name}", shape, F32, kind="ExternalOutput").ap() for name, shape in _OUTS}
    build(nc, ins, outs)
    r = run(nc, [feed], core_ids=[0])
    return tuple(r.results[0][f"out_{name}"] for name, _ in _OUTS)
```

```python
from contextlib import ExitStack

import concourse.bass as bass
from concourse import mybir

F32 = mybir.dt.float32
F32R = mybir.dt.float32r
ALU = mybir.AluOpType
ACT = mybir.ActivationFunctionType
AX = mybir.AxisListType

P = 128
D = 1024
KD = D // P
TL, TC = 512, 128
T = TL + TC
NP = 128
HALF = T // 2
ROWS, GRID_W = 8, 64
BLK = P // ROWS
NB = TL // P
HD = 64
NH = 8
NH_MLA = 16
KW = 32
NKEY = KW * ROWS
RPB_C = 31
KQ, KKV = 3, 2
ROPE = 32
DFF = 4096
CH = 8
NCH = DFF // (CH * P)
EPS = 1e-6
MLA_SCALE = 96 ** -0.5
LN2 = 0.6931471805599453
LOWEST = -3.0e38

STAGE = 4
PIECE = 1024

SHIFT1, SCALE1, GATE1, SHIFT2, SCALE2, GATE2 = range(6)
A1, G1, A2, G2 = range(4)
ROW_GAIN, ROW_C, ROW_CTX, ROW_QN, ROW_KVN, VROWS = 0, 64, 72, 80, 83, 85

NORMS = (("in0", KD), ("y0a", KD), ("in0m", KD), ("y0m", KD), ("in1", KD), ("cq", KQ), ("ckv", KKV),
         ("y1a", KD), ("in1m", KD), ("y1m", KD))
PIECES = (("ac", 20), ("rv", 4), ("nv", 4), ("out0", 8), ("mlp0", 16 * NCH), ("in_c", 6),
          ("uq", 8), ("uk", 2), ("uv", 2), ("out1", 8), ("mlp1", 16 * NCH))
UNITS = (("ac", 20, "a"), ("out0", 8, "d"), ("mlp0", 16 * NCH, None), ("in_c", 6, "a"), ("uq", 16, "ad"),
         ("uk", 8, "a"), ("out1", 8, "d"), ("mlp1", 16 * NCH, None))


def first_of(table):
    out, at = {}, 0
    for row in table:
        out[row[0]] = at
        at += row[1]
    out["end"] = at
    return out


def evacuations():
    a = d = 0
    out = []
    for _, n, who in UNITS:
        for j in range(n):
            w = who or ("a" if j % 16 < 8 else "d")
            a += "a" in w
            d += "d" in w
            out.append((a if "a" in w else 0, d if "d" in w else 0))
    return out


NORM_AT = first_of(NORMS)
NORM_NO = {name: n for n, (name, _) in enumerate(NORMS)}
NORM_K = dict(NORMS)
ADD_AT = {name: sum(k - 2 for _, k in NORMS[:n]) for n, (name, _) in enumerate(NORMS)}
PIECE_AT = first_of(PIECES)
UNIT_AT = first_of(UNITS)
EVAC = evacuations()
MOD_NO = {"in0": 0, "in0m": 1, "in1": 2, "in1m": 3}
N_NA = NH * (NB + 1)
N_MLA = NH_MLA * (NB + 1)
ADA_W = 256
N_ADA = 2 * 6 * D // ADA_W
ADA_RING = 3
ADA_PARTS = (("start", 13), ("group", 11), ("out0", 8), ("mlp0", 8), ("out1", 8))
ADA_AT = first_of(ADA_PARTS)
ADA_SPLIT = ADA_AT["group"]
V_BANKS = (0, 4, 5, 6, 7)
GN_FIRST = 0
GATE_AT = (12, 14, 16, 18)
FIRST_KEY = (0, 64, 192, 256)
SPAN = ((0, TL), (TL, T))


def build(nc, i, o):
    top = ExitStack()
    with top:
        def sem(name):
            return top.enter_context(nc.semaphore(name))

        def sb(name, shape, dt=F32, stack=top):
            return stack.enter_context(nc.sbuf_tensor(name, shape, dt))

        def lay(offset, *rows):
            with ExitStack() as s:
                if offset:
                    sb(f"pad{len(pads)}", [P, offset * 256], stack=s)
                    pads.append(offset)
                return [sb(name, shape, dt, s) for name, shape, dt in rows]

        pads = []
        ps = top.enter_context(nc.psum_tensor("ps", [P, 8, 512], F32))

        def first_bank(g):
            if UNIT_AT["uq"] <= g < UNIT_AT["out1"]:
                return 2 * ((g - UNIT_AT["uq"]) % 3)
            return 2 * (g % 2)

        def pair(g, rows=slice(0, P)):
            b = first_bank(g)
            return ps[rows, b:b + 2, 0:HALF]

        def two(ap):
            return ap.rearrange("p (n c) -> p n c", n=2)

        xT = sb("xT", [P, KD, T])
        ident = sb("ident", [P, P])
        ones = sb("ones", [P, P])
        gnb = sb("gnb", [P, P])
        vecT = sb("vecT", [P, VROWS])
        badaT = sb("badaT", [P, 2, 48])
        mod = sb("mod", [P, 2, 48, 2])
        coef = sb("coef", [P, 2, 4, KD, 2])
        csil, cexp = sb("csil", [P, KD, 2]), sb("cexp", [P, 16])
        dec, lg, kpos, kdec = sb("dec", [P, 16]), sb("lg", [P, 8, 16]), sb("kpos", [P, 2]), sb("kdec", [P, 2, NH])
        rstd = sb("rstd", [P, T])
        rs = sb("rs", [P, 2, 5])
        eps = sb("eps", [P, 1])
        smM = sb("smM", [P, 3, 3])
        sq = sb("sq", [P, 2, T])
        nt = sb("nt", [P, 2, T])
        stage = sb("stage", [P, STAGE, PIECE])
        w_hi = sb("w_hi", [P, 2, PIECE], F32R)
        w_lo = sb("w_lo", [P, 2, PIECE], F32R)

        xtok, vrow, brow = lay(0, ("xtok", [P, 5, D], F32), ("vrow", [VROWS, P], F32), ("brow", [96, P], F32))
        ada_a, modrow_a = lay(64, ("ada_a", [P, ADA_RING, KD, ADA_W], F32), ("modrow_a", [2, 2, ADA_W], F32))
        ada_b, modrow_b = lay(44, ("ada_b", [P, ADA_RING, KD, ADA_W], F32), ("modrow_b", [2, 2, ADA_W], F32))
        ada_c, modrow_c = lay(112, ("ada_c", [P, ADA_RING, KD, ADA_W], F32), ("modrow_c", [2, 2, ADA_W], F32))
        ada_d, modrow_d = lay(100, ("ada_d", [P, ADA_RING, KD, ADA_W], F32), ("modrow_d", [2, 2, ADA_W], F32))
        oT, kzn, kz, rv, gate, nv, hA_hi, hA_lo = lay(
            0, ("oT", [P, KD, T], F32), ("kzn", [P, NH, T + NP], F32), ("kz", [P, NH, T], F32),
            ("rv", [P, 5, 512], F32), ("gate", [P, 4, T], F32), ("nv", [P, 5, 512], F32),
            ("hA_hi", [P, KD, T], F32R), ("hA_lo", [P, KD, T], F32R))
        dmat, tpos, sd, state, kd, fin = lay(
            94, ("dmat", [P, 2, 1024], F32), ("tpos", [P, 2, TL], F32), ("sd", [P, 5, 512], F32),
            ("state", [P, NH, HD], F32), ("kd", [P, 2, P], F32), ("fin", [P, NH, HD], F32))
        edec, qE = sq[:, :, 0:TL], nt[:, :, 0:TL]
        [dist] = lay(134, ("dist", [P, 1024], F32))
        mask, bm, kpast, vpast, pA, pTA, smA, nkt, nvs = lay(
            94, ("mask", [P, NB, NKEY], F32), ("bm", [P, 2, NKEY + NP], F32),
            ("kpast", [P, NH, HD], F32), ("vpast", [P, NH, HD], F32),
            ("pA", [P, 3, 384], F32), ("pTA", [P, 2, 384], F32), ("smA", [P, 4, 3], F32),
            ("nkt", [P, NH, HD], F32), ("nvs", [P, 3, 512], F32))
        [bias] = lay(121, ("bias", [P, NH, ROWS, 48], F32))
        s32 = sq[:, :, 0:384]
        hM_hi, hM_lo, h2_hi, h2_lo, yT, r32, s2 = lay(
            0, ("hM_hi", [P, KD, T], F32R), ("hM_lo", [P, KD, T], F32R), ("h2_hi", [P, CH, T], F32R),
            ("h2_lo", [P, CH, T], F32R), ("yT", [P, KD, T], F32), ("r32", [P, 2, T], F32), ("s2", [P, 2, T], F32))
        qm, km, vm, ck_hi, ck_lo, rope, kmas, ckn = lay(
            0, ("qm", [P, NH_MLA, T], F32), ("km", [P, NH_MLA, T + NP], F32), ("vm", [P, 6, D], F32),
            ("ck_hi", [P, KKV, T + NP], F32R), ("ck_lo", [P, KKV, T + NP], F32R), ("rope", [P, TL], F32),
            ("kmas", [P, T + NP], F32), ("ckn", [P, KKV, T + NP], F32))
        [cT] = lay(40, ("cT", [P, 6, T], F32))
        pastc, tokc, rt = lay(60, ("pastc", [P, 288], F32), ("tokc", [P, 288], F32), ("rt", [P, 2, TL], F32))
        cq_hi, cq_lo = lay(88, ("cq_hi", [P, KQ, T], F32R), ("cq_lo", [P, KQ, T], F32R))
        pM, pTM = lay(112, ("pM", [P, 3, T], F32), ("pTM", [P, 2, T], F32))
        [o6] = lay(40, ("o6", [P, 6, 2 * (T + NP)], F32R))
        [o2] = lay(126, ("o2", [P, 2, 2 * T], F32R))
        [xN] = lay(40, ("xN", [P, KD, T], F32))
        [ytok] = lay(0, ("ytok", [P, 5, D], F32))

        const_in, rows_in, x_in = sem("const_in"), sem("rows_in"), sem("x_in")
        ada_in = [sem(f"ada_in{n}") for n in range(ADA_RING)]
        decay_in, dist_in = sem("decay_in"), sem("dist_in")
        w_in = [sem(f"w_in{n}") for n in range(STAGE)]
        ret_in, na_in, na_bias_in, mla_in = sem("ret_in"), sem("na_in"), sem("na_bias_in"), sem("mla_in")
        stored = sem("stored")
        w_hi_done, w_lo_done = sem("w_hi_done"), sem("w_lo_done")
        unit_done, act_evac, dve_evac = sem("unit_done"), sem("act_evac"), sem("dve_evac")
        filled, rows_t, rows_out, x_t, x_out = [sem(n) for n in ("filled", "rows_t", "rows_out", "x_t", "x_out")]
        c_exp, c_ready = sem("c_exp"), sem("c_ready")
        ada_done, modrow_done, mod_t, mod_out = [sem(n) for n in ("ada_done", "modrow_done", "mod_t", "mod_out")]
        sq_done, added, sums_done, root_done, rs_ready, rstd_done = [
            sem(n) for n in ("sq_done", "added", "sums_done", "root_done", "rs_ready", "rstd_done")]
        x_done, h_full, h_hi_done, h_lo_done = [sem(n) for n in ("x_done", "h_full", "h_hi_done", "h_lo_done")]
        v_done, v_out = sem("v_done"), sem("v_out")
        decay_exp, decay_arg = sem("decay_exp"), sem("decay_arg")
        d_arg, d_exp, e_exp, qe_done = [sem(n) for n in ("d_arg", "d_exp", "e_exp", "qe_done")]
        rs_done, sd_done, ret_done, ret_out = [sem(n) for n in ("rs_done", "sd_done", "ret_done", "ret_out")]
        sd_used = sem("sd_used")
        g_exp, g_done, gn_mm, gn_cen, gn_sq, gn_var, gn_root, gn_done = [
            sem(n) for n in ("g_exp", "g_done", "gn_mm", "gn_cen", "gn_sq", "gn_var", "gn_root", "gn_done")]
        bias_zero, bm_done, past_t, past_out, nk_t, nk_out, nvs_done = [
            sem(n) for n in ("bias_zero", "bm_done", "past_t", "past_out", "nk_t", "nk_out", "nvs_done")]
        na_s, na_max, na_e, na_p, na_t, na_pt, na_pv, na_out = [
            sem(n) for n in ("na_s", "na_max", "na_e", "na_p", "na_t", "na_pt", "na_pv", "na_out")]
        o_hi_done, o_lo_done = sem("o_hi_done"), sem("o_lo_done")
        h2_hi_done, h2_lo_done, y_zero = sem("h2_hi_done"), sem("h2_lo_done"), sem("y_zero")
        cn_full, cn_hi, cn_lo = sem("cn_full"), sem("cn_hi"), sem("cn_lo")
        pc_t, pc_out, tok_t, tok_out, kmas_done, km_rope, qrope_done, vm_done, vm_out, km_zero, ctx_rope = [
            sem(n) for n in ("pc_t", "pc_out", "tok_t", "tok_out", "kmas_done", "km_rope", "qrope_done", "vm_done",
                             "vm_out", "km_zero", "ctx_rope")]
        m_s, m_max, m_e, m_p, m_t, m_pt, m_pv, m_out = [
            sem(n) for n in ("m_s", "m_max", "m_e", "m_p", "m_t", "m_pt", "m_pv", "m_out")]
        y_t, y_out, y_scaled, xN_pool = [sem(n) for n in ("y_t", "y_out", "y_scaled", "xN_pool")]

        class Chain:

            def __init__(self, engine, name):
                self.engine, self.sem, self.n, self.at = engine, sem(name), 0, 0

            def link(self, instruction):
                self.n += 1
                instruction.then_inc(self.sem, 1)
                self.engine.wait_ge(self.sem, self.at + self.n)

        w_ac = i["w_in_ac"][0].rearrange("(k p) m -> p k m", p=P)
        mats = {
            "out0": i["w_out_ac"][0].rearrange("(k p) m -> p k m", p=P),
            "in_c": i["w_in_c_swap"].rearrange("(k p) m -> p k m", p=P),
            "uq": i["w_uq_heads"].rearrange("(k p) m -> p k m", p=P),
            "uk": i["w_uk"][0].rearrange("(k p) m -> p k m", p=P),
            "uv": i["w_uv"][0].rearrange("(k p) m -> p k m", p=P),
            "out1": i["w_out_c"][0].rearrange("(k p) m -> p k m", p=P),
        }
        mlp_in = [i["w_mlp_in"][n].rearrange("(k p) m -> p k m", p=P) for n in range(2)]
        mlp_out = [i["w_mlp_out"][n].rearrange("(k p) m -> p k m", p=P) for n in range(2)]
        AC_COLS = [0, 512, 1536, 2048, 2560]
        RV_COL, NV_COL = 1024, 3072

        def piece_source(name, j):
            if name == "ac":
                c = AC_COLS[j // 4] + P * (j % 4)
                return w_ac[:, :, c:c + P]
            if name in ("rv", "nv"):
                c = RV_COL if name == "rv" else NV_COL
                return w_ac[:, 2 * j:2 * j + 2, c:c + 512]
            if name == "in_c":
                return mats[name][:, :, P * j:min(P * (j + 1), 704)]
            if name == "uq":
                return mats[name][:, :, 2 * P * j:2 * P * (j + 1)]
            if name in ("uk", "uv"):
                return mats[name][:, :, 512 * j:512 * (j + 1)]
            if name.startswith("mlp"):
                layer, c, j = int(name[3]), j // 16, j % 16
                if j < CH:
                    return mlp_in[layer][:, :, P * (CH * c + j):P * (CH * c + j + 1)]
                return mlp_out[layer][:, CH * c:CH * (c + 1), P * (j - CH):P * (j - CH + 1)]
            return mats[name][:, :, P * j:P * (j + 1)]

        def sums_at(name):
            c = 256 + 8 * (name == "ckv")
            return ps[:, 7, c:c + 5]

        def spread(name):
            b = 6 if name == "ckv" else 4
            return ps[:, b:b + 2, :].rearrange("p n c -> p (n c)")[:, 0:T]

        def piece_width(n):
            for name, k in PIECES:
                if PIECE_AT[name] <= n < PIECE_AT[name] + k:
                    if name == "in_c" and n - PIECE_AT[name] == 5:
                        return KD * 64
                    return 768 if name == "uq" else PIECE
            return PIECE


        def piece_used(n):
            name = [x for x, k in PIECES if PIECE_AT[x] <= n][-1]
            j = n - PIECE_AT[name]
            if name in ("rv", "nv"):
                return v_done, j + 1 + 4 * (name == "nv")
            if name == "uv":
                return vm_done, 6 * (j + 1)
            if name == "uk":
                return unit_done, UNIT_AT["uk"] + 4 * (j + 1)
            if name == "uq":
                return unit_done, UNIT_AT["uq"] + 2 * j + 2
            return unit_done, UNIT_AT[name] + j + 1

        def act_split(act, n, at=0):
            if isinstance(at, int) and n + at >= PIECE_AT["end"]:
                return
            width = piece_width(n)
            act.wait_ge(w_in[n % STAGE], 16 * (n // STAGE + 1) + at * (16 // STAGE))
            if n >= 2:
                used, count = piece_used(n - 2)
                act.wait_ge(used, count + at)
            nc.scalar.activation(w_hi[:, n % 2, 0:width], stage[:, n % STAGE, 0:width], ACT.Copy)\
                .then_inc(w_hi_done, 1)

        def dve_split(dve, n, at=0):
            if isinstance(at, int) and n + at >= PIECE_AT["end"]:
                return
            width = piece_width(n)
            dve.wait_ge(w_hi_done, n + 1 + at)
            nc.vector.tensor_tensor(w_lo[:, n % 2, 0:width], stage[:, n % STAGE, 0:width],
                                    w_hi[:, n % 2, 0:width].bitcast(F32), ALU.subtract).then_inc(w_lo_done, 1)

        def ada_place(n):
            part = [p for p, _ in ADA_PARTS if ADA_AT[p] <= n][-1]
            ring, rows = {"start": (ada_a, modrow_a), "group": (ada_b, modrow_b), "out1": (ada_d, modrow_d)}\
                .get(part, (ada_c, modrow_c))
            return ring[:, (n - ADA_AT[part]) % ADA_RING], rows

        def load_ada(queue, n):
            src = i["w_ada"][n // (N_ADA // 2)].rearrange("(k p) m -> p k m", p=P)
            c = ADA_W * (n % (N_ADA // 2))
            queue.dma_start(ada_place(n)[0], src[:, :, c:c + ADA_W])\
                .then_inc(ada_in[n % ADA_RING], 16)

        o_tiles = [(o6[:, k] if k < 6 else o2[:, k - 6]) for k in range(KD)]
        o_hi = [x[:, 0:T] for x in o_tiles]
        o_lo = [x[:, T:2 * T] for x in o_tiles]

        def gn_step(n):
            s = n - ADA_SPLIT - GN_FIRST
            return s if 0 <= s < 8 else None

        def result_parts(k):
            out = xN[:, k, 0:TL].rearrange("p (r c) -> p c r", r=ROWS)
            y, x = [v[:, 0:TL].rearrange("p (c r) -> p c r", r=ROWS) for v in (nt[:, k % 2, :], xT[:, k, :])]
            return [(out, y, x), (xN[:, k, TL:T], nt[:, k % 2, TL:T], xT[:, k, TL:T])]

        def by_rows(latents):
            return latents.rearrange("p (c r) -> p r c", r=ROWS)

        block = top.enter_context(nc.Block())

        @block.sync
        def _(sp):
            def load_piece(name, j):
                n = PIECE_AT[name] + j
                src = piece_source(name, j)
                if n >= STAGE:
                    sp.wait_ge(w_lo_done, n - STAGE + 1)
                dst = stage[:, n % STAGE, 0:piece_width(n)].rearrange("p (k m) -> p k m", k=src.shape[1])
                sp.dma_start(dst, src).then_inc(w_in[n % STAGE], 16)

            def load_pieces(name):
                for j in range(dict(PIECES)[name]):
                    load_piece(name, j)

            def load_mlp(layer):
                first = PIECE_AT[f"mlp{layer}"]
                with sp.Fori(0, NCH) as c:
                    for j in range(2 * CH):
                        n = first + j
                        sp.wait_ge(w_lo_done, n - STAGE + 1 + c * (2 * CH))
                        if j < CH:
                            src = mlp_in[layer][:, :, bass.ds(c * (CH * P) + P * j, P)]
                        else:
                            src = mlp_out[layer][:, bass.ds(c * CH, CH), P * (j - CH):P * (j - CH + 1)]
                        sp.dma_start(stage[:, n % STAGE, :].rearrange("p (k m) -> p k m", k=KD), src)\
                            .then_inc(w_in[n % STAGE], 16)

            sp.dma_start(ident[:], i["c_ident"]).then_inc(const_in, 16)
            sp.dma_start(vrow[ROW_C:ROW_C + 8, :], i["c"][0].rearrange("(k p) -> k p", p=P)).then_inc(rows_in, 16)
            sp.dma_start(vrow[ROW_CTX:ROW_CTX + 8, :], i["c_ctx"].rearrange("(k p) -> k p", p=P)).then_inc(rows_in, 16)
            sp.dma_start(vrow[0:64, :], i["norm_gains"].rearrange("l g (k p) -> (l g k) p", p=P)).then_inc(rows_in, 16)
            sp.dma_start(vrow[ROW_QN:ROW_QN + KQ, :], i["mla_q_norm"][0].rearrange("(k p) -> k p", p=P))\
                .then_inc(rows_in, 16)
            sp.dma_start(vrow[ROW_KVN:VROWS, :], i["mla_kv_norm"][0].rearrange("(k p) -> k p", p=P))\
                .then_inc(rows_in, 16)
            sp.dma_start(brow[:], i["b_ada"].rearrange("l (f p) -> (l f) p", p=P)).then_inc(rows_in, 16)
            for n in range(ADA_RING):
                load_ada(sp, n)
            sp.dma_start(xtok[:, 0:NB, :], i["x_sample"][0].rearrange("(b p) d -> p b d", p=P)).then_inc(x_in, 16)
            sp.dma_start(xtok[:, NB, :], i["x_prompt"][0]).then_inc(x_in, 16)
            sp.dma_start(kpos[:], i["c_kpos"]).then_inc(decay_in, 16)
            sp.dma_start(dec[:, 0:8], i["ret_decay_fwd"].to_broadcast([P, NH])).then_inc(decay_in, 16)
            sp.dma_start(dec[:, 8:16], i["ret_decay_bwd"].to_broadcast([P, NH])).then_inc(decay_in, 16)
            for n in range(ADA_RING, ADA_SPLIT):
                sp.wait_ge(ada_done, n - ADA_RING + 1)
                load_ada(sp, n)
                if n == 8:
                    for j in range(STAGE):
                        load_piece("ac", j)
            sp.dma_start(dist[:], i["c_dist"]).then_inc(dist_in, 16)
            for j in range(STAGE, 20):
                load_piece("ac", j)
            load_pieces("rv")
            load_pieces("nv")
            for j in range(STAGE):
                load_piece("out0", j)
            sp.wait_ge(v_done, 8)
            sp.dma_start(tpos[:], i["c_tpos"]).then_inc(ret_in, 16)
            sp.dma_start(state[0:64], i["state_ret_fwd"][0, 0].rearrange("h k v -> k h v")).then_inc(ret_in, 16)
            sp.dma_start(state[64:P], i["state_ret_bwd"][0, 0].rearrange("h k v -> k h v")).then_inc(ret_in, 16)
            sp.wait_ge(bias_zero, 1)
            rpb = i["na_rpb"]
            for c in range(BLK):
                for r in range(ROWS):
                    q = ROWS * c + r
                    sp.dma_start(bias[q:q + 1, :, :, c + 1:c + 1 + RPB_C],
                                 rpb[0:1, :, ROWS - 1 - r:2 * ROWS - 1 - r, :]).then_inc(na_bias_in, 16)
            sp.wait_ge(ret_out, NH)
            sp.dma_start(o["new_ret_fwd"][0, 0].rearrange("h k v -> k h v"), fin[0:64]).then_inc(stored, 16)
            sp.dma_start(o["new_ret_bwd"][0, 0].rearrange("h k v -> k h v"), fin[64:P]).then_inc(stored, 16)
            sp.wait_ge(stored, 32)
            sp.wait_ge(ret_out, NH)
            sp.dma_start(mask[:], i["c_mask"]).then_inc(na_in, 16)
            sp.dma_start(kpast[:], i["cache_na_k"][0, 0].rearrange("h t d -> t h d")).then_inc(na_in, 16)
            sp.dma_start(vpast[:], i["cache_na_v"][0, 0].rearrange("h t d -> t h d")).then_inc(na_in, 16)
            sp.dma_start(o["new_na_v"][0, 0].rearrange("h t d -> t h d"),
                         nv[:, NB, :].rearrange("p (h d) -> p h d", h=NH)).then_inc(stored, 16)
            sp.wait_ge(nk_out, NH)
            sp.dma_start(o["new_na_k"][0, 0].rearrange("h t d -> t h d"), nkt[:]).then_inc(stored, 16)
            for j in range(STAGE, 8):
                load_piece("out0", j)
            load_mlp(0)
            for j in range(STAGE):
                load_piece("in_c", j)
            sp.wait_ge(unit_done, UNIT_AT["in_c"])
            sp.wait_ge(ada_done, ADA_AT["out1"])
            sp.dma_start(pastc[:, 0:256], i["cache_mla_ckv"][0, 0]).then_inc(mla_in, 16)
            sp.dma_start(pastc[:, 256:288], i["cache_mla_kpe"][0, 0]).then_inc(mla_in, 16)
            sp.dma_start(rope[:], i["c_rope"]).then_inc(mla_in, 16)
            for j in range(STAGE, 6):
                load_piece("in_c", j)
            for j in range(6):
                load_piece("uq", j)
            sp.wait_ge(tok_out, 1)
            sp.dma_start(o["new_mla_ckv"][0, 0], tokc[:, 0:256]).then_inc(stored, 16)
            sp.dma_start(o["new_mla_kpe"][0, 0], tokc[:, 256:288]).then_inc(stored, 16)
            for j in range(6, 8):
                load_piece("uq", j)
            load_pieces("uk")
            load_pieces("uv")
            load_pieces("out1")
            load_mlp(1)
            for a, b in ((0, 4), (4, 7), (7, 8)):
                sp.wait_ge(y_out, b)
                cols = slice(P * a, P * b)
                sp.dma_start(o["y_sample"][0, :, cols].rearrange("(b p) d -> p b d", p=P), ytok[:, 0:NB, cols])\
                    .then_inc(stored, 16)
                sp.dma_start(o["y_prompt"][0, :, cols], ytok[:, NB, cols]).then_inc(stored, 16)
            sp.wait_ge(stored, 16 * 12)

        @block.tensor
        def _(pe):
            mm = nc.tensor.matmul

            def free_pair(g, at=0):
                if g == UNIT_AT["uq"] + 2:
                    return
                back = 3 if UNIT_AT["uq"] + 3 <= g < UNIT_AT["out1"] else 2
                if g >= back:
                    a, d = EVAC[g - back]
                    if a:
                        pe.wait_ge(act_evac, a + at)
                    if d:
                        pe.wait_ge(dve_evac, d + at)

            def unit(g, n, k_tiles, m, x_hi, x_lo, at=0, half_at=0, ready=None, base=0, wide=None):
                wide = wide or m
                pe.wait_ge(w_lo_done, n + 1 + at)
                free_pair(g, half_at)
                hi, lo = [w[:, n % 2, 0:k_tiles * wide].rearrange("p (k m) -> p k m", k=k_tiles)[:, :, base:base + m]
                          for w in (w_hi, w_lo)]
                for k in range(k_tiles):
                    if ready:
                        ready(k)
                    for s in range(2):
                        out = ps[0:m, first_bank(g) + s, 0:HALF]
                        xh, xl = [(x[k] if isinstance(x, list) else x[:, k, :])[:, s * HALF:(s + 1) * HALF]
                                  for x in (x_hi, x_lo)]
                        mm(out, lo[:, k], xh, start=k == 0, stop=False)
                        mm(out, hi[:, k], xl, start=False, stop=False)
                        last = mm(out, hi[:, k], xh, start=False, stop=k == k_tiles - 1)
                last.then_inc(unit_done, 1)

            def sum_squares(name):
                at, no, n = NORM_AT[name], NORM_NO[name], NORM_K[name]
                pe.wait_ge(sq_done, at + 1)
                if n > 2:
                    pe.wait_ge(added, ADD_AT[name] + n - 2)
                for b in range(5):
                    mm(sums_at(name)[:, b:b + 1], rstd[:, P * b:P * (b + 1)], ones[:, 0:1],
                       start=b == 0, stop=False)
                pe.wait_ge(sq_done, at + n)
                for b in range(5):
                    last = mm(sums_at(name)[:, b:b + 1], sq[:, (n - 1) % 2, P * b:P * (b + 1)], ones[:, 0:1],
                              start=False, stop=b == 4)
                last.then_inc(sums_done, 1)

            def spread_root(name):
                no = NORM_NO[name]
                pe.wait_ge(rs_ready, no + 1)
                for b in range(5):
                    last = mm(spread(name)[:, P * b:P * (b + 1)], rs[:, no % 2, b:b + 1].to_broadcast([P, P]),
                              ident[:], start=True, stop=True)
                last.then_inc(rstd_done, 1)

            def norm(name):
                sum_squares(name)
                spread_root(name)

            def h_ready(name):
                return lambda k: pe.wait_ge(h_lo_done, KD * MOD_NO[name] + k + 1)

            pe.wait_ge(const_in, 16)
            pe.wait_ge(filled, 5)
            pe.wait_ge(rows_in, 16 * 6)
            nc.tensor.transpose(ps[:, 4, 0:VROWS], vrow[:], ident[0:VROWS, 0:VROWS]).then_inc(rows_t, 1)
            nc.tensor.transpose(ps[:, 5, 0:96], brow[:], ident[0:96, 0:96]).then_inc(rows_t, 1)

            def turn_mod(n):
                pe.wait_ge(modrow_done, n + 1)
                if n >= 2:
                    pe.wait_ge(mod_out, n - 1)
                modrow = ada_place(n)[1]
                for j in range(2):
                    last = nc.tensor.transpose(ps[:, 2 + n % 2, 2 * j:2 * j + 2],
                                               modrow[:, n % 2, P * j:P * (j + 1)], ident[0:2, 0:2])
                last.then_inc(mod_t, 1)

            def ada_step(n):
                pe.wait_ge(ada_in[n % ADA_RING], 16 * (n // ADA_RING + 1))
                if n >= 2:
                    pe.wait_ge(modrow_done, n - 1)
                slot = ada_place(n)[0]
                for k in range(KD):
                    last = mm(ps[0:2, n % 2, 0:ADA_W], csil[:, k, :], slot[:, k, :],
                              start=k == 0, stop=k == KD - 1)
                last.then_inc(ada_done, 1)
                if n != 8 and n not in ADA_AT.values():
                    turn_mod(n - 1)
                if n == 7 or n + 1 in ADA_AT.values():
                    turn_mod(n)

            pe.wait_ge(c_ready, 1)
            for n in range(3):
                ada_step(n)
            pe.wait_ge(x_in, 16 * 2)
            pe.wait_ge(rows_out, 2)
            for j in range(10):
                b, g = j // 2, j % 2
                if j >= 4:
                    pe.wait_ge(x_out, j - 3)
                for n in range(4):
                    last = nc.tensor.transpose(ps[:, 4 + j % 4, P * n:P * (n + 1)],
                                               xtok[:, b, P * (4 * g + n):P * (4 * g + n + 1)], ident[:])
                last.then_inc(x_t, 1)
            ada_step(3)
            ada_step(4)
            pe.wait_ge(x_out, 10)
            for n in range(5, 8):
                ada_step(n)
            sum_squares("in0")
            ada_step(8)
            spread_root("in0")
            for n in range(9, ADA_SPLIT):
                ada_step(n)

            pe.wait_ge(mod_out, ADA_SPLIT)
            for j in range(20):
                unit(j, j, KD, P, hA_hi, hA_lo, ready=h_ready("in0") if j == 0 else None)
            for part in range(2):
                if part:
                    pe.wait_ge(v_out, 5)
                else:
                    pe.wait_ge(act_evac, EVAC[18][0])
                for j in range(4):
                    n = PIECE_AT["rv"] + 4 * part + j
                    pe.wait_ge(w_lo_done, n + 1)
                    for b in range(5):
                        for kk in range(2):
                            k = 2 * j + kk
                            xh, xl = [x[:, k, P * b:P * (b + 1)] for x in (hA_hi, hA_lo)]
                            wh, wl = [w[:, n % 2, 512 * kk:512 * (kk + 1)] for w in (w_hi, w_lo)]
                            out = ps[:, V_BANKS[b], :]
                            mm(out, xh, wl, start=k == 0, stop=False)
                            mm(out, xl, wh, start=False, stop=False)
                            last = mm(out, xh, wh, start=False, stop=k == KD - 1)
                    last.then_inc(v_done, 1)

            def ret_scores(h):
                q = oT[:, h // 2, :]
                for kt in range(5):
                    if h:
                        pe.wait_ge(sd_done, 5 * (h - 1) + kt + 1)
                    elif kt in (0, 4):
                        pe.wait_ge(v_out, 6 if kt == 0 else 9)
                    if kt < NB:
                        mm(ps[:, kt, :], kz[:, h, P * kt:P * (kt + 1)], q[:, 0:TL], start=True, stop=True)\
                            .then_inc(rs_done, 1)
                    else:
                        mm(ps[:, 6, 0:P], kz[:, h, TL:T], q[:, TL:T], start=True, stop=True)
                        nc.tensor.transpose(ps[:, 6, P:2 * P], kz[:, h, TL:T], ident[:]).then_inc(rs_done, 1)

            def ret_values(h):
                pe.wait_ge(qe_done, h + 1)
                pe.wait_ge(sd_done, 5 * h + 5)
                if h >= 2:
                    pe.wait_ge(ret_out, h - 1)
                out = ps[0:HD, 4 + h % 2, :]
                for kt in range(NB):
                    mm(out, rv[:, kt, HD * h:HD * (h + 1)], sd[:, kt, :], start=kt == 0, stop=False)\
                        .then_inc(sd_used, 1)
                mm(out, state[:, h, :], qE[:, h % 2, :], start=False, stop=True)
                if h:
                    pe.wait_ge(ret_out, h)
                v = rv[:, NB, HD * h:HD * (h + 1)]
                mm(ps[0:HD, 7, 0:P], v, sd[:, 4, 0:P], start=True, stop=True)
                mm(ps[:, 7, P:P + HD], kd[:, h % 2, :], v, start=True, stop=True).then_inc(ret_done, 1)

            pe.wait_ge(act_evac, 20)
            ret_scores(0)
            pe.wait_ge(v_out, 10)
            pe.wait_ge(ret_in, 16 * 3)
            for h in range(NH):
                if h < NH - 1:
                    ret_scores(h + 1)
                ret_values(h)
            pe.wait_ge(ret_out, NH)
            for n in range(ADA_SPLIT, ADA_AT["out0"]):
                ada_step(n)
                s = gn_step(n)
                if s is None:
                    continue
                m = s // 2
                if s % 2 == 0:
                    if m:
                        pe.wait_ge(gn_cen, m)
                    for s in range(2):
                        last = mm(ps[:, 4 + s, 0:HALF], gnb[:], oT[:, m, s * HALF:(s + 1) * HALF],
                                  start=True, stop=True)
                else:
                    pe.wait_ge(gn_sq, m + 1)
                    if m:
                        pe.wait_ge(gn_var, m)
                    for s in range(2):
                        last = mm(ps[:, 6 + s, 0:HALF], gnb[:], sq[:, 0, s * HALF:(s + 1) * HALF],
                                  start=True, stop=True)
                last.then_inc(gn_mm, 1)

            pe.wait_ge(mod_out, ADA_AT["out0"])
            pe.wait_ge(na_in, 16 * 3)
            for m in range(4):
                nc.tensor.transpose(ps[:, m, 0:P], kpast[:, 2 * m:2 * m + 2, :].rearrange("p h d -> p (h d)"),
                                    ident[:]).then_inc(past_t, 1)
            pe.wait_ge(gn_var, 4)
            for h in range(NH):
                if h >= 4:
                    pe.wait_ge(nk_out, h - 3)
                nc.tensor.transpose(ps[:, 4 + h % 4, 0:P], kzn[:, h, TL:T], ident[:]).then_inc(nk_t, 1)
            pe.wait_ge(past_out, 4)
            pe.wait_ge(nk_out, NH)
            pe.wait_ge(nvs_done, 1)

            def na_scores(t):
                m, b, h = t // 10, t % 10 // 2, 2 * (t // 10) + t % 2
                if t >= 2:
                    pe.wait_ge(na_max, t - 1)
                q = oT[:, 4 + m, P * b:P * (b + 1)]
                if b < NB:
                    mm(ps[:, t % 2, 0:NKEY], q, kzn[:, h, FIRST_KEY[b]:FIRST_KEY[b] + NKEY], start=True, stop=True)
                    mm(ps[:, t % 2, NKEY:NKEY + NP], q, kzn[:, h, T:T + NP], start=True, stop=True).then_inc(na_s, 1)
                else:
                    mm(ps[:, t % 2, 0:TC], q, kzn[:, h, TL:T], start=True, stop=True).then_inc(na_s, 1)

            def na_turn(t):
                pe.wait_ge(na_p, t + 1)
                if t >= 2:
                    pe.wait_ge(na_pt, t - 1)
                for kt in range(3 if t % 10 < 8 else 1):
                    last = nc.tensor.transpose(ps[:, 2 + t % 2, P * kt:P * (kt + 1)],
                                               pA[:, t % 3, P * kt:P * (kt + 1)], ident[:])
                last.then_inc(na_t, 1)

            def na_values(t):
                b, h = t % 10 // 2, 2 * (t // 10) + t % 2
                pe.wait_ge(na_pt, t + 1)
                if t >= 2:
                    pe.wait_ge(na_out, t - 1)
                hs = slice(HD * h, HD * (h + 1))
                if b < NB:
                    v = [(nv[:, 0], nv[:, 1]), (nvs[:, 0], nvs[:, 1]), (nvs[:, 1], nvs[:, 2]), (nv[:, 2], nv[:, 3])][b]
                    v = [v[0][:, hs], v[1][:, hs], vpast[:, h, :]]
                else:
                    v = [nv[:, NB, hs]]
                for kt in range(len(v)):
                    last = mm(ps[0:HD, 4 + t % 2, 0:P], v[kt], pTA[:, t % 2, P * kt:P * (kt + 1)],
                              start=kt == 0, stop=kt == len(v) - 1)
                last.then_inc(na_pv, 1)

            for t in range(N_NA + 3):
                if t < N_NA:
                    na_scores(t)
                if 2 <= t < N_NA + 2:
                    na_turn(t - 2)
                if t >= 3:
                    na_values(t - 3)

            def project_out(layer):
                name = f"out{layer}"

                def ready(k):
                    pe.wait_ge(o_lo_done, KD + 2 * (k + 1) if layer else k + 1)

                x_hi, x_lo = (o_hi, o_lo) if layer else (h2_hi, h2_lo)
                for j in range(8):
                    unit(UNIT_AT[name] + j, PIECE_AT[name] + j, KD, P, x_hi, x_lo, ready=ready if j == 0 else None)

            def norms_with_ada(y_name, x_name, part):
                n = ADA_AT[part]
                sum_squares(y_name)
                ada_step(n)
                spread_root(y_name)
                for j in range(1, 5):
                    ada_step(n + j)
                sum_squares(x_name)
                ada_step(n + 5)
                spread_root(x_name)
                ada_step(n + 6)
                ada_step(n + 7)
                pe.wait_ge(mod_out, n + 8)

            def mlp(layer):
                g0, n0 = UNIT_AT[f"mlp{layer}"], PIECE_AT[f"mlp{layer}"]
                with pe.Fori(0, NCH) as c:
                    for j in range(2 * CH):
                        if j < CH:
                            ready = h_ready("in0m" if layer == 0 else "in1m") if j == 0 else None
                            unit(g0 + j, n0 + j, KD, P, hM_hi, hM_lo, at=c * (2 * CH), half_at=c * CH, ready=ready)
                        else:
                            ready = (lambda k: pe.wait_ge(h2_lo_done, layer * NCH * CH + k + 1 + c * CH)) \
                                if j == CH else None
                            unit(g0 + j, n0 + j, CH, P, h2_hi, h2_lo, at=c * (2 * CH), half_at=c * CH, ready=ready)

            pe.wait_ge(na_max, N_NA)
            pe.wait_ge(na_pt, N_NA)
            pe.wait_ge(na_out, N_NA)
            project_out(0)
            norms_with_ada("y0a", "in0m", "out0")
            mlp(0)
            norms_with_ada("y0m", "in1", "mlp0")

            g0, n0 = UNIT_AT["in_c"], PIECE_AT["in_c"]
            pe.wait_ge(mla_in, 16 * 3)
            for k in range(KKV):
                nc.tensor.transpose(ps[:, 6, P * k:P * (k + 1)], pastc[:, P * k:P * (k + 1)], ident[:])
            nc.tensor.transpose(ps[0:ROPE, 7, 0:P], pastc[:, 256:288], ident[:]).then_inc(pc_t, 1)
            for j in range(6):
                unit(g0 + j, n0 + j, KD, P if j < 5 else 64, hM_hi, hM_lo, ready=h_ready("in1") if j == 0 else None)
                if j == 3:
                    pe.wait_ge(pc_out, 1)
                    sum_squares("cq")
                if j == 4:
                    spread_root("cq")
            sum_squares("ckv")
            g0, n0 = UNIT_AT["uq"], PIECE_AT["uq"]
            for h in range(NH_MLA):
                ready = (lambda k: pe.wait_ge(cn_lo, k + 1)) if h == 0 else None
                unit(g0 + h, n0 + h // 2, KQ, P, cq_hi, cq_lo, ready=ready, base=P * (h % 2), wide=2 * P)
                if h == 1:
                    spread_root("ckv")
                if h == 6:
                    pe.wait_ge(cn_lo, KQ + KKV)
                    for k in range(KKV):
                        nc.tensor.transpose(ps[:, 6, P * k:P * (k + 1)], ckn[:, k, TL + NP:T + NP], ident[:])
                    nc.tensor.transpose(ps[:, 7, 0:ROPE], cT[0:ROPE, 5, TL:T], ident[0:ROPE, 0:ROPE])\
                        .then_inc(tok_t, 1)
            g0, n0 = UNIT_AT["uk"], PIECE_AT["uk"]
            for m in range(8):
                g, n = g0 + m, n0 + m // 4
                pe.wait_ge(w_lo_done, n + 1)
                free_pair(g)
                for k in range(KKV):
                    c = 512 * k + P * (m % 4)
                    wh, wl = [w[:, n % 2, c:c + P] for w in (w_hi, w_lo)]
                    for s in range(2):
                        out = ps[:, first_bank(g) + s, 0:384]
                        xh, xl = [x[:, k, 384 * s:384 * (s + 1)] for x in (ck_hi, ck_lo)]
                        mm(out, wl, xh, start=k == 0, stop=False)
                        mm(out, wh, xl, start=False, stop=False)
                        last = mm(out, wh, xh, start=False, stop=k == KKV - 1)
                last.then_inc(unit_done, 1)
            pe.wait_ge(act_evac, EVAC[UNIT_AT["uk"] + 7][0])
            pe.wait_ge(tok_out, 1)
            for j in range(12):
                s, b = j // 6, j % 6
                n = PIECE_AT["uv"] + s
                pe.wait_ge(w_lo_done, n + 1)
                if j >= 4:
                    pe.wait_ge(vm_out, j - 3)
                for k in range(KKV):
                    wh, wl = [w[:, n % 2, 512 * k:512 * (k + 1)] for w in (w_hi, w_lo)]
                    xh, xl = [x[:, k, P * b:P * (b + 1)] for x in (ck_hi, ck_lo)]
                    out = ps[:, 4 + j % 4, :]
                    mm(out, xh, wl, start=k == 0, stop=False)
                    mm(out, xl, wh, start=False, stop=False)
                    last = mm(out, xh, wh, start=False, stop=k == KKV - 1)
                last.then_inc(vm_done, 1)

            def mla_scores(t):
                h, b = t // 5, t % 5
                if b == 0:
                    pe.wait_ge(kmas_done, h + 1)
                if t >= 2:
                    pe.wait_ge(m_e, t - 1)
                q = qm[:, h, P * b:P * (b + 1)]
                if b < NB:
                    for s in range(2):
                        last = mm(ps[:, 2 * (t % 2) + s, 0:HALF], q, km[:, h, HALF * s:HALF * (s + 1)],
                                  start=True, stop=True)
                else:
                    last = mm(ps[:, 2 * (t % 2), 0:TC], q, km[:, h, TL + NP:T + NP], start=True, stop=True)
                last.then_inc(m_s, 1)

            def mla_turn(t):
                pe.wait_ge(m_p, t + 1)
                if t:
                    pe.wait_ge(m_pt, t)
                for kt in range(5 if t % 5 < NB else 1):
                    last = nc.tensor.transpose(ps[:, 4 + kt // 4, P * (kt % 4):P * (kt % 4 + 1)],
                                               pM[:, t % 3, P * kt:P * (kt + 1)], ident[:])
                last.then_inc(m_t, 1)

            def mla_values(t):
                h, b = t // 5, t % 5
                pe.wait_ge(m_pt, t + 1)
                if t >= 2:
                    pe.wait_ge(m_out, t - 1)
                tiles = range(5) if b < NB else (5,)
                for j, kt in enumerate(tiles):
                    last = mm(ps[0:HD, 6 + t % 2, 0:P], vm[:, kt, HD * h:HD * (h + 1)],
                              pTM[:, t % 2, P * j:P * (j + 1)], start=j == 0, stop=j == len(tiles) - 1)
                last.then_inc(m_pv, 1)

            pe.wait_ge(act_evac, EVAC[UNIT_AT["uk"] + 7][0])
            pe.wait_ge(vm_out, 12)
            pe.wait_ge(ctx_rope, 1)
            for t in range(N_MLA + 3):
                if t < N_MLA:
                    mla_scores(t)
                if 2 <= t < N_MLA + 2:
                    mla_turn(t - 2)
                if t >= 3:
                    mla_values(t - 3)
            pe.wait_ge(m_e, N_MLA)
            project_out(1)
            norms_with_ada("y1a", "in1m", "out1")
            mlp(1)
            norm("y1m")

            pe.wait_ge(dve_evac, EVAC[-1][1])
            for k in range(KD):
                if k % 2:
                    pe.wait_ge(x_done, 3 * KD + k // 2 + 1)
                else:
                    pe.wait_ge(xN_pool, k // 2 + 1)
                if k >= 2:
                    pe.wait_ge(y_out, k - 1)
                for b in range(5):
                    last = nc.tensor.transpose(ps[:, 2 * (k % 2) + b // 4, P * (b % 4):P * (b % 4 + 1)],
                                               xN[:, k, P * b:P * (b + 1)], ident[:])
                last.then_inc(y_t, 1)

        @block.scalar
        def _(act):
            chain = Chain(act, "act_chain")
            f = nc.scalar.activation

            def square(name, k, src):
                no = NORM_NO[name]
                if k == 0 and no:
                    act.wait_ge(sums_done, no)
                if k >= 3:
                    act.wait_ge(added, ADD_AT[name] + k - 2)
                dst = sq[:, k % 2, :] if k else rstd[:]
                f(dst, src, ACT.Square).then_inc(sq_done, 1)

            def square_root(name, features):
                no = NORM_NO[name]
                act.wait_ge(sums_done, no + 1)
                if no >= 2:
                    act.wait_ge(rstd_done, no - 1)
                f(rs[:, no % 2, :], sums_at(name), ACT.Sqrt, scale=1.0 / features, bias=eps[:]).then_inc(root_done, 1)

            def norms_with_ada(y_name, x_name, part, x_first, out):
                n = ADA_AT[part]

                def rows(j):
                    mod_rows(n + j)
                    if j + ADA_RING < 8:
                        load_ada(nc.scalar, n + j + ADA_RING)

                square_root(y_name, D)
                rows(0)
                for k in range(KD):
                    act.wait_ge(x_done, x_first + k + 1)
                    square(x_name, k, xT[:, k, :])
                    if k in (3, 5, 6):
                        rows(1 + (3, 5, 6).index(k))
                rows(4)
                square_root(x_name, D)
                rows(5)
                operand(x_name, out, lambda k: rows(6 + k) if k < 2 else None)

            def operand(name, out, beside=None):
                for k in range(KD):
                    act.wait_ge(h_full, KD * MOD_NO[name] + k + 1)
                    f(out[:, k, :], nt[:, k % 2, :], ACT.Copy).then_inc(h_hi_done, 1)
                    if beside:
                        beside(k)

            def y_square(name, k, g0):
                if k >= 0:
                    act.wait_ge(dve_evac, EVAC[g0 + k][1])
                    square(name, k, yT[:, k, :])

            def mod_rows(n):
                act.wait_ge(ada_done, n + 1)
                if n >= 2:
                    act.wait_ge(mod_t, n - 1)
                modrow = ada_place(n)[1]
                f(modrow[:, n % 2, :], ps[0:2, n % 2, 0:ADA_W], ACT.Copy).then_inc(modrow_done, 1)

            act.wait_ge(rows_out, 1)
            f(cexp[:], vecT[:, ROW_C:ROW_C + 16], ACT.Exp, scale=-1.0).then_inc(c_exp, 1)
            for n in range(5):
                mod_rows(n)
            act.wait_ge(x_out, 10)
            for k in range(KD):
                square("in0", k, xT[:, k, :])
                if k in (3, 6):
                    mod_rows(5 + k // 6)
            mod_rows(7)
            square_root("in0", D)
            act_split(act, 0)
            mod_rows(8)
            operand("in0", hA_hi, lambda k: mod_rows(8 + k // 2) if k in (2, 4, 6) else None)
            for n in range(12, ADA_SPLIT):
                mod_rows(n)
            act.wait_ge(filled, 7)
            for j in range(20):
                act_split(act, j + 1)
                act.wait_ge(unit_done, j + 1)
                kind, m, src = j // 4, j % 4, pair(j)
                if kind == 0:
                    last = f(two(oT[:, m, :]), src, ACT.Copy)
                elif kind == 1:
                    f(two(kz[0:64, 2 * m, :]), pair(j, slice(0, 64)), ACT.Copy, scale=HD ** -0.5)
                    last = f(two(kz[64:P, 2 * m + 1, :]), pair(j, slice(64, P)), ACT.Copy, scale=HD ** -0.5)
                elif kind == 2:
                    last = f(two(gate[:, m, :]), src, ACT.Copy)
                elif kind == 3:
                    last = f(two(oT[:, 4 + m, :]), src, ACT.Copy, scale=HD ** -0.5)
                else:
                    f(two(kzn[0:64, 2 * m, 0:T]), pair(j, slice(0, 64)), ACT.Copy)
                    last = f(two(kzn[64:P, 2 * m + 1, 0:T]), pair(j, slice(64, P)), ACT.Copy)
                last.then_inc(act_evac, 1)
                if j in GATE_AT:
                    m = GATE_AT.index(j)
                    act.wait_ge(act_evac, EVAC[8 + m][0])
                    if m >= 2:
                        act.wait_ge(g_done, m - 1)
                    f(nt[:, m % 2, :], gate[:, m, :], ACT.Exp, scale=-1.0).then_inc(g_exp, 1)
                if j == 5:
                    act.wait_ge(decay_in, 16 * 3)
                    f(lg[:, 0, :], dec[:], ACT.Exp, scale=LN2).then_inc(decay_exp, 1)
                if j == 8:
                    act.wait_ge(decay_arg, 1)
                    f(lg[:, 2, :], lg[:, 1, :], ACT.Ln).then_inc(decay_exp, 1)
                if j == 11:
                    act.wait_ge(decay_arg, 2)
                    f(kdec[:], kdec[:], ACT.Exp).then_inc(decay_exp, 1)
            for n in range(21, 29):
                act_split(act, n)

            def head_decays(h):
                act.wait_ge(d_arg, h + 1)
                f(dmat[:, h % 2, :], dmat[:, h % 2, :], ACT.Exp).then_inc(d_exp, 1)

            act.wait_ge(v_done, 8)
            for b in range(5):
                f(nv[:, b, :], ps[:, V_BANKS[b], :], ACT.Copy).then_inc(v_out, 1)
                if b == 0:
                    head_decays(0)
            act.wait_ge(ret_in, 16 * 3)

            def ret_copy(h):
                act.wait_ge(ret_done, h + 1)
                rows = slice(64 * (h % 2), 64 * (h % 2) + 64)
                f(oT[rows, h // 2, 0:TL], ps[0:64, 4 + h % 2, :], ACT.Copy)
                f(oT[rows, h // 2, TL:T], ps[0:64, 7, 0:P], ACT.Copy)
                f(fin[:, h, :], ps[:, 7, P:P + HD], ACT.Copy).then_inc(ret_out, 1)

            for h in range(NH):
                rows = slice(64 * (h % 2), 64 * (h % 2) + 64)
                if h >= 2:
                    act.wait_ge(qe_done, h - 1)
                for s in range(2):
                    last = f(edec[rows, s, :], tpos[rows, s, :], ACT.Exp, scale=lg[rows, 7, 8 * s + h:8 * s + h + 1])
                last.then_inc(e_exp, 1)
                if h:
                    head_decays(h)
                    ret_copy(h - 1)
                if h in (5, 7):
                    load_ada(nc.scalar, ADA_SPLIT + (h == 7))
            ret_copy(NH - 1)
            load_ada(nc.scalar, ADA_SPLIT + 2)
            for n in range(ADA_SPLIT, ADA_AT["out0"]):
                mod_rows(n)
                if n + ADA_RING < ADA_AT["out0"]:
                    load_ada(nc.scalar, n + ADA_RING)
                s = gn_step(n)
                if s is None:
                    continue
                if s % 2 == 0:
                    act.wait_ge(gn_cen, s // 2 + 1)
                    f(sq[:, 0, :], nt[:, 0, :], ACT.Square).then_inc(gn_sq, 1)
                else:
                    act.wait_ge(gn_var, s // 2 + 1)
                    f(rstd[:], rstd[:], ACT.Sqrt).then_inc(gn_root, 1)

            for m in range(4):
                act.wait_ge(past_t, m + 1)
                f(kzn[0:64, 2 * m, T:T + NP], ps[0:64, m, 0:P], ACT.Copy)
                f(kzn[64:P, 2 * m + 1, T:T + NP], ps[64:P, m, 0:P], ACT.Copy).then_inc(past_out, 1)
            for h in range(NH):
                act.wait_ge(nk_t, h + 1)
                c = HD * (h % 2)
                f(nkt[:, h, :], ps[:, 4 + h % 4, c:c + HD], ACT.Copy).then_inc(nk_out, 1)

            def na_exp(t):
                w = 384 if t % 10 < 8 else TC
                act.wait_ge(na_max, t + 1)
                if t >= 3:
                    act.wait_ge(na_t, t - 2)
                e = t % 3
                f(pA[:, e, 0:w], s32[:, t % 2, 0:w], ACT.Exp, bias=smA[:, 1, e:e + 1],
                  accum_out=smA[:, 2, e:e + 1]).then_inc(na_e, 1)

            def na_copy(t):
                w = 384 if t % 10 < 8 else TC
                act.wait_ge(na_t, t + 1)
                if t >= 2:
                    act.wait_ge(na_pv, t - 1)
                f(pTA[:, t % 2, 0:w], ps[:, 2 + t % 2, 0:w], ACT.Copy).then_inc(na_pt, 1)

            for t in range(N_NA + 2):
                if t < N_NA:
                    na_exp(t)
                if t >= 2:
                    na_copy(t - 2)

            def mlp(layer):
                g0, n0 = UNIT_AT[f"mlp{layer}"], PIECE_AT[f"mlp{layer}"]
                base = layer * NCH * CH

                def chunk(c):
                    at, half = c * (2 * CH), c * CH
                    for j in range(2 * CH):
                        act_split(act, n0 + j + 1, at)
                        if j < CH:
                            act.wait_ge(unit_done, g0 + j + 1 + at)
                            if not isinstance(c, int) or base + j - 1 + half > 0:
                                act.wait_ge(h2_lo_done, base + j - 1 + half)
                            f(two(r32[:, j % 2, :]), pair(g0 + j), ACT.Relu).then_inc(act_evac, 1)
                            act.wait_ge(act_evac, EVAC[g0][0] + j + half)
                            f(h2_hi[:, j, :], r32[:, j % 2, :], ACT.Square).then_inc(h2_hi_done, 1)
                        elif isinstance(c, int) and c == NCH - 1:
                            y_square(f"y{layer}m", j - CH - 1, last0)

                last0 = g0 + NCH * 2 * CH - CH
                chunk(0)
                with act.Fori(1, NCH - 1) as c:
                    chunk(c)
                chunk(NCH - 1)
                y_square(f"y{layer}m", KD - 1, last0)

            act.wait_ge(na_out, N_NA)
            for k in range(KD):
                f(h2_hi[:, k, :], oT[:, k, :], ACT.Copy).then_inc(o_hi_done, 1)
            act.wait_ge(stored, 16 * 4)
            for n in range(ADA_RING):
                load_ada(nc.scalar, ADA_AT["out0"] + n)
            for j in range(8):
                act_split(act, PIECE_AT["out0"] + j + 1)
                y_square("y0a", j - 1, UNIT_AT["out0"])
            y_square("y0a", KD - 1, UNIT_AT["out0"])
            norms_with_ada("y0a", "in0m", "out0", 0, hM_hi)
            for n in range(ADA_RING):
                load_ada(nc.scalar, ADA_AT["mlp0"] + n)
            mlp(0)
            norms_with_ada("y0m", "in1", "mlp0", KD, hM_hi)

            act.wait_ge(pc_t, 1)
            for k in range(KKV):
                f(ckn[:, k, TL:TL + NP], ps[:, 6, P * k:P * (k + 1)], ACT.Copy)
            act.wait_ge(km_zero, 1)
            f(kmas[96:P, TL:TL + NP], ps[0:ROPE, 7, 0:P], ACT.Copy).then_inc(pc_out, 1)
            for j in range(6):
                g, n = UNIT_AT["in_c"] + j, PIECE_AT["in_c"] + j
                act_split(act, n + 1)
                if j == 5:
                    for k in range(KQ):
                        act.wait_ge(cn_full, k + 1)
                        f(cq_hi[:, k, :], nt[:, k % 2, :], ACT.Copy).then_inc(cn_hi, 1)
                act.wait_ge(unit_done, g + 1)
                m = P if j < 5 else 64
                f(two(cT[0:m, j, :]), pair(g, slice(0, m)), ACT.Copy).then_inc(act_evac, 1)
                if j < 5:
                    act.wait_ge(act_evac, EVAC[g][0])
                    square("cq" if j < KQ else "ckv", j % KQ, cT[:, j, :])
                if j == KQ:
                    square_root("cq", KQ * P)
            square_root("ckv", KKV * P)
            act.wait_ge(act_evac, EVAC[UNIT_AT["in_c"] + 5][0])
            f(kmas[96:P, TL + NP:T + NP], cT[0:ROPE, 5, TL:T], ACT.Copy).then_inc(km_rope, 1)
            for h in range(NH_MLA):
                g = UNIT_AT["uq"] + h
                if h % 2 == 0:
                    act_split(act, PIECE_AT["uq"] + h // 2 + 1)
                act.wait_ge(unit_done, g + 1)
                if h == 0:
                    act.wait_ge(cn_lo, KQ)
                f(two(qm[0:64, h, :]), pair(g, slice(0, 64)), ACT.Copy, scale=MLA_SCALE)
                f(two(qm[96:P, h, :]), pair(g, slice(64, 96)), ACT.Copy, scale=MLA_SCALE).then_inc(act_evac, 1)
                if h == 1:
                    act.wait_ge(pc_out, 1)
                    for k in range(KKV):
                        act.wait_ge(cn_full, KQ + k + 1)
                        f(ck_hi[:, k, :], ckn[:, k, :], ACT.Copy).then_inc(cn_hi, 1)
                if h == 7:
                    act.wait_ge(tok_t, 1)
                    f(tokc[:, 0:256], ps[:, 6, 0:256], ACT.Copy)
                    f(tokc[:, 256:288], ps[:, 7, 0:ROPE], ACT.Copy).then_inc(tok_out, 1)
            act_split(act, PIECE_AT["uk"] + 1)
            act.wait_ge(tok_out, 1)
            act.wait_ge(stored, 16 * 6)
            act.wait_ge(qrope_done, NH_MLA)
            act.wait_ge(km_rope, 2)
            for m in range(8):
                g = UNIT_AT["uk"] + m
                if m == 4:
                    act_split(act, PIECE_AT["uv"])
                act.wait_ge(unit_done, g + 1)
                for s in range(2):
                    src = ps[64 * s:64 * s + 64, first_bank(g):first_bank(g) + 2, 0:384]
                    last = f(km[0:64, 2 * m + s, :].rearrange("p (n c) -> p n c", n=2), src, ACT.Copy)
                last.then_inc(act_evac, 1)
            act_split(act, PIECE_AT["uv"] + 1)
            act.wait_ge(vm_done, 12)

            def mla_exp(t):
                act.wait_ge(m_max, t + 1)
                if t >= 3:
                    act.wait_ge(m_t, t - 2)
                b2, e = 2 * (t % 2), t % 3
                if t % 5 < NB:
                    src, dst = ps[:, b2:b2 + 2, 0:HALF], two(pM[:, e, :])
                else:
                    src, dst = ps[:, b2, 0:TC], pM[:, e, 0:TC]
                f(dst, src, ACT.Exp, bias=smM[:, 0, e:e + 1], accum_out=smM[:, 1, e:e + 1])\
                    .then_inc(m_e, 1)

            def mla_copy(t):
                act.wait_ge(m_t, t + 1)
                if t >= 2:
                    act.wait_ge(m_pv, t - 1)
                w = T if t % 5 < NB else TC
                src = ps[:, 4:6, :].rearrange("p n c -> p (n c)")
                f(pTM[:, t % 2, 0:w], src[:, 0:w], ACT.Copy).then_inc(m_pt, 1)

            def head_high(h):
                act.wait_ge(m_out, 5 * (h + 1))
                if h == 12:
                    act.wait_ge(kmas_done, NH_MLA)
                rows = slice(64 * (h % 2), 64 * (h % 2) + 64)
                f(o_hi[h // 2][rows], qm[rows, h, :], ACT.Copy).then_inc(o_hi_done, 1)

            for t in range(N_MLA + 2):
                if t < N_MLA:
                    mla_exp(t)
                if t >= 2:
                    mla_copy(t - 2)
                h, at = divmod(t - 15, 5)
                if h >= 0 and at == 0 and h < NH_MLA - 4:
                    head_high(h)
            act_split(act, PIECE_AT["out1"])
            for h in range(NH_MLA - 4, NH_MLA):
                head_high(h)
            for n in range(ADA_RING):
                load_ada(nc.scalar, ADA_AT["out1"] + n)
            for j in range(8):
                act_split(act, PIECE_AT["out1"] + j + 1)
                y_square("y1a", j - 1, UNIT_AT["out1"])
            y_square("y1a", KD - 1, UNIT_AT["out1"])
            norms_with_ada("y1a", "in1m", "out1", 2 * KD, hM_hi)
            mlp(1)
            square_root("y1m", D)
            for k in range(KD):
                act.wait_ge(y_t, k + 1)
                src = ps[:, 2 * (k % 2):2 * (k % 2) + 2, :].rearrange("p n c -> p (n c)")[:, 0:T]
                f(ytok[:, :, P * k:P * (k + 1)], src.rearrange("p (b f) -> p b f", b=5), ACT.Copy).then_inc(y_out, 1)

        @block.vector
        def _(dve):
            chain = Chain(dve, "dve_chain")
            link = chain.link
            tt, ts, stt = nc.vector.tensor_tensor, nc.vector.tensor_scalar, nc.vector.scalar_tensor_tensor

            def root(name):
                no = NORM_NO[name]
                dve.wait_ge(root_done, no + 1)
                nc.vector.reciprocal(rs[:, no % 2, :], rs[:, no % 2, :]).then_inc(rs_ready, 1)

            def spread_ready(name):
                dve.wait_ge(rstd_done, NORM_NO[name] + 1)
                return spread(name)

            def add_residual(name, layer, which, beside=None):
                root(name)
                rstd = spread_ready(name)
                first = KD * (2 * layer + (which == G2))
                for k in range(KD):
                    if k >= 2:
                        dve.wait_ge(x_done, first + k - 1)
                    link(tt(nt[:, k % 2, :], yT[:, k, :], rstd, ALU.mult))
                    for g, (a, b) in enumerate(SPAN):
                        last = stt(xT[:, k, a:b], nt[:, k % 2, a:b], coef[:, layer, which, k, g:g + 1],
                                   xT[:, k, a:b], ALU.mult, ALU.add)
                    last.then_inc(x_done, 1)
                    if beside:
                        beside(k)

            def last_residual():
                root("y1m")
                rstd = spread_ready("y1m")
                for k in range(KD):
                    if k >= 2 and k % 2 == 0:
                        dve.wait_ge(xN_pool, k // 2)
                    for g, (a, b) in enumerate(SPAN):
                        last = stt(nt[:, k % 2, a:b], yT[:, k, a:b], coef[:, 1, G2, k, g:g + 1], rstd[:, a:b],
                                   ALU.mult, ALU.mult)
                    if k % 2 == 0:
                        last.then_inc(y_scaled, 1)
                    else:
                        link(last)
                        for out, y, x in result_parts(k):
                            last = tt(out, y, x, ALU.add)
                        last.then_inc(x_done, 1)
                        if k < KD - 1:
                            dve.wait_ge(x_done, 3 * KD + k // 2 + 1)

            def modulate(name, layer, which, shift, beside=None):
                rstd = spread_ready(name)
                for k in range(KD):
                    if k >= 2:
                        dve.wait_ge(h_lo_done, KD * MOD_NO[name] + k - 1)
                    link(tt(nt[:, k % 2, :], xT[:, k, :], rstd, ALU.mult))
                    for g, (a, b) in enumerate(SPAN):
                        last = ts(nt[:, k % 2, a:b], nt[:, k % 2, a:b], coef[:, layer, which, k, g:g + 1],
                                  mod[:, layer, 8 * shift + k, g:g + 1], ALU.mult, ALU.add)
                    last.then_inc(h_full, 1)
                    if beside:
                        beside(k)

            def mod_columns(n):
                layer, c = divmod(n, N_ADA // 2)
                dve.wait_ge(mod_t, n + 1)
                cols = ps[:, 2 + n % 2, 0:4].rearrange("p (j g) -> p j g", g=2)
                for g in range(2):
                    last = tt(mod[:, layer, 2 * c:2 * c + 2, g], cols[:, :, g], badaT[:, layer, 2 * c:2 * c + 2],
                              ALU.add)
                last.then_inc(mod_out, 1)
                which = {SCALE1: A1, GATE1: G1, SCALE2: A2, GATE2: G2}.get(c // 4)
                if c % 4 == 3 and which is not None:
                    dve.wait_ge(mod_out, n + 1)
                    part = c // 4
                    for g in range(2):
                        gain = vecT[:, ROW_GAIN + 32 * layer + 8 * which:ROW_GAIN + 32 * layer + 8 * which + 8]
                        m = mod[:, layer, 8 * part:8 * part + 8, g]
                        last = stt(coef[:, layer, which, :, g], m, 1.0 if which in (A1, A2) else 0.0, gain,
                                   ALU.add, ALU.mult)
                    link(last)

            dve.wait_ge(rows_t, 1)
            nc.vector.tensor_copy(vecT[:], ps[:, 4, 0:VROWS]).then_inc(rows_out, 1)
            dve.wait_ge(rows_t, 2)
            nc.vector.tensor_copy(badaT[:].rearrange("p l f -> p (l f)"), ps[:, 5, 0:96]).then_inc(rows_out, 1)
            dve.wait_ge(c_exp, 1)
            link(ts(cexp[:], cexp[:], 1.0, None, ALU.add))
            link(nc.vector.reciprocal(cexp[:], cexp[:]))
            for g in range(2):
                last = tt(csil[:, :, g], vecT[:, ROW_C + 8 * g:ROW_C + 8 * g + 8], cexp[:, 8 * g:8 * g + 8], ALU.mult)
            last.then_inc(c_ready, 1)
            mod_columns(0)
            mod_columns(1)
            for j in range(10):
                b, g = j // 2, j % 2
                dve.wait_ge(x_t, j + 1)
                src, tiles = ps[:, 4 + j % 4, :], slice(4 * g, 4 * g + 4)
                if b < NB:
                    dst = xT[:, tiles, 0:TL].rearrange("p k (c r) -> p k r c", r=ROWS)[:, :, 2 * b:2 * b + 2, :]
                    last = nc.vector.tensor_copy(dst, src.rearrange("p (k r c) -> p k r c", k=4, r=2))
                else:
                    last = nc.vector.tensor_copy(xT[:, tiles, TL:T], src.rearrange("p (k t) -> p k t", k=4))
                last.then_inc(x_out, 1)
            mod_columns(2)
            mod_columns(3)

            for n in range(4, 8):
                mod_columns(n)
            root("in0")
            dve_split(dve, 0)
            modulate("in0", 0, A1, SHIFT1, lambda k: mod_columns(7 + k // 2) if k in (2, 4, 6) else None)
            for n in range(11, ADA_SPLIT):
                mod_columns(n)
            y, w, ln, z, z2, s, big, out = [lg[:, n, :] for n in range(8)]
            back = lg[:, 0, 0:8]

            def decay_start():
                dve.wait_ge(decay_exp, 1)
                link(ts(w, y, -1.0, 1.0, ALU.mult, ALU.add))
                ts(w, w, 1e-30, None, ALU.max).then_inc(decay_arg, 1)
                ts(big, y, 0.5, None, ALU.is_gt)
                link(ts(y, y, 0.5, None, ALU.min))
                link(ts(z, y, -1.0, 2.0, ALU.mult, ALU.add))
                link(nc.vector.reciprocal(z, z))
                link(tt(z, z, y, ALU.mult))
                link(tt(z2, z, z, ALU.mult))
                link(ts(s, z2, 1.0 / 21, 1.0 / 19, ALU.mult, ALU.add))

            def decay_series(first, last):
                for d in range(first, last, -2):
                    link(tt(s, s, z2, ALU.mult))
                    link(ts(s, s, 1.0 / d, None, ALU.add))

            def decay_end():
                link(tt(s, s, z, ALU.mult))
                link(ts(s, s, -2.0, None, ALU.mult))
                dve.wait_ge(decay_exp, 2)
                link(tt(ln, ln, s, ALU.subtract))
                link(tt(ln, ln, big, ALU.mult))
                link(tt(out, ln, s, ALU.add))
                for s_ in range(2):
                    last = ts(kdec[:, s_, :], out[:, 8 * s_:8 * s_ + 8], kpos[:, s_:s_ + 1], None, ALU.mult)
                last.then_inc(decay_arg, 1)
                link(ts(back, out[:, 8:16], -1.0, None, ALU.mult))

            for n in range(1, 10):
                dve_split(dve, n)
                if n == 7:
                    decay_start()
                if n == 8:
                    decay_series(17, 8)
                if n == 9:
                    decay_series(7, 0)
            for n in range(10, 24):
                dve_split(dve, n)
                if n == 10:
                    decay_end()
                if n - 2 in GATE_AT:
                    m = GATE_AT.index(n - 2)
                    dve.wait_ge(g_exp, m + 1)
                    link(ts(nt[:, m % 2, :], nt[:, m % 2, :], 1.0, None, ALU.add))
                    link(nc.vector.reciprocal(nt[:, m % 2, :], nt[:, m % 2, :]))
                    tt(gate[:, m, :], gate[:, m, :], nt[:, m % 2, :], ALU.mult).then_inc(g_done, 1)
            dve_split(dve, 24)
            dve.wait_ge(v_done, 4)
            for b in range(5):
                nc.vector.tensor_copy(rv[:, b, :], ps[:, V_BANKS[b], :]).then_inc(v_out, 1)
            for n in range(25, 29):
                dve_split(dve, n)
            dve.wait_ge(v_done, 8)

            def decay_args(h):
                link(ts(dmat[:, h % 2, :], dist[:], back[:, h:h + 1], None, ALU.mult))
                stt(dmat[:, h % 2, :], dist[:], out[:, h:h + 1], dmat[:, h % 2, :], ALU.mult, ALU.min)\
                    .then_inc(d_arg, 1)

            dve.wait_ge(dist_in, 16)
            decay_args(0)
            dve.wait_ge(decay_exp, 3)
            for h in range(NH):
                rows = slice(64 * (h % 2), 64 * (h % 2) + 64)

                def decayed_queries():
                    dve.wait_ge(e_exp, h + 1)
                    if h >= 2:
                        dve.wait_ge(ret_done, h - 1)
                    for s_ in range(2):
                        last = tt(qE[64 * s_:64 * s_ + 64, h % 2, :], oT[rows, h // 2, 0:TL], edec[rows, s_, :],
                                  ALU.mult)
                    last.then_inc(qe_done, 1)

                if h:
                    decayed_queries()
                dve.wait_ge(d_exp, h + 1)
                for c in (384, 896):
                    last = tt(dmat[:, h % 2, c:c + P], dmat[:, h % 2, c:c + P], ident[:], ALU.add)
                link(last)
                if h < NH - 1:
                    decay_args(h + 1)
                for kt in range(5):
                    dve.wait_ge(rs_done, 5 * h + kt + 1)
                    if h and kt < NB:
                        dve.wait_ge(sd_used, NB * (h - 1) + kt + 1)
                    elif h:
                        dve.wait_ge(ret_done, h)
                    if kt < NB:
                        c = ROWS * (48 - BLK * kt)
                        tt(sd[:, kt, :], ps[:, kt, :], dmat[:, h % 2, c:c + TL], ALU.mult).then_inc(sd_done, 1)
                    else:
                        tt(sd[:, 4, 0:P], ps[:, 6, 0:P], dmat[:, h % 2, 896:1024], ALU.mult)
                        c = P + HD * (h % 2)
                        for s_ in range(2):
                            last = ts(kd[:, h % 2, HD * s_:HD * (s_ + 1)], ps[:, 6, c:c + HD], kdec[:, s_, h:h + 1],
                                      None, ALU.mult)
                        last.then_inc(sd_done, 1)
                if h == 0:
                    decayed_queries()
            for n in range(ADA_SPLIT, ADA_AT["out0"]):
                if n > ADA_SPLIT:
                    mod_columns(n - 1)
                s = gn_step(n)
                if s is None:
                    continue
                m = s // 2
                if s % 2 == 0:
                    if m:
                        dve.wait_ge(gn_done, m)
                    else:
                        dve.wait_ge(g_done, 4)
                    dve.wait_ge(gn_mm, 2 * m + 1)
                    tt(two(nt[:, 0, :]), two(oT[:, m, :]), ps[:, 4:6, 0:HALF], ALU.subtract).then_inc(gn_cen, 1)
                else:
                    dve.wait_ge(gn_mm, 2 * m + 2)
                    ts(two(rstd[:]), ps[:, 6:8, 0:HALF], EPS, None, ALU.add).then_inc(gn_var, 1)
                    dve.wait_ge(gn_root, m + 1)
                    link(nc.vector.reciprocal(rstd[:], rstd[:]))
                    link(tt(nt[:, 0, :], nt[:, 0, :], rstd[:], ALU.mult))
                    tt(oT[:, m, :], nt[:, 0, :], gate[:, m, :], ALU.mult).then_inc(gn_done, 1)
            mod_columns(ADA_AT["out0"] - 1)

            dve.wait_ge(na_in, 16 * 3)
            for j in range(3):
                nc.vector.tensor_copy(nvs[0:64, j, :], nv[64:P, j, :])
                last = nc.vector.tensor_copy(nvs[64:P, j, :], nv[0:64, j + 1, :])
            last.then_inc(nvs_done, 1)

            def na_rowmax(t):
                w = 384 if t % 10 < 8 else TC
                n = 8 * (t // 10) + t % 10
                dve.wait_ge(na_s, t + 1)
                if t % 10 < 8:
                    dve.wait_ge(bm_done, n + 1)
                    add = bm[:, n % 2, :]
                else:
                    add = bm[:, 0, NKEY:NKEY + NP]
                if t >= 2:
                    dve.wait_ge(na_e, t - 1)
                e, f = t % 3, t % 2
                link(nc.vector.tensor_tensor_reduce(s32[:, f, 0:w], ps[:, f, 0:w], add, 1.0, LOWEST, ALU.add, ALU.max,
                                                    smA[:, 0, e:e + 1]))
                ts(smA[:, 1, e:e + 1], smA[:, 0, e:e + 1], -1.0, None, ALU.mult).then_inc(na_max, 1)

            def na_norm(t):
                w = 384 if t % 10 < 8 else TC
                e = t % 3
                dve.wait_ge(na_e, t + 1)
                link(nc.vector.reciprocal(smA[:, 3, e:e + 1], smA[:, 2, e:e + 1]))
                ts(pA[:, e, 0:w], pA[:, e, 0:w], smA[:, 3, e:e + 1], None, ALU.mult).then_inc(na_p, 1)

            def na_store(t):
                m, b = t // 10, t % 10 // 2
                rows = slice(64 * (t % 2), 64 * (t % 2) + 64)
                dve.wait_ge(na_pv, t + 1)
                nc.vector.tensor_copy(oT[rows, 4 + m, P * b:P * (b + 1)], ps[0:64, 4 + t % 2, 0:P])\
                    .then_inc(na_out, 1)

            for t in range(N_NA + 4):
                if t < N_NA:
                    na_rowmax(t)
                if 1 <= t <= N_NA:
                    na_norm(t - 1)
                if t >= 4:
                    na_store(t - 4)

            def project_out(layer):
                for j in range(8):
                    dve_split(dve, PIECE_AT[f"out{layer}"] + j + 1)
                    g = UNIT_AT[f"out{layer}"] + j
                    dve.wait_ge(unit_done, g + 1)
                    nc.vector.tensor_copy(two(yT[:, j, :]), pair(g)).then_inc(dve_evac, 1)

            def mlp(layer):
                g0, n0 = UNIT_AT[f"mlp{layer}"], PIECE_AT[f"mlp{layer}"]
                base = layer * NCH * CH
                dve.wait_ge(y_zero, layer + 1)

                def chunk(c):
                    at, half = c * (2 * CH), c * CH
                    for j in range(2 * CH):
                        dve_split(dve, n0 + j + 1, at)
                        if j < CH:
                            dve.wait_ge(act_evac, EVAC[g0][0] + j + half)
                            tt(s2[:, j % 2, :], r32[:, j % 2, :], r32[:, j % 2, :], ALU.mult)\
                                .then_inc(chain.sem, 1)
                            dve.wait_ge(chain.sem, chain.n + j + 1 + half)
                            dve.wait_ge(h2_hi_done, base + j + 1 + half)
                            tt(h2_lo[:, j, :], s2[:, j % 2, :], h2_hi[:, j, :].bitcast(F32), ALU.subtract)\
                                .then_inc(h2_lo_done, 1)
                        else:
                            dve.wait_ge(unit_done, g0 + j + 1 + at)
                            y = two(yT[:, j - CH, :])
                            tt(y, y, pair(g0 + j), ALU.add).then_inc(dve_evac, 1)

                with dve.Fori(0, NCH - 1) as c:
                    chunk(c)
                chunk(NCH - 1)
                chain.n += NCH * CH

            def norms_with_ada(part, residual, operand):
                n = ADA_AT[part]
                add_residual(*residual, lambda k: mod_columns(n + (4, 5, 7).index(k)) if k in (4, 5, 7) else None)
                mod_columns(n + 3)
                root(operand[0])
                mod_columns(n + 4)
                modulate(*operand, lambda k: mod_columns(n + 5 + (1, 2, 4).index(k)) if k in (1, 2, 4) else None)

            project_out(0)
            norms_with_ada("out0", ("y0a", 0, G1), ("in0m", 0, A2, SHIFT2))
            mlp(0)
            norms_with_ada("mlp0", ("y0m", 0, G2), ("in1", 1, A1, SHIFT1))

            for j in range(5):
                dve_split(dve, PIECE_AT["in_c"] + j + 1)
            root("cq")
            dve_split(dve, PIECE_AT["uq"])
            rstd_q = spread_ready("cq")
            for k in range(KQ):
                if k >= 2:
                    dve.wait_ge(cn_lo, k - 1)
                link(tt(nt[:, k % 2, :], cT[:, k, :], rstd_q, ALU.mult))
                ts(nt[:, k % 2, :], nt[:, k % 2, :], vecT[:, ROW_QN + k:ROW_QN + k + 1], None, ALU.mult)\
                    .then_inc(cn_full, 1)
            root("ckv")
            dve_split(dve, PIECE_AT["uq"] + 1)

            def key_latents():
                rstd_kv = spread_ready("ckv")
                dve.wait_ge(cn_lo, KQ)
                dve.wait_ge(pc_out, 1)
                for k in range(KKV):
                    link(tt(nt[:, k, :], cT[:, KQ + k, :], rstd_kv, ALU.mult))
                    gain = vecT[:, ROW_KVN + k:ROW_KVN + k + 1]
                    ts(ckn[:, k, 0:TL], nt[:, k, 0:TL], gain, None, ALU.mult)
                    ts(ckn[:, k, TL + NP:T + NP], nt[:, k, TL:T], gain, None, ALU.mult).then_inc(cn_full, 1)
                dve.wait_ge(act_evac, EVAC[UNIT_AT["in_c"] + 5][0])
                tt(rt[0:ROPE, 0, :], cT[0:ROPE, 5, 0:TL], rope[0:ROPE, :], ALU.mult)
                link(tt(rt[0:ROPE, 1, :], cT[ROPE:64, 5, 0:TL], rope[ROPE:64, :], ALU.mult))
                tt(kmas[64:96, 0:TL], rt[0:ROPE, 0, :], rt[0:ROPE, 1, :], ALU.add).then_inc(km_rope, 1)

            for h in range(NH_MLA):
                g = UNIT_AT["uq"] + h
                if h == 2:
                    key_latents()
                if h and h % 2 == 0:
                    dve_split(dve, PIECE_AT["uq"] + h // 2 + 1)
                dve.wait_ge(act_evac, EVAC[g][0])
                if h:
                    dve.wait_ge(qrope_done, h)
                for s_, (a, b) in enumerate(((0, HALF), (HALF, TL))):
                    bank = first_bank(g) + s_
                    tt(rt[64:96, 0, a:b], ps[64:96, bank, 0:b - a], rope[64:96, a:b], ALU.mult)
                    last = tt(rt[64:96, 1, a:b], ps[96:P, bank, 0:b - a], rope[96:P, a:b], ALU.mult)
                last.then_inc(dve_evac, 1)
                dve.wait_ge(dve_evac, EVAC[g][1])
                tt(qm[64:96, h, 0:TL], rt[64:96, 0, :], rt[64:96, 1, :], ALU.add).then_inc(qrope_done, 1)
            dve_split(dve, PIECE_AT["uk"] + 1)
            dve_split(dve, PIECE_AT["uv"])
            dve_split(dve, PIECE_AT["uv"] + 1)
            for j in range(12):
                dve.wait_ge(vm_done, j + 1)
                if j == 0:
                    dve.wait_ge(unit_done, UNIT_AT["uq"] + NH_MLA)
                nc.vector.tensor_copy(vm[:, j % 6, 512 * (j // 6):512 * (j // 6 + 1)], ps[:, 4 + j % 4, :])\
                    .then_inc(vm_out, 1)

            def mla_rowmax(t):
                e, b2 = t % 3, 2 * (t % 2)
                dve.wait_ge(m_s, t + 1)
                if t >= 2:
                    dve.wait_ge(m_e, t - 1)
                src = ps[:, b2:b2 + 2, 0:HALF] if t % 5 < NB else ps[:, b2, 0:TC]
                nc.vector.tensor_reduce(smM[:, 0, e:e + 1], src, AX.XY if t % 5 < NB else AX.X, ALU.max,
                                        negate=True).then_inc(m_max, 1)

            def mla_norm(t):
                w, e = (T if t % 5 < NB else TC), t % 3
                dve.wait_ge(m_e, t + 1)
                link(nc.vector.reciprocal(smM[:, 2, e:e + 1], smM[:, 1, e:e + 1]))
                ts(pM[:, e, 0:w], pM[:, e, 0:w], smM[:, 2, e:e + 1], None, ALU.mult).then_inc(m_p, 1)

            def mla_store(t):
                h, b = t // 5, t % 5
                dve.wait_ge(m_pv, t + 1)
                rows = slice(64 * (h % 2), 64 * (h % 2) + 64)
                nc.vector.tensor_copy(qm[rows, h, P * b:P * (b + 1)], ps[0:64, 6 + t % 2, 0:P]).then_inc(m_out, 1)

            for t in range(N_MLA + 4):
                if t < N_MLA:
                    mla_rowmax(t)
                if 1 <= t <= N_MLA:
                    mla_norm(t - 1)
                if t >= 4:
                    mla_store(t - 4)
            dve_split(dve, PIECE_AT["out1"])
            project_out(1)
            norms_with_ada("out1", ("y1a", 1, G1), ("in1m", 1, A2, SHIFT2))
            mlp(1)
            last_residual()

        @block.gpsimd
        def _(pool):
            sub = nc.gpsimd.tensor_tensor
            nc.gpsimd.memset(ones[:], 1.0).then_inc(filled, 1)
            nc.gpsimd.memset(eps[:], EPS).then_inc(filled, 1)
            nc.gpsimd.memset(gnb[:], 0.0).then_inc(filled, 1)
            pool.wait_ge(filled, 3)
            nc.gpsimd.memset(gnb[0:64, 0:64], 1.0 / HD).then_inc(filled, 1)
            nc.gpsimd.memset(gnb[64:P, 64:P], 1.0 / HD).then_inc(filled, 1)
            pool.wait_ge(filled, 5)
            nc.gpsimd.memset(kz[:], 0.0).then_inc(filled, 1)
            pool.wait_ge(rows_t, 2)
            nc.gpsimd.memset(kzn[:], 0.0).then_inc(filled, 1)

            def add_squares(name):
                for k in range(1, NORM_K[name] - 1):
                    pool.wait_ge(sq_done, NORM_AT[name] + k + 1)
                    if k > 1:
                        pool.wait_ge(added, ADD_AT[name] + k - 1)
                    sub(rstd[:], rstd[:], sq[:, k % 2, :], ALU.add).then_inc(added, 1)

            add_squares("in0")

            def low_parts(name, hi, lo):
                for k in range(KD):
                    pool.wait_ge(h_hi_done, KD * MOD_NO[name] + k + 1)
                    sub(lo[:, k, :], nt[:, k % 2, :], hi[:, k, :].bitcast(F32), ALU.subtract).then_inc(h_lo_done, 1)

            low_parts("in0", hA_hi, hA_lo)
            pool.wait_ge(v_done, 8)
            nc.gpsimd.memset(bias[:], 0.0).then_inc(bias_zero, 1)
            pool.wait_ge(stored, 32)
            pool.wait_ge(ret_out, NH)
            nc.gpsimd.memset(bm[:], 0.0).then_inc(bias_zero, 1)
            pool.wait_ge(bias_zero, 2)
            pool.wait_ge(na_in, 16 * 3)
            pool.wait_ge(na_bias_in, 16 * BLK * ROWS)
            for n in range(8 * 4):
                m, b, h = n // 8, n % 8 // 2, 2 * (n // 8) + n % 2
                if n >= 2:
                    pool.wait_ge(na_max, 10 * ((n - 2) // 8) + (n - 2) % 8 + 1)
                u = (16, 8, 8, 0)[b]
                sub(bm[:, n % 2, 0:NKEY].rearrange("p (c r) -> p c r", r=ROWS),
                    bias[:, h, :, u:u + KW].rearrange("p r c -> p c r"),
                    mask[:, b, :].rearrange("p (c r) -> p c r", r=ROWS), ALU.add).then_inc(bm_done, 1)

            for k in range(KD):
                pool.wait_ge(o_hi_done, k + 1)
                sub(h2_lo[:, k, :], oT[:, k, :], h2_hi[:, k, :].bitcast(F32), ALU.subtract).then_inc(o_lo_done, 1)
            add_squares("y0a")
            add_squares("in0m")
            pool.wait_ge(x_done, KD)
            nc.gpsimd.memset(yT[:], 0.0).then_inc(y_zero, 1)
            low_parts("in0m", hM_hi, hM_lo)
            add_squares("y0m")
            add_squares("in1")
            low_parts("in1", hM_hi, hM_lo)
            pool.wait_ge(h_lo_done, 3 * KD)
            pool.wait_ge(ada_done, ADA_AT["out1"])
            nc.gpsimd.memset(kmas[64:P, :], 0.0).then_inc(km_zero, 1)
            pool.wait_ge(km_zero, 1)
            add_squares("cq")
            for k in range(KQ):
                pool.wait_ge(cn_hi, k + 1)
                sub(cq_lo[:, k, :], nt[:, k % 2, :], cq_hi[:, k, :].bitcast(F32), ALU.subtract).then_inc(cn_lo, 1)
            for k in range(KKV):
                pool.wait_ge(cn_hi, KQ + k + 1)
                sub(ck_lo[:, k, :], ckn[:, k, :], ck_hi[:, k, :].bitcast(F32), ALU.subtract).then_inc(cn_lo, 1)
            pool.wait_ge(cn_lo, KQ + KKV)
            nc.gpsimd.memset(qm[64:96, :, TL:T], 0.0).then_inc(ctx_rope, 1)
            pool.wait_ge(ctx_rope, 1)
            pool.wait_ge(km_rope, 2)
            pool.wait_ge(pc_out, 1)
            pool.wait_ge(tok_out, 1)
            pool.wait_ge(stored, 16 * 6)
            pool.wait_ge(qrope_done, NH_MLA)
            for h in range(NH_MLA):
                nc.gpsimd.tensor_copy(km[64:P, h, :], kmas[64:P, :]).then_inc(kmas_done, 1)

            pool.wait_ge(kmas_done, NH_MLA)
            for h in range(NH_MLA):
                pool.wait_ge(o_hi_done, KD + h + 1)
                if h:
                    pool.wait_ge(o_lo_done, KD + h)
                rows = slice(64 * (h % 2), 64 * (h % 2) + 64)
                sub(o_lo[h // 2][rows], qm[rows, h, :], o_hi[h // 2][rows].bitcast(F32), ALU.subtract)\
                    .then_inc(o_lo_done, 1)

            pool.wait_ge(o_lo_done, KD + NH_MLA)
            add_squares("y1a")
            add_squares("in1m")
            pool.wait_ge(x_done, 3 * KD)
            nc.gpsimd.memset(yT[:], 0.0).then_inc(y_zero, 1)
            low_parts("in1m", hM_hi, hM_lo)
            add_squares("y1m")
            for k in range(0, KD, 2):
                pool.wait_ge(y_scaled, k // 2 + 1)
                for out, y, x in result_parts(k):
                    last = sub(out, y, x, ALU.add)
                last.then_inc(xN_pool, 1)


_INS = ["x_prompt", "x_sample", "state_ret_fwd", "state_ret_bwd", "cache_na_k", "cache_na_v", "cache_mla_ckv",
        "cache_mla_kpe", "c", "c_ctx", "w_ada", "b_ada", "norm_gains", "w_mlp_in", "w_mlp_out", "w_in_ac",
        "w_out_ac", "ret_decay_fwd", "ret_decay_bwd", "na_rpb", "mla_q_norm", "mla_kv_norm", "w_uk", "w_uv",
        "w_out_c"]
_OUTS = [("y_prompt", (1, 128, 1024)), ("y_sample", (1, 512, 1024)), ("new_ret_fwd", (1, 1, 8, 64, 64)),
         ("new_ret_bwd", (1, 1, 8, 64, 64)), ("new_na_k", (1, 1, 8, 128, 64)), ("new_na_v", (1, 1, 8, 128, 64)),
         ("new_mla_ckv", (1, 1, 128, 256)), ("new_mla_kpe", (1, 1, 128, 32))]


def shape_constants():
    import numpy as np

    part = np.arange(P)
    col, row = part // ROWS, part % ROWS
    u, rq = np.divmod(np.arange(112 * ROWS), ROWS)
    lat = (rq[None, :] - row[:, None]) * GRID_W + (u[None, :] - 48 - col[:, None])
    ctx = part[None, :] - part[:, None]
    d = np.concatenate([lat, ctx], axis=1)
    dist = d.astype(np.float32)
    token = np.arange(TL)
    time = (token % ROWS) * GRID_W + token // ROWS
    tpos = np.broadcast_to(np.stack([time + 1, TL - time]), (P, 2, TL)).astype(np.float32)
    kpos = np.stack([P - 1 - part, part], axis=1).astype(np.float32)
    mask = np.zeros((P, NB, KW, ROWS), np.float32)
    for b in range(NB):
        first = int(np.clip(b * BLK - 8, 0, GRID_W - KW))
        qc = b * BLK + col
        start = np.clip(qc - 8, 0, GRID_W - 16)
        kc = first + np.arange(KW)
        ok = (kc[None, :] >= start[:, None]) & (kc[None, :] < start[:, None] + 16)
        mask[:, b] = np.where(ok, 0.0, -1e30)[:, :, None]
    nf = ROPE // 4
    inv = (np.float32(10000.0) ** (-np.arange(nf, dtype=np.float32) / np.float32(nf))).astype(np.float32)
    ang = np.concatenate([(time // GRID_W).astype(np.float32)[:, None] * inv,
                          (time % GRID_W).astype(np.float32)[:, None] * inv], axis=-1)
    cos = np.repeat(np.cos(ang), 2, axis=1).T
    sin = np.repeat(np.sin(ang), 2, axis=1).T * np.where(np.arange(ROPE) % 2 == 0, -1.0, 1.0)[:, None]
    rope = np.concatenate([cos, sin, cos * MLA_SCALE, sin * MLA_SCALE]).astype(np.float32)
    return {"c_ident": np.eye(P, dtype=np.float32), "c_dist": dist, "c_tpos": tpos, "c_kpos": kpos,
            "c_mask": mask.reshape(P, NB, NKEY), "c_rope": rope}


def kernel(**inputs):
    import concourse.bacc as bacc
    import numpy as np
    from concourse.bass_utils import run_bass_kernel_spmd as run

    nc = bacc.Bacc("TRN2", target_bir_lowering=False, num_devices=1)
    arrays = {name: np.ascontiguousarray(inputs[name]) for name in _INS}
    swap = np.arange(ROPE) ^ 1
    w = np.asarray(inputs["w_in_c"])[0]
    arrays["w_in_c_swap"] = np.ascontiguousarray(np.concatenate([w, w[:, 640 + swap]], axis=1))
    w = np.asarray(inputs["w_uq"])[0].reshape(KQ * P, NH_MLA, 96)
    arrays["w_uq_heads"] = np.ascontiguousarray(
        np.concatenate([w, w[:, :, 64 + swap]], axis=2).reshape(KQ * P, NH_MLA * P))
    arrays.update(shape_constants())
    ins, feed = {}, {}
    for name, a in arrays.items():
        feed[f"in_{name}"] = a
        ins[name] = nc.dram_tensor(f"in_{name}", a.shape, mybir.dt.from_np(a.dtype), kind="ExternalInput").ap()
    outs = {name: nc.dram_tensor(f"out_{name}", shape, F32, kind="ExternalOutput").ap() for name, shape in _OUTS}
    build(nc, ins, outs)
    r = run(nc, [feed], core_ids=[0])
    return tuple(r.results[0][f"out_{name}"] for name, _ in _OUTS)
```
